# Optimizing a Trainium2 kernel written in Bass

```python
import jax, jax.numpy as jnp
from jax import lax
import numpy as np
import math

D_MODEL = 1024
BATCH = 1
SEQ = 256
DEPTH = 2

N_MIXERS = 4
N_MEM = 256
EPS = 1e-6
NEG = -1e30
D_FF = ((8 * D_MODEL // 3 + 255) // 256) * 256

POOL_WINDOWS = (2, 4, 8, 16)
POOL_GROUP = D_MODEL // len(POOL_WINDOWS)

NSA_HEADS = 16
NSA_KV_HEADS = 4
NSA_HEAD_DIM = D_MODEL // NSA_HEADS
NSA_CMP_BLOCK = 32
NSA_CMP_STRIDE = 16
NSA_SEL_BLOCK = 64
NSA_N_SELECT = 16
NSA_WINDOW = 512
NSA_CMP_HIDDEN = 4 * NSA_HEAD_DIM
NSA_Q_BLOCK = 64
NSA_KV_WIDTH = NSA_KV_HEADS * NSA_HEAD_DIM
NSA_FORCE = 1e4
NSA_IN_WIDTH = D_MODEL + 6 * NSA_KV_WIDTH + 3 * NSA_HEADS

GLA_HEADS = 4
GLA_DK = D_MODEL // 2 // GLA_HEADS
GLA_DV = D_MODEL // GLA_HEADS
GLA_GATE_RANK = 16
GLA_TAU = 16.0
GLA_CHUNK = 64
GLA_IN_WIDTH = 2 * GLA_HEADS * GLA_DK + 2 * GLA_HEADS * GLA_DV + GLA_GATE_RANK

CONV_WIDTH = 31

XATTN_HEADS = 4
XATTN_HEAD_DIM = D_MODEL // XATTN_HEADS


F32 = jnp.float32

def n_layers_of(m):
    return len(range(m, DEPTH, N_MIXERS))

def rms_norm(x, g):
    xf = x.astype(F32)
    y = xf * lax.rsqrt(jnp.mean(xf * xf, axis=-1, keepdims=True) + EPS)
    return (y * g.astype(F32)).astype(x.dtype)

def swiglu_ffn(h, w_in, w_out):
    g, u = jnp.split(h @ w_in, 2, axis=-1)
    return (jax.nn.silu(g) * u) @ w_out

def pool_mixer(h, w, b, scale):
    B, S, D = h.shape
    hf = h.astype(F32)
    c = jnp.pad(jnp.cumsum(hf, axis=1), ((0, 0), (1, 0), (0, 0)))
    t = jnp.arange(S)
    groups = []
    for gi, win in enumerate(POOL_WINDOWS):
        cg = c[:, :, gi * POOL_GROUP:(gi + 1) * POOL_GROUP]
        start = jnp.maximum(t + 1 - win, 0)
        win_sum = cg[:, 1:] - jnp.take(cg, start, axis=1)
        cnt = (t + 1 - start).astype(F32)[None, :, None]
        groups.append(win_sum / cnt - hf[:, :, gi * POOL_GROUP:(gi + 1) * POOL_GROUP])
    p = jnp.stack(groups, axis=2)
    y = jnp.einsum('bsgc,gcd->bsgd', p, w.astype(F32)).reshape(B, S, D) + b.astype(F32)
    return (y * scale.astype(F32)).astype(h.dtype)

def nsa_mixer(h, w_in, cmp_pos, cmp_w1, cmp_w2, w_o):
    B, S, D = h.shape
    H, G, dh = NSA_HEADS, NSA_KV_HEADS, NSA_HEAD_DIM
    R = H // G
    SEL = NSA_SEL_BLOCK
    proj = (h @ w_in).astype(F32)
    splits = np.cumsum([D] + [NSA_KV_WIDTH] * 6).tolist()
    q, kc, vc, ks, vs, kw, vw, gates = jnp.split(proj, splits, axis=-1)
    q = q.reshape(B, S, G, R, dh).transpose(0, 2, 3, 1, 4) * dh ** -0.5
    gates = jax.nn.sigmoid(gates).reshape(B, S, G, R, 3).transpose(0, 2, 3, 1, 4)

    def kv_heads(a):
        return a.reshape(B, S, G, dh).transpose(0, 2, 1, 3)

    n_cmp = (S - NSA_CMP_BLOCK) // NSA_CMP_STRIDE + 1
    cmp_idx = np.arange(n_cmp)[:, None] * NSA_CMP_STRIDE + np.arange(NSA_CMP_BLOCK)[None, :]

    def compress(a, pos, w1, w2):
        blk = (a[:, :, cmp_idx] + pos.astype(F32)).reshape(B, G, n_cmp, NSA_CMP_BLOCK * dh)
        return jax.nn.gelu(blk @ w1.astype(F32)) @ w2.astype(F32)

    k_cmp = compress(kv_heads(kc), cmp_pos[0], cmp_w1[0], cmp_w2[0])
    v_cmp = compress(kv_heads(vc), cmp_pos[1], cmp_w1[1], cmp_w2[1])
    cmp_end = jnp.asarray(cmp_idx[:, -1])

    n_slc = S // SEL
    cs = np.arange(n_cmp) * NSA_CMP_STRIDE
    ss = np.arange(n_slc) * SEL
    ov = np.clip(np.minimum(cs[:, None] + NSA_CMP_BLOCK, ss[None, :] + SEL)
                 - np.maximum(cs[:, None], ss[None, :]), 0, None) / NSA_CMP_BLOCK
    ov = jnp.asarray(ov, F32)
    k_eff = min(NSA_N_SELECT, n_slc)
    blk_ids = jnp.arange(n_slc)

    ks_blk = kv_heads(ks).reshape(B, G, n_slc, SEL, dh)
    vs_blk = kv_heads(vs).reshape(B, G, n_slc, SEL, dh)
    kw_pad = jnp.pad(kv_heads(kw), ((0, 0), (0, 0), (NSA_WINDOW, 0), (0, 0)))
    vw_pad = jnp.pad(kv_heads(vw), ((0, 0), (0, 0), (NSA_WINDOW, 0), (0, 0)))
    bi = jnp.arange(B)[:, None, None, None]
    gi = jnp.arange(G)[None, :, None, None]
    Qb = min(NSA_Q_BLOCK, S)
    n_qb = S // Qb

    def block(qi):
        s0 = qi * Qb
        t = s0 + jnp.arange(Qb)
        qb = lax.dynamic_slice_in_dim(q, s0, Qb, axis=3)
        gb = lax.dynamic_slice_in_dim(gates, s0, Qb, axis=3)
        vis = cmp_end[None, :] <= t[:, None]
        sc = jnp.where(vis, jnp.einsum('bgrqd,bgnd->bgrqn', qb, k_cmp), NEG)
        p_cmp = jax.nn.softmax(sc, axis=-1) * jnp.any(vis, axis=-1)[:, None]
        o_cmp = jnp.einsum('bgrqn,bgnd->bgrqd', p_cmp, v_cmp)
        imp = jnp.einsum('bgrqn,nm->bgqm', p_cmp, ov)
        cur = t // SEL
        forced = (blk_ids[None, :] == 0) | (blk_ids[None, :] == cur[:, None]) | (blk_ids[None, :] == cur[:, None] - 1)
        imp = jnp.where(forced, NSA_FORCE, imp)
        imp = jnp.where(blk_ids[None, :] * SEL <= t[:, None], imp, -1.0)
        _, idx = lax.top_k(imp, k_eff)
        ksel = ks_blk[bi, gi, idx].reshape(B, G, Qb, k_eff * SEL, dh)
        vsel = vs_blk[bi, gi, idx].reshape(B, G, Qb, k_eff * SEL, dh)
        pos = (idx[..., None] * SEL + jnp.arange(SEL)).reshape(B, G, Qb, k_eff * SEL)
        sc = jnp.einsum('bgrqd,bgqkd->bgrqk', qb, ksel)
        sc = jnp.where((pos <= t[:, None])[:, :, None], sc, NEG)
        o_slc = jnp.einsum('bgrqk,bgqkd->bgrqd', jax.nn.softmax(sc, axis=-1), vsel)
        kwin = lax.dynamic_slice_in_dim(kw_pad, s0, NSA_WINDOW + Qb, axis=2)
        vwin = lax.dynamic_slice_in_dim(vw_pad, s0, NSA_WINDOW + Qb, axis=2)
        wpos = s0 - NSA_WINDOW + jnp.arange(NSA_WINDOW + Qb)
        wmask = (wpos[None, :] <= t[:, None]) & (wpos[None, :] > t[:, None] - NSA_WINDOW) & (wpos[None, :] >= 0)
        sc = jnp.where(wmask, jnp.einsum('bgrqd,bgkd->bgrqk', qb, kwin), NEG)
        o_win = jnp.einsum('bgrqk,bgkd->bgrqd', jax.nn.softmax(sc, axis=-1), vwin)
        return gb[..., 0:1] * o_cmp + gb[..., 1:2] * o_slc + gb[..., 2:3] * o_win

    o = lax.map(block, jnp.arange(n_qb))
    o = o.transpose(1, 0, 4, 2, 3, 5).reshape(B, S, H * dh)
    return o.astype(h.dtype) @ w_o

def gla_mixer(h, w_in, w_gate_up, b_gate, norm_g, w_o):
    B, S, D = h.shape
    Hh, dk, dv, C = GLA_HEADS, GLA_DK, GLA_DV, GLA_CHUNK
    proj = (h @ w_in).astype(F32)
    qw, vw = Hh * dk, Hh * dv
    q, k, v, og, gdown = jnp.split(proj, [qw, 2 * qw, 2 * qw + vw, 2 * qw + 2 * vw], axis=-1)
    log_a = jax.nn.log_sigmoid(gdown @ w_gate_up.astype(F32) + b_gate.astype(F32)) / GLA_TAU
    nc = S // C

    def heads(a, d):
        return a.reshape(B, nc, C, Hh, d).transpose(0, 3, 1, 2, 4)

    q = heads(q, dk) * dk ** -0.5
    k = heads(k, dk)
    v = heads(v, dv)
    b = jnp.cumsum(heads(log_a, dk), axis=3)
    b_last = b[:, :, :, -1:, :]
    q_t = q * jnp.exp(b)
    k_t = k * jnp.exp(-b)
    causal = jnp.tril(jnp.ones((C, C), dtype=bool))
    A = jnp.where(causal, jnp.einsum('bhncd,bhnsd->bhncs', q_t, k_t), 0.0)
    o_intra = jnp.einsum('bhncs,bhnsv->bhncv', A, v)
    kv = jnp.einsum('bhncd,bhncv->bhndv', k * jnp.exp(b_last - b), v)
    decay = jnp.exp(b_last[:, :, :, 0, :])

    def step(state, inp):
        kv_n, dec_n = inp
        return dec_n[..., None] * state + kv_n, state

    init = jnp.zeros((B, Hh, dk, dv), F32)
    _, s_prev = lax.scan(step, init, (kv.transpose(2, 0, 1, 3, 4), decay.transpose(2, 0, 1, 3)))
    s_prev = s_prev.transpose(1, 2, 0, 3, 4)
    o = o_intra + jnp.einsum('bhncd,bhndv->bhncv', q_t, s_prev)
    o = rms_norm(o.transpose(0, 2, 3, 1, 4).reshape(B, S, Hh, dv), norm_g)
    o = o.reshape(B, S, Hh * dv) * jax.nn.silu(og)
    return o.astype(h.dtype) @ w_o

def conv_mixer(h, w_in, b_in, w_dw, b_dw, ln_g, ln_b, w_out, b_out):
    D = h.shape[-1]
    a, gate = jnp.split(h @ w_in + b_in, 2, axis=-1)
    u = a * jax.nn.sigmoid(gate)
    u = jnp.pad(u, ((0, 0), (CONV_WIDTH - 1, 0), (0, 0)))
    u = lax.conv_general_dilated(u, w_dw[:, None, :].astype(u.dtype), window_strides=(1,), padding='VALID',
                                 dimension_numbers=('NWC', 'WIO', 'NWC'), feature_group_count=D) + b_dw
    uf = u.astype(F32)
    mu = jnp.mean(uf, axis=-1, keepdims=True)
    var = jnp.mean(jnp.square(uf - mu), axis=-1, keepdims=True)
    uf = (uf - mu) * lax.rsqrt(var + EPS) * ln_g.astype(F32) + ln_b.astype(F32)
    return jax.nn.silu(uf).astype(h.dtype) @ w_out + b_out

def memory_cross_attention(h, mem_n, w_q, w_kv, w_o):
    B, S, D = h.shape
    N = mem_n.shape[1]
    Hx, dh = XATTN_HEADS, XATTN_HEAD_DIM
    q = (h @ w_q).astype(F32).reshape(B, S, Hx, dh) * dh ** -0.5
    k, v = jnp.split((mem_n @ w_kv).astype(F32), 2, axis=-1)
    k = k.reshape(B, N, Hx, dh)
    v = v.reshape(B, N, Hx, dh)
    p = jax.nn.softmax(jnp.einsum('bqhd,bkhd->bhqk', q, k), axis=-1)
    o = jnp.einsum('bhqk,bkhd->bqhd', p, v).reshape(B, S, D)
    return o.astype(h.dtype) @ w_o

def first_inputs(seed: int = 0) -> dict:
    key = jax.random.key(seed)
    keys = iter(jax.random.split(key, 64))
    D, F, L = D_MODEL, D_FF, DEPTH
    nA, nB, nC, nD = (n_layers_of(m) for m in range(N_MIXERS))

    def w(shape, fan_in):
        return jax.random.normal(next(keys), shape, F32) * fan_in ** -0.5

    def gain(shape):
        return 1.0 + 0.02 * jax.random.normal(next(keys), shape, F32)

    def small(shape, s=0.02):
        return s * jax.random.normal(next(keys), shape, F32)

    return {
        "x": jax.random.normal(next(keys), (BATCH, SEQ, D), F32),
        "mem": jax.random.normal(next(keys), (BATCH, N_MEM, D), F32),
        "ffn1_norm": gain((L, D)),
        "ffn1_w_in": w((L, D, 2 * F), D),
        "ffn1_w_out": w((L, F, D), F),
        "mix_norm": gain((L, D)),
        "xattn_norm": gain((L, D)),
        "mem_norm": gain((L, D)),
        "xattn_w_q": w((L, D, D), D),
        "xattn_w_kv": w((L, D, 2 * D), D),
        "xattn_w_o": w((L, D, D), D),
        "ffn2_norm": gain((L, D)),
        "ffn2_w_in": w((L, D, 2 * F), D),
        "ffn2_w_out": w((L, F, D), F),
        "pool_w": w((nA, len(POOL_WINDOWS), POOL_GROUP, POOL_GROUP), POOL_GROUP),
        "pool_b": small((nA, D)),
        "pool_scale": 1.0 + 0.1 * jax.random.normal(next(keys), (nA, D), F32),
        "nsa_w_in": w((nB, D, NSA_IN_WIDTH), D),
        "nsa_cmp_pos": small((nB, 2, NSA_CMP_BLOCK, NSA_HEAD_DIM), 0.1),
        "nsa_cmp_w1": w((nB, 2, NSA_CMP_BLOCK * NSA_HEAD_DIM, NSA_CMP_HIDDEN), NSA_CMP_BLOCK * NSA_HEAD_DIM),
        "nsa_cmp_w2": w((nB, 2, NSA_CMP_HIDDEN, NSA_HEAD_DIM), NSA_CMP_HIDDEN),
        "nsa_w_o": w((nB, D, D), D),
        "gla_w_in": w((nC, D, GLA_IN_WIDTH), D),
        "gla_w_gate_up": w((nC, GLA_GATE_RANK, GLA_HEADS * GLA_DK), GLA_GATE_RANK),
        "gla_b_gate": small((nC, GLA_HEADS * GLA_DK)),
        "gla_norm": gain((nC, GLA_DV)),
        "gla_w_o": w((nC, D, D), D),
        "conv_w_in": w((nD, D, 2 * D), D),
        "conv_b_in": small((nD, 2 * D)),
        "conv_dw": w((nD, CONV_WIDTH, D), CONV_WIDTH),
        "conv_b_dw": small((nD, D)),
        "conv_ln_g": gain((nD, D)),
        "conv_ln_b": small((nD, D)),
        "conv_w_out": w((nD, D, D), D),
        "conv_b_out": small((nD, D)),
        "final_norm": gain((D,)),
    }

def first_block(x, mem, ffn1_norm, ffn1_w_in, ffn1_w_out, mix_norm, xattn_norm, mem_norm,
              xattn_w_q, xattn_w_kv, xattn_w_o, ffn2_norm, ffn2_w_in, ffn2_w_out,
              pool_w, pool_b, pool_scale,
              nsa_w_in, nsa_cmp_pos, nsa_cmp_w1, nsa_cmp_w2, nsa_w_o,
              gla_w_in, gla_w_gate_up, gla_b_gate, gla_norm, gla_w_o,
              conv_w_in, conv_b_in, conv_dw, conv_b_dw, conv_ln_g, conv_ln_b, conv_w_out, conv_b_out,
              final_norm):
    for i in range(DEPTH):
        m, j = i % N_MIXERS, i // N_MIXERS
        x = x + 0.5 * swiglu_ffn(rms_norm(x, ffn1_norm[i]), ffn1_w_in[i], ffn1_w_out[i])
        h = rms_norm(x, mix_norm[i])
        if m == 0:
            y = pool_mixer(h, pool_w[j], pool_b[j], pool_scale[j])
        elif m == 1:
            y = nsa_mixer(h, nsa_w_in[j], nsa_cmp_pos[j], nsa_cmp_w1[j], nsa_cmp_w2[j], nsa_w_o[j])
        elif m == 2:
            y = gla_mixer(h, gla_w_in[j], gla_w_gate_up[j], gla_b_gate[j], gla_norm[j], gla_w_o[j])
        else:
            y = conv_mixer(h, conv_w_in[j], conv_b_in[j], conv_dw[j], conv_b_dw[j],
                           conv_ln_g[j], conv_ln_b[j], conv_w_out[j], conv_b_out[j])
        x = x + y
        x = x + memory_cross_attention(rms_norm(x, xattn_norm[i]), rms_norm(mem, mem_norm[i]),
                                       xattn_w_q[i], xattn_w_kv[i], xattn_w_o[i])
        x = x + 0.5 * swiglu_ffn(rms_norm(x, ffn2_norm[i]), ffn2_w_in[i], ffn2_w_out[i])
    return rms_norm(x, final_norm)


DEPTH_2 = 1

HEAD_DIM = 64
DIFF_HEADS = 4
DIFF_V_DIM = 2 * HEAD_DIM
DSA_HEADS = 4
DSA_LATENT = 128
DSA_V_DIM = 64
IDX_HEADS = 8
IDX_DIM = 32
DSA_TOPK_MAX = 256
MOBA_HEADS = 4
MOBA_BLOCK = 256
MOBA_TOPK_MAX = 3
N_BUCKETS = 32
MAX_DISTANCE = 128
N_BIAS_HEADS = DIFF_HEADS + DSA_HEADS + MOBA_HEADS
D_FF_2 = 4 * D_MODEL
Q_BLOCK = 128
MOBA_Q_CHUNK = 32

A_Q = DIFF_HEADS * 2 * HEAD_DIM
A_K = DIFF_HEADS * 2 * HEAD_DIM
A_V = DIFF_HEADS * DIFF_V_DIM
B_Q = DSA_HEADS * DSA_LATENT
B_KV = DSA_LATENT
B_IQ = IDX_HEADS * IDX_DIM
B_IK = IDX_DIM
B_IW = IDX_HEADS
C_QKV = MOBA_HEADS * HEAD_DIM
G_COLS = 3 * D_MODEL
SPLIT_SIZES = (A_Q, A_K, A_V, B_Q, B_KV, B_IQ, B_IK, B_IW, C_QKV, C_QKV, C_QKV, G_COLS)
IN_COLS = A_Q + A_K + A_V + B_Q + B_KV + B_IQ + B_IK + B_IW + 3 * C_QKV + G_COLS


def rmsnorm(x, g):
    xf = x.astype(jnp.float32)
    y = xf * lax.rsqrt(jnp.mean(xf * xf, axis=-1, keepdims=True) + EPS)
    return y.astype(x.dtype) * g

def split_cols(p):
    out = []
    off = 0
    for n in SPLIT_SIZES:
        out.append(p[..., off:off + n])
        off += n
    return out

def t5_bucket(dist):
    max_exact = N_BUCKETS // 2
    n = jnp.maximum(dist, 0)
    nf = jnp.maximum(n, 1).astype(jnp.float32)
    large = max_exact + (jnp.log(nf / max_exact) / math.log(MAX_DISTANCE / max_exact)
                         * (N_BUCKETS - max_exact)).astype(jnp.int32)
    large = jnp.minimum(large, N_BUCKETS - 1)
    return jnp.where(n < max_exact, n, large)

def diff_attention(q, k, v, lam, lam_init, subln_g, bias_a):
    B, S, H = q.shape[0], q.shape[1], q.shape[2]
    E = v.shape[-1]
    kpos = jnp.arange(S)
    scale = HEAD_DIM ** -0.5
    bias_t = bias_a.T

    def block(i):
        q0 = i * Q_BLOCK
        qb = lax.dynamic_slice_in_dim(q, q0, Q_BLOCK, axis=1)
        qpos = q0 + jnp.arange(Q_BLOCK)
        dist = qpos[:, None] - kpos[None, :]
        bias = bias_t[:, t5_bucket(dist)]
        logits = jnp.einsum('bqhmd,bkhmd->bhmqk', qb, k).astype(jnp.float32) * scale + bias[None, :, None]
        logits = jnp.where(dist >= 0, logits, -jnp.inf)
        p = jax.nn.softmax(logits, axis=-1)
        attn = p[:, :, 0] - lam * p[:, :, 1]
        return jnp.einsum('bhqk,bkhe->bqhe', attn.astype(v.dtype), v)

    o = lax.map(block, jnp.arange(S // Q_BLOCK))
    o = jnp.moveaxis(o, 0, 1).reshape(B, S, H, E)
    o = rmsnorm(o, subln_g) * (1.0 - lam_init)
    return o.reshape(B, S, H * E)

def dsa_attention(q_lat, kv_lat, iq, ik, iw, w_uv, bias_b):
    B, S, H, R = q_lat.shape
    topk = min(DSA_TOPK_MAX, S // 4)
    kpos = jnp.arange(S)
    bidx = jnp.arange(B)[:, None, None]
    hidx = jnp.arange(H)[None, None, :, None]
    bias_t = bias_b.T
    idx_scale = (IDX_HEADS ** -0.5) * (IDX_DIM ** -0.5)

    def block(i):
        q0 = i * Q_BLOCK
        qpos = q0 + jnp.arange(Q_BLOCK)
        qb = lax.dynamic_slice_in_dim(q_lat, q0, Q_BLOCK, axis=1)
        iqb = lax.dynamic_slice_in_dim(iq, q0, Q_BLOCK, axis=1)
        iwb = lax.dynamic_slice_in_dim(iw, q0, Q_BLOCK, axis=1)
        causal = qpos[:, None] >= kpos[None, :]
        s_idx = jax.nn.relu(jnp.einsum('bqhd,bkd->bqhk', iqb, ik))
        score = jnp.einsum('bqhk,bqh->bqk', s_idx, iwb).astype(jnp.float32) * idx_scale
        score = jnp.where(causal[None], score, -jnp.inf)
        _, sel = lax.top_k(score, topk)
        dist = qpos[None, :, None] - sel
        valid = dist >= 0
        kv_sel = kv_lat[bidx, sel]
        logits = jnp.einsum('bqhr,bqkr->bqhk', qb, kv_sel).astype(jnp.float32) * (R ** -0.5)
        bias = bias_t[hidx, t5_bucket(dist)[:, :, None, :]]
        logits = jnp.where(valid[:, :, None, :], logits + bias, -jnp.inf)
        p = jax.nn.softmax(logits, axis=-1)
        return jnp.einsum('bqhk,bqkr->bqhr', p.astype(kv_sel.dtype), kv_sel)

    o = lax.map(block, jnp.arange(S // Q_BLOCK))
    o = jnp.moveaxis(o, 0, 1).reshape(B, S, H, R)
    o = jnp.einsum('bshr,hre->bshe', o, w_uv)
    return o.reshape(B, S, H * DSA_V_DIM)

def moba_attention(q, k, v, bias_c):
    B, S, H, Dh = q.shape
    nb = -(-S // MOBA_BLOCK)
    sp = nb * MOBA_BLOCK
    pad = ((0, 0), (0, sp - S), (0, 0), (0, 0))
    k_bh = jnp.pad(k, pad).reshape(B, nb, MOBA_BLOCK, H, Dh).transpose(0, 3, 1, 2, 4)
    v_bh = jnp.pad(v, pad).reshape(B, nb, MOBA_BLOCK, H, Dh).transpose(0, 3, 1, 2, 4)
    k_mean = jnp.mean(k_bh, axis=3)
    topb = min(MOBA_TOPK_MAX, nb)
    bias_t = bias_c.T
    bi = jnp.arange(B)[:, None, None, None]
    hi = jnp.arange(H)[None, :, None, None]
    hi5 = jnp.arange(H)[None, :, None, None, None]
    blk_ids = jnp.arange(nb)
    in_blk = jnp.arange(MOBA_BLOCK)
    scale = Dh ** -0.5

    def chunk(i):
        q0 = i * MOBA_Q_CHUNK
        qpos = q0 + jnp.arange(MOBA_Q_CHUNK)
        j = q0 // MOBA_BLOCK
        qc = lax.dynamic_slice_in_dim(q, q0, MOBA_Q_CHUNK, axis=1).transpose(0, 2, 1, 3)
        gate = jnp.einsum('bhqd,bhnd->bhqn', qc, k_mean).astype(jnp.float32)
        gate = jnp.where(blk_ids < j, gate, -jnp.inf)
        _, sel = lax.top_k(gate, topb)
        sel_valid = sel < j
        k_sel = k_bh[bi, hi, sel]
        v_sel = v_bh[bi, hi, sel]
        lp = jnp.einsum('bhqd,bhqnkd->bhqnk', qc, k_sel).astype(jnp.float32) * scale
        dist_p = qpos[None, None, :, None, None] - (sel[..., None] * MOBA_BLOCK + in_blk)
        lp = lp + bias_t[hi5, t5_bucket(dist_p)]
        lp = jnp.where(sel_valid[..., None], lp, -jnp.inf).reshape(B, H, MOBA_Q_CHUNK, topb * MOBA_BLOCK)
        k_own = lax.dynamic_slice_in_dim(k_bh, j, 1, axis=2)[:, :, 0]
        v_own = lax.dynamic_slice_in_dim(v_bh, j, 1, axis=2)[:, :, 0]
        lo = jnp.einsum('bhqd,bhkd->bhqk', qc, k_own).astype(jnp.float32) * scale
        dist_o = qpos[:, None] - (j * MOBA_BLOCK + in_blk)[None, :]
        lo = jnp.where(dist_o >= 0, lo + bias_t[:, t5_bucket(dist_o)][None], -jnp.inf)
        p = jax.nn.softmax(jnp.concatenate([lp, lo], axis=-1), axis=-1)
        pp = p[..., :topb * MOBA_BLOCK].reshape(B, H, MOBA_Q_CHUNK, topb, MOBA_BLOCK)
        po = p[..., topb * MOBA_BLOCK:]
        o = (jnp.einsum('bhqnk,bhqnkd->bhqd', pp.astype(v.dtype), v_sel)
             + jnp.einsum('bhqk,bhkd->bhqd', po.astype(v.dtype), v_own))
        return o.transpose(0, 2, 1, 3)

    o = lax.map(chunk, jnp.arange(S // MOBA_Q_CHUNK))
    return jnp.moveaxis(o, 0, 1).reshape(B, S, H * Dh)

def second_inputs(seed: int = 0) -> dict:
    key = jax.random.key(seed)
    ks = jax.random.split(key, 20)

    def nrm(k, shape, s):
        return jax.random.normal(k, shape, jnp.float32) * s

    return {
        'x': nrm(ks[0], (BATCH, SEQ, D_MODEL), 1.0),
        'c': nrm(ks[1], (BATCH, D_MODEL), 1.0),
        'rel_bias': nrm(ks[2], (N_BUCKETS, N_BIAS_HEADS), 0.5),
        'ada_w': nrm(ks[3], (DEPTH_2, D_MODEL, 6 * D_MODEL), D_MODEL ** -0.5),
        'ada_b': nrm(ks[4], (DEPTH_2, 6 * D_MODEL), 0.02),
        'norm_mix': 1.0 + nrm(ks[5], (DEPTH_2, D_MODEL), 0.02),
        'w_in': nrm(ks[6], (DEPTH_2, D_MODEL, IN_COLS), D_MODEL ** -0.5),
        'gate_b': nrm(ks[7], (DEPTH_2, G_COLS), 0.02),
        'diff_lambda': nrm(ks[8], (DEPTH_2, 4, HEAD_DIM), 0.1),
        'diff_subln': 1.0 + nrm(ks[9], (DEPTH_2, DIFF_V_DIM), 0.02),
        'dsa_kv_norm': 1.0 + nrm(ks[10], (DEPTH_2, DSA_LATENT), 0.02),
        'dsa_w_uv': nrm(ks[11], (DEPTH_2, DSA_HEADS, DSA_LATENT, DSA_V_DIM), DSA_LATENT ** -0.5),
        'w_br_a': nrm(ks[12], (DEPTH_2, A_V, D_MODEL), A_V ** -0.5),
        'w_br_b': nrm(ks[13], (DEPTH_2, DSA_HEADS * DSA_V_DIM, D_MODEL), (DSA_HEADS * DSA_V_DIM) ** -0.5),
        'w_br_c': nrm(ks[14], (DEPTH_2, C_QKV, D_MODEL), C_QKV ** -0.5),
        'w_o': nrm(ks[15], (DEPTH_2, D_MODEL, D_MODEL), D_MODEL ** -0.5),
        'norm_mlp': 1.0 + nrm(ks[16], (DEPTH_2, D_MODEL), 0.02),
        'w_ff1': nrm(ks[17], (DEPTH_2, D_MODEL, D_FF_2), D_MODEL ** -0.5),
        'w_ff2': nrm(ks[18], (DEPTH_2, D_FF_2, D_MODEL), D_FF_2 ** -0.5),
        'norm_final': 1.0 + nrm(ks[19], (D_MODEL,), 0.02),
    }

def second_block(x, c, rel_bias, ada_w, ada_b, norm_mix, w_in, gate_b, diff_lambda, diff_subln,
              dsa_kv_norm, dsa_w_uv, w_br_a, w_br_b, w_br_c, w_o, norm_mlp, w_ff1, w_ff2,
              norm_final):
    B, S, _ = x.shape
    bias_tab = rel_bias.astype(jnp.float32)
    bias_a = bias_tab[:, :DIFF_HEADS]
    bias_b = bias_tab[:, DIFF_HEADS:DIFF_HEADS + DSA_HEADS]
    bias_c = bias_tab[:, DIFF_HEADS + DSA_HEADS:]
    cond = jax.nn.silu(c)
    for l in range(DEPTH_2):
        mod = (cond @ ada_w[l] + ada_b[l]).reshape(B, 6, D_MODEL)[:, :, None, :]
        shift1, scale1, gate1 = mod[:, 0], mod[:, 1], mod[:, 2]
        shift2, scale2, gate2 = mod[:, 3], mod[:, 4], mod[:, 5]

        u = rmsnorm(x, norm_mix[l]) * (1.0 + scale1) + shift1
        aq, ak, av, bq, bkv, biq, bik, biw, cq, ck, cv, g = split_cols(u @ w_in[l])

        lam_init = 0.8 - 0.6 * math.exp(-0.3 * l)
        dl = diff_lambda[l].astype(jnp.float32)
        lam = jnp.exp(jnp.sum(dl[0] * dl[1])) - jnp.exp(jnp.sum(dl[2] * dl[3])) + lam_init
        y_a = diff_attention(aq.reshape(B, S, DIFF_HEADS, 2, HEAD_DIM),
                             ak.reshape(B, S, DIFF_HEADS, 2, HEAD_DIM),
                             av.reshape(B, S, DIFF_HEADS, DIFF_V_DIM),
                             lam, lam_init, diff_subln[l], bias_a) @ w_br_a[l]
        y_b = dsa_attention(bq.reshape(B, S, DSA_HEADS, DSA_LATENT),
                            rmsnorm(bkv, dsa_kv_norm[l]),
                            biq.reshape(B, S, IDX_HEADS, IDX_DIM), bik, biw,
                            dsa_w_uv[l], bias_b) @ w_br_b[l]
        y_c = moba_attention(cq.reshape(B, S, MOBA_HEADS, HEAD_DIM),
                             ck.reshape(B, S, MOBA_HEADS, HEAD_DIM),
                             cv.reshape(B, S, MOBA_HEADS, HEAD_DIM), bias_c) @ w_br_c[l]
        gates = jax.nn.sigmoid(g + gate_b[l]).reshape(B, S, 3, D_MODEL)
        merged = gates[:, :, 0] * y_a + gates[:, :, 1] * y_b + gates[:, :, 2] * y_c
        x = x + gate1 * (merged @ w_o[l])

        u2 = rmsnorm(x, norm_mlp[l]) * (1.0 + scale2) + shift2
        h = jnp.square(jax.nn.relu(u2 @ w_ff1[l]))
        x = x + gate2 * (h @ w_ff2[l])
    return rmsnorm(x, norm_final)


def setup_inputs(seed=0):
    out = dict(first_inputs(seed))
    for name, value in second_inputs(seed + 1).items():
        if name != "x":
            out[name + "_2"] = value
    return out


def reference(
    x, mem, ffn1_norm, ffn1_w_in, ffn1_w_out, mix_norm, xattn_norm, mem_norm, xattn_w_q,
    xattn_w_kv, xattn_w_o, ffn2_norm, ffn2_w_in, ffn2_w_out, pool_w, pool_b, pool_scale,
    nsa_w_in, nsa_cmp_pos, nsa_cmp_w1, nsa_cmp_w2, nsa_w_o, gla_w_in, gla_w_gate_up, gla_b_gate,
    gla_norm, gla_w_o, conv_w_in, conv_b_in, conv_dw, conv_b_dw, conv_ln_g, conv_ln_b,
    conv_w_out, conv_b_out, final_norm, c_2, rel_bias_2, ada_w_2, ada_b_2, norm_mix_2, w_in_2,
    gate_b_2, diff_lambda_2, diff_subln_2, dsa_kv_norm_2, dsa_w_uv_2, w_br_a_2, w_br_b_2,
    w_br_c_2, w_o_2, norm_mlp_2, w_ff1_2, w_ff2_2, norm_final_2,
):
    x = first_block(
        x, mem, ffn1_norm, ffn1_w_in, ffn1_w_out, mix_norm, xattn_norm, mem_norm, xattn_w_q,
        xattn_w_kv, xattn_w_o, ffn2_norm, ffn2_w_in, ffn2_w_out, pool_w, pool_b, pool_scale,
        nsa_w_in, nsa_cmp_pos, nsa_cmp_w1, nsa_cmp_w2, nsa_w_o, gla_w_in, gla_w_gate_up,
        gla_b_gate, gla_norm, gla_w_o, conv_w_in, conv_b_in, conv_dw, conv_b_dw, conv_ln_g,
        conv_ln_b, conv_w_out, conv_b_out, final_norm,
    )
    return second_block(
        x, c_2, rel_bias_2, ada_w_2, ada_b_2, norm_mix_2, w_in_2, gate_b_2, diff_lambda_2,
        diff_subln_2, dsa_kv_norm_2, dsa_w_uv_2, w_br_a_2, w_br_b_2, w_br_c_2, w_o_2,
        norm_mlp_2, w_ff1_2, w_ff2_2, norm_final_2,
    )


_drawn_inputs = setup_inputs


def setup_inputs(seed=0):
    import zlib

    import numpy as np

    out = dict(_drawn_inputs(seed))
    spreads = {}
    factors = {'ffn1_norm': 3.989,
     'mix_norm': 3.039,
     'xattn_norm': 8.0,
     'mem_norm': 8.0,
     'ffn2_norm': 5.268,
     'pool_b': 2.711,
     'norm_mix_2': 4.531,
     'gate_b_2': 8.0,
     'diff_lambda_2': 6.101,
     'diff_subln_2': 8.0,
     'dsa_kv_norm_2': 8.0,
     'norm_mlp_2': 3.582}
    for name, (base, spread) in spreads.items():
        noise = np.random.default_rng([zlib.crc32(name.encode()), seed]).standard_normal(out[name].shape)
        drawn = base * np.exp(spread * noise) if base else spread * noise
        out[name] = __import__('jax').numpy.asarray(drawn.astype(out[name].dtype))
    for name, factor in factors.items():
        out[name] = (out[name] * factor).astype(out[name].dtype)
    return out
```

```python
import math
from contextlib import ExitStack

import numpy as np

import concourse.bass as bass
from concourse import mybir

F32 = mybir.dt.float32
F32R = mybir.dt.float32r
ALU = mybir.AluOpType
ACT = mybir.ActivationFunctionType
AX = mybir.AxisListType.X

P = 128
D = 1024
S = 256
T = S // P
KD = D // P
FF = 2816
HI = 256
EPS = 1e-6
NEG = -1e30
BIG = 3.0e38

SLOTS = 4
SLAB = 2048

NSA_H, NSA_G, NSA_R, NSA_DH = 16, 4, 4, 64
N_CMP, CMP_BLOCK, CMP_STRIDE, CMP_HID = 15, 32, 16, 256
COLS = dict(aq=0, ak=512, av=1024, bq=1536, bkv=2048, biq=2176, bik=2432, biw=2464,
            cq=2472, ck=2728, cv=2984, g=3240)
N_BUCKETS, MAX_DISTANCE = 32, 128
TOPK = 64
LAM_INIT = 0.8 - 0.6 * math.exp(-0.3 * 0)
POOL_WINDOWS = (2, 4, 8, 16)

C_IDENT, C_FLIP, C_CAUSAL, C_CMP, C_VIS = 0, 128, 256, 512, 544
C_HOT, C_BAND, C_END = 546, 930, 930 + 4 * 384


def constant_table():
    c = np.zeros((P, C_END), np.float32)
    i = np.arange(P)
    c[i, C_IDENT + i] = 1.0
    c[i, C_FLIP + 127 - i] = 1.0
    q, k = i[:, None], i[None, :]
    c[:, C_CAUSAL + 128:C_CAUSAL + 256] = np.where(k <= q, 0.0, NEG)
    n = np.arange(N_CMP)
    for t in range(T):
        end = n * CMP_STRIDE + CMP_BLOCK - 1
        c[:, C_CMP + 16 * t:C_CMP + 16 * t + N_CMP] = np.where(end[None, :] <= 128 * t + q, 0.0, NEG)
    c[:, C_VIS] = i >= CMP_BLOCK - 1
    dist = 255 - np.arange(384)
    half = N_BUCKETS // 2
    nf = np.maximum(dist, 1).astype(np.float32)
    large = half + (np.log(nf / np.float32(half)) / np.float32(math.log(MAX_DISTANCE / half))
                    * np.float32(N_BUCKETS - half)).astype(np.int32)
    bucket = np.where(dist < half, dist, np.minimum(large, N_BUCKETS - 1))
    bucket = np.where(dist < 0, N_BUCKETS, bucket)
    c[bucket, C_HOT + np.arange(384)] = 1.0
    for w, win in enumerate(POOL_WINDOWS):
        for tile, to in ((0, np.arange(S)), (1, np.arange(P, S))):
            frm = tile * P + i
            gap = to[None, :] - frm[:, None]
            cnt = np.minimum(to + 1, win).astype(np.float32)
            m = np.where((gap >= 0) & (gap < win), np.float32(1) / cnt[None, :], 0) - (gap == 0)
            at = C_BAND + 384 * w + 256 * tile
            c[:, at:at + len(to)] = m
    return c


class Uses:

    def __init__(self):
        self.n = [0] * SLOTS

    def next(self, slot):
        self.n[slot] += 1
        return self.n[slot]


class Count:

    def __init__(self):
        self.n = 0

    def next(self, k=1):
        self.n += k
        return self.n


def build(nc, A, out):
    ds = bass.ds
    with ExitStack() as ctx:
        def sb(name, shape, dt=F32):
            return ctx.enter_context(nc.sbuf_tensor(name, shape, dt))

        def sem(name):
            return ctx.enter_context(nc.semaphore(name))

        raw = sb("raw", [P, SLOTS, SLAB])
        whi = sb("whi", [P, SLOTS, SLAB], F32R)
        wlo = sb("wlo", [P, SLOTS, SLAB], F32R)
        x = sb("x", [P, T, D])
        xn = sb("xn", [P, T, D])
        aT_hi = sb("aT_hi", [P, KD, S], F32R)
        aT_lo = sb("aT_lo", [P, KD, S], F32R)
        hs = sb("hs", [P, T, 512])
        hT_hi = sb("hT_hi", [P, 4, S], F32R)
        hT_lo = sb("hT_lo", [P, 4, S], F32R)
        gain = sb("gain", [P, 2, D])
        cst = sb("cst", [P, C_HOT])
        area = sb("area", [P, 14000])
        zero = sb("zero", [P, 512], F32R)
        small = sb("small", [P, 64])
        ps = ctx.enter_context(nc.psum_tensor("ps", [P, 8, 512], F32))

        ident = cst[:, C_IDENT:C_IDENT + 128]
        ssq, var, rstd = small[:, 0:2], small[:, 2:4], small[:, 4:6]
        minus_half = small[:, 6:8]
        nmx, den, rec = small[:, 8:14], small[:, 14:20], small[:, 20:26]

        landed = [sem(f"landed{s}") for s in range(SLOTS)]
        hi_ready = [sem(f"hi_ready{s}") for s in range(SLOTS)]
        lo_ready = [sem(f"lo_ready{s}") for s in range(SLOTS)]
        consumed = [sem(f"consumed{s}") for s in range(SLOTS)]
        stage_act, stage_dve = sem("stage_act"), sem("stage_dve")
        x_in, mem_in, const_in, gain_in = sem("x_in"), sem("mem_in"), sem("const_in"), [sem(f"gain_in{b}") for b in range(2)]
        zero_made, mix_in = sem("zero_made"), sem("mix_in")
        squared, rstd_made, rows_normed = sem("squared"), sem("rstd_made"), sem("rows_normed")
        rows_turned, aT_hi_made, aT_made = sem("rows_turned"), sem("aT_hi_made"), sem("aT_made")
        pool_step, act_step, dve_step = sem("pool_step"), sem("act_step"), sem("dve_step")
        act_evac, dve_evac = sem("act_evac"), sem("dve_evac")
        gate_half, silu_made, hid_made = sem("gate_half"), sem("silu_made"), sem("hid_made")
        hid_turned, hT_hi_made, hT_made = sem("hid_turned"), sem("hT_hi_made"), sem("hT_made")
        scored, maxed, exped, weighed = sem("scored"), sem("maxed"), sem("exped"), sem("weighed")
        probs_turned, probs_kept, pv_done = sem("probs_turned"), sem("probs_kept"), sem("pv_done")
        o_hi, o_kept = sem("o_hi"), sem("o_kept")
        pos_in, pos_made, w2_in, gelu_made, cmp_made = (sem(n) for n in ("pos_in", "pos_made", "w2_in", "gelu_made", "cmp_made"))
        cond_in, cond_turned, cond_made, ada_in = (sem(n) for n in ("cond_in", "cond_turned", "cond_made", "ada_in"))
        hot_in, dist_made, dist_out, skew_in = (sem(n) for n in ("hot_in", "dist_made", "dist_out", "skew_in"))
        lam_summed, row_in, gate_b_in, bias_turned = (sem(n) for n in ("lam_summed", "row_in", "gate_b_in", "bias_turned"))
        summed, powered, index_scored, lat_kept = (sem(n) for n in ("summed", "powered", "index_scored", "lat_kept"))
        branch_done, branch_kept, mask_row = sem("branch_done"), sem("branch_kept"), sem("mask_row")
        stored = sem("stored")

        kT = area[:, 0:2048].rearrange("p (k s) -> p k s", k=KD)
        vm = area[:, 2048:4096].rearrange("p (t d) -> p t d", t=T)
        qT = area[:, 4096:6144].rearrange("p (k s) -> p k s", k=KD)
        PT = area[:, 6144:8192]
        pool_b = area[:, 6144:7168]
        pool_s = area[:, 7168:8192]
        band = area[:, 8192:8192 + 4 * 384].rearrange("p (w c) -> p w c", w=4)
        xnf = xn[:, :, :].rearrange("p t n -> p (t n)")
        hsf = hs[:, :, :].rearrange("p t n -> p (t n)")
        Pb = [xnf[:, 528 * b:528 * b + 528] for b in range(2)]
        ksT = area[:, 6144:7168].rearrange("p (g s) -> p g s", g=4)
        kwT = area[:, 7168:8192].rearrange("p (g s) -> p g s", g=4)
        vs = area[:, 8192:8704].rearrange("p (t n) -> p t n", t=T)
        vw = area[:, 8704:9216].rearrange("p (t n) -> p t n", t=T)
        gates = area[:, 9216:9312].rearrange("p (t n) -> p t n", t=T)
        blk = area[:, 9344:11264].rearrange("p (v j g n) -> p v j g n", v=2, j=16, g=4)
        nsaP = [area[:, 9344 + 2048 * b:11392 + 2048 * b].rearrange("p (r n) -> p r n", r=4) for b in range(2)]
        nsaPc = [a.rearrange("p (r n) -> p r n", r=4) for a in (area[:, 13440:13952], xnf[:, 1056:1568])]
        pos_rows, posT = hsf[0:32, 0:128], hsf[:, 128:160]
        hidT = hsf[:, 160:400].rearrange("p (v h n) -> p v h n", v=2, h=2)
        w2k = hsf[:, 400:656].rearrange("p (h n) -> p h n", h=2)
        w2v = hsf[:, 656:784].rearrange("p (h n) -> p h n", h=2)
        kcT = xnf[:, 1568:1628]
        vcmp = xnf[0:15, 1628:1884]
        aTf_hi = aT_hi[:, :, :].rearrange("p k s -> p (k s)")
        aTf_lo = aT_lo[:, :, :].rearrange("p k s -> p (k s)")

        yT = area[:, 0:2048].rearrange("p (k s) -> p k s", k=KD)
        yTf = area[:, 0:2048]
        mod = area[:, 0:3072]
        out_gate = area[:, 2048:3072]
        bgate = area[:, 3072:9216].rearrange("p (t n) -> p t n", t=T)
        aqT = area[:, 9216:10240].rearrange("p (k s) -> p k s", k=4)
        akT = area[:, 10240:11264].rearrange("p (k s) -> p k s", k=4)
        av = area[:, 11264:12288].rearrange("p (t n) -> p t n", t=T)
        bqT = area[:, 9216:10240].rearrange("p (k s) -> p k s", k=4)
        kvn = area[:, 10240:10496].rearrange("p (t n) -> p t n", t=T)
        iqT = area[:, 10496:11008].rearrange("p (k s) -> p k s", k=2)
        ikT = area[:, 11008:11264]
        cqT = area[:, 11264:11776].rearrange("p (k s) -> p k s", k=2)
        ckT = area[:, 11776:12288].rearrange("p (k s) -> p k s", k=2)
        cv = area[:, 12288:12800].rearrange("p (t n) -> p t n", t=T)
        iw = area[:, 12800:12816].rearrange("p (t n) -> p t n", t=T)
        bias = area[:, 12816:13840].rearrange("p (h k) -> p h k", h=4)
        kvT = area[:, 1536:1792]
        w_uv = area[:, 1792:2048].rearrange("p (h e) -> p h e", h=4)
        oA = hsf.rearrange("p (t h e) -> p t h e", t=T, h=4)
        PTd = hsf.rearrange("p (h m q) -> p h m q", h=4, m=2)
        skew = hsf.rearrange("p (h k) -> p h k", h=4)
        PTu = [xnf[:, 1056 + 256 * b:1312 + 256 * b] for b in range(2)]
        o_lat, score_part = xnf[:, 1056:1568], xnf[:, 1568:1824]
        sel, work, top8 = Pb[0][:, 256:512], Pb[1][:, 256:512], xnf[:, 1824:1832]
        subln, kv_gain = xnf[:, 1568:1696], xnf[:, 1832:1960]
        cond_rows, condT = hsf[0:8, 0:128], hsf[:, 128:136]
        hot, rel, dist_rows = xnf[0:33, 0:384], xnf[0:33, 384:396], xnf[0:12, 512:896]
        lam_in, lam_prod = xnf[:, 1024:1280], xnf[:, 1280:1408]
        neg_lam, lam2 = small[:, 60:61], small[:, 58:60]
        ss8, var8, rstd8, minus_half8 = (small[:, c:c + 8] for c in (26, 34, 42, 50))
        dist_dram = nc.dram_tensor("dist_rows", (12, 384), F32, kind="Internal").ap()

        def twice(slot):
            return (whi[:, slot, :].rearrange("p (g a n) -> p g a n", a=2, n=64),
                    raw[:, slot, 0:SLAB // 2].rearrange("p (g n) -> p g n", n=64).unsqueeze(2)
                    .to_broadcast([P, SLAB // 128, 2, 64]))

        def PTc(h):
            return PT[:, 512 * (h % 2):512 * (h % 2) + 512].rearrange("p (m q) -> p m q", m=2)

        L = range(2)
        gains = []
        for l in L:
            gains += [A["mem_norm"][l], A["ffn1_norm"][l], A["mix_norm"][l], A["xattn_norm"][l], A["ffn2_norm"][l]]

        gains += [A["final_norm"], A["norm_mix_2"][0], A["norm_mlp_2"][0], A["norm_final_2"]]

        block = ctx.enter_context(nc.Block())

        def program(e):
            for l in L:
                e.norm(5 * l, mem=True)
                e.kv(l)
                e.norm(5 * l + 1)
                e.ffn(A["ffn1_w_in"][l], A["ffn1_w_out"][l])
                e.norm(5 * l + 2, turn=l > 0)
                if l == 0:
                    e.pool()
                else:
                    e.nsa_inputs()
                    e.nsa_compress()
                    e.nsa_attend()
                    e.project(A["nsa_w_o"][0])
                e.norm(5 * l + 3)
                e.query(l)
                e.cross()
                e.project(A["xattn_w_o"][l])
                e.norm(5 * l + 4)
                e.ffn(A["ffn2_w_in"][l], A["ffn2_w_out"][l])
            e.norm(10, turn=False, keep=True)
            e.cond(0)
            e.ada(0)
            e.norm(11, modulate=True)
            e.gate_inputs()
            e.diff_inputs()
            e.diff()
            e.diff_norm()
            e.sparse_inputs()
            e.latent()
            e.select(0)
            e.dsa(0)
            e.select(1)
            e.dsa(1)
            e.moba()
            e.merge()
            e.project(A["w_o_2"][0], gated=True)
            e.cond(1)
            e.ada(1)
            e.norm(12, modulate=True)
            e.mlp()
            e.norm(13, turn=False, keep=True)
            e.end()

        @block.sync
        def _(sp):
            uses = Uses()
            stages = Count()

            def slab(slot, halves, n=None):
                if n is None:
                    n = uses.next(slot)
                if not (type(n) is int and n == 1):
                    sp.wait_ge(lo_ready[slot], n - 1)
                for dst, src in halves:
                    sp.dma_start(dst, src).then_inc(landed[slot], 16)

            def pieces(w, cols, n, pair):
                wv = w.rearrange("(k p) n -> p k n", p=P)
                for s in range(2):
                    d = raw[:, pair + s, 0:4 * n].rearrange("p (k n) -> p k n", k=4)
                    slab(pair + s, [(d[:, :, to:to + m], wv[:, 4 * s:4 * s + 4, c:c + m]) for to, c, m in cols])

            def chunk(w, c0, n, pair):
                wv = w.rearrange("(k p) n -> p k n", p=P)
                for s in range(2):
                    d = raw[:, pair + s, 0:4 * n].rearrange("p (k n) -> p k n", k=4)
                    slab(pair + s, [(d[:, 2 * j:2 * j + 2, :],
                                     wv[:, 4 * s + 2 * j:4 * s + 2 * j + 2, c0:c0 + n]) for j in range(2)])

            class Sp:
                def norm(self, m, mem=False, turn=True, keep=False, modulate=False):
                    stages.next()

                def kv(self, l):
                    stages.next()
                    for c in range(4):
                        chunk(A["xattn_w_kv"][l], 512 * c, 512, 2 * (c % 2))

                def ffn(self, w_in, w_out):
                    stages.next()
                    rounds = FF // HI
                    wi = w_in.rearrange("(k p) n -> p k n", p=P)
                    wo = w_out.rearrange("(k p) n -> p k n", p=P)

                    def up(i, base):
                        for s in range(2):
                            d = raw[:, s, :].rearrange("p (k h n) -> p k h n", k=4, h=2)
                            slab(s, [(d[:, :, h, :], wi[:, 4 * s:4 * s + 4, ds(FF * h + i * HI, HI)])
                                     for h in range(2)], base[s] + i + 1)

                    def down(i, base):
                        d = raw[:, 2, :].rearrange("p (k n) -> p k n", k=2)
                        slab(2, [(d[:, j:j + 1, :], wo[:, ds(2 * i + j, 1), :]) for j in range(2)],
                             base[2] + i + 1)

                    base = list(uses.n)
                    up(0, base)
                    with sp.Fori(1, rounds) as i:
                        up(i, base)
                        down(i - 1, base)
                    down(rounds - 1, base)
                    for s in range(3):
                        uses.n[s] += rounds

                def pool(self):
                    stages.next()
                    chunk(A["xattn_w_q"][0], 0, 512, 0)
                    w = A["pool_w"][0].rearrange("g (k p) n -> p (g k) n", p=P)
                    d = raw[:, 2, :].rearrange("p (k n) -> p k n", n=256)
                    slab(2, [(d[:, 4 * j:4 * j + 4, :], w[:, 4 * j:4 * j + 4, :]) for j in range(2)])

                def query(self, l):
                    stages.next()
                    for c in range(1 if l == 0 else 0, 2):
                        chunk(A["xattn_w_q"][l], 512 * c, 512, 2 * c)

                def cross(self):
                    stages.next()

                def project(self, w, gated=False):
                    stages.next()
                    for c in range(2):
                        chunk(w, 512 * c, 512, 2 * c)

                def nsa_inputs(self):
                    stages.next()
                    w = A["nsa_w_in"][0]
                    for c in range(2):
                        chunk(w, 512 * c, 512, 2 * c)
                    for c, c0 in enumerate((1024, 1280, 1536, 2048)):
                        chunk(w, c0, 256, 2 * (c % 2))
                    wv = w.rearrange("(k p) n -> p k n", p=P)
                    for s in range(2):
                        d = raw[:, s, :].rearrange("p (k h n) -> p k h n", k=4, h=2)
                        slab(s, [(d[:, :, h, :], wv[:, 4 * s:4 * s + 4, c0:c0 + 256]) for h, c0 in enumerate((1792, 2304))])
                    chunk(w, 2560, 48, 2)

                def nsa_compress(self):
                    stages.next()
                    for v in range(2):
                        w = A["nsa_cmp_w1"][0, v].rearrange("(j p) n -> p j n", p=P)
                        for s in range(2):
                            d = raw[:, 2 * v + s, :].rearrange("p (j n) -> p j n", j=8)
                            slab(2 * v + s, [(d[:, 4 * j:4 * j + 4, :], w[:, 8 * s + 4 * j:8 * s + 4 * j + 4, :])
                                             for j in range(2)])

                def nsa_attend(self):
                    stages.next()

                def skip(self, *_):
                    stages.next()

                cond = diff = diff_norm = latent = select = dsa = skip

                def moba(self):
                    stages.next(2)

                def ada(self, part):
                    stages.next()
                    for c in range(6):
                        chunk(A["ada_w_2"][0], 3072 * part + 512 * c, 512, 2 * (c % 2))

                def gate_inputs(self):
                    stages.next()
                    for c in range(6):
                        chunk(A["w_in_2"][0], COLS["g"] + 512 * c, 512, 2 * (c % 2))

                def diff_inputs(self):
                    stages.next(2)
                    for c, n in enumerate(("aq", "ak", "av")):
                        chunk(A["w_in_2"][0], COLS[n], 512, 2 * (c % 2))

                def sparse_inputs(self):
                    stages.next(2)
                    w = A["w_in_2"][0]
                    chunk(w, COLS["bq"], 512, 0)
                    pieces(w, [(0, COLS["bkv"], 384)] + [(384 + 32 * j, COLS["bik"], 32) for j in range(4)], 512, 2)
                    chunk(w, COLS["cq"], 512, 0)
                    pieces(w, [(0, COLS["cv"], 256), (256, COLS["biw"], 8)], 264, 2)

                def merge(self):
                    stages.next()
                    a = A["w_br_a_2"][0].rearrange("(k p) n -> p k n", p=P)
                    for s in range(2):
                        d = raw[:, s, :].rearrange("p (k n) -> p k n", k=4)
                        slab(s, [(d[:, 2 * j:2 * j + 2, :], a[:, 2 * j:2 * j + 2, 512 * s:512 * s + 512]) for j in range(2)])
                    for s, n in ((2, "w_br_b_2"), (3, "w_br_c_2")):
                        w = A[n][0].rearrange("(k p) n -> p k n", p=P)
                        d = raw[:, s, :].rearrange("p (k n) -> p k n", k=2)
                        slab(s, [(d[:, j:j + 1, :], w[:, j:j + 1, :]) for j in range(2)])

                def mlp(self):
                    stages.next()
                    rounds = 8
                    wi = A["w_ff1_2"][0].rearrange("(k p) n -> p k n", p=P)
                    wo = A["w_ff2_2"][0].rearrange("(k p) n -> p k n", p=P)
                    base = list(uses.n)

                    def up(i):
                        for s in range(2):
                            d = raw[:, s, :].rearrange("p (k n) -> p k n", k=4)
                            slab(s, [(d[:, 2 * j:2 * j + 2, :], wi[:, 4 * s + 2 * j:4 * s + 2 * j + 2, ds(512 * i, 512)])
                                     for j in range(2)], base[s] + i + 1)

                    def down(i):
                        for s in range(2):
                            d = raw[:, 2 + s, :].rearrange("p (k n) -> p k n", k=2)
                            slab(2 + s, [(d[:, j:j + 1, :], wo[:, ds(4 * i + 2 * s + j, 1), :]) for j in range(2)],
                                 base[2 + s] + i + 1)

                    up(0)
                    with sp.Fori(1, rounds) as i:
                        up(i)
                        down(i - 1)
                    down(rounds - 1)
                    for s in range(4):
                        uses.n[s] += rounds

                def end(self):
                    sp.wait_ge(stage_act, stages.n)
                    sp.wait_ge(stage_dve, stages.n)

            for t in range(T):
                sp.dma_start(x[:, t, :], A["x"][0, t * P:(t + 1) * P, :]).then_inc(x_in, 16)
            sp.dma_start(cst[:, :], A["constants"][:, 0:C_HOT]).then_inc(const_in, 16)
            program(Sp())
            for t in range(T):
                sp.dma_start(out[0, t * P:(t + 1) * P, :], x[:, t, :]).then_inc(stored, 16)
            sp.wait_ge(stored, 16 * T)

        @block.gpsimd
        def _(pool):
            stages, steps = Count(), Count()
            squares = Count()

            def enter():
                if stages.n:
                    pool.wait_ge(stage_act, stages.n)
                    pool.wait_ge(stage_dve, stages.n)
                stages.next()

            def load_gain(m):
                pool.dma_start(gain[:, m % 2, :], gains[m].unsqueeze(0).to_broadcast([P, D])).then_inc(gain_in[m % 2], 16)

            def power(src, dst, n, mean):
                pool.tensor_scalar(var8[:, 0:n], src, 1.0 / mean, EPS, ALU.mult, ALU.add).then_inc(pool_step, 1)
                pool.wait_ge(pool_step, steps.next())
                return pool.tensor_tensor(dst, var8[:, 0:n], minus_half8[:, 0:n], ALU.pow)

            def spread(to, row, done):
                pool.dma_start(to, row.unsqueeze(0).to_broadcast([P, row.shape[0]])).then_inc(done, 16)

            def load_skew(b):
                pool.dma_start(skew, bass.AP(dist_dram.tensor, 4 * 384 * b, [[1, P], [384, 4], [1, S]])).then_inc(skew_in, 16)

            class Pool:
                def norm(self, m, mem=False, turn=True, keep=False, modulate=False):
                    enter()
                    if mem:
                        for t in range(T):
                            pool.dma_start(xn[:, t, :], A["mem"][0, t * P:(t + 1) * P, :]).then_inc(mem_in, 16)
                    if m + 1 < len(gains):
                        load_gain(m + 1)
                    pool.wait_ge(squared, squares.next(2))
                    power(ssq, rstd, T, D).then_inc(rstd_made, 1)

                def kv(self, l):
                    enter()

                def ffn(self, w_in, w_out):
                    enter()

                def pool(self):
                    enter()
                    pool.dma_start(pool_b, A["pool_b"][0].unsqueeze(0).to_broadcast([P, D])).then_inc(mix_in, 16)
                    pool.dma_start(pool_s, A["pool_scale"][0].unsqueeze(0).to_broadcast([P, D])).then_inc(mix_in, 16)
                    pool.dma_start(area[:, 8192:8192 + 4 * 384], A["constants"][:, C_BAND:C_END]).then_inc(mix_in, 16)

                def query(self, l):
                    enter()

                def cross(self):
                    enter()

                def project(self, w, gated=False):
                    enter()

                def nsa_inputs(self):
                    enter()
                    pool.dma_start(pos_rows, A["nsa_cmp_pos"][0].rearrange("v (j a) d -> (v j) (a d)", a=2))\
                        .then_inc(pos_in, 16)
                    for to, v in ((w2k[:, :, 0:64], 0), (w2k[:, :, 64:128], 0), (w2v, 1)):
                        pool.dma_start(to, A["nsa_cmp_w2"][0, v].rearrange("(h p) n -> p h n", p=P)).then_inc(w2_in, 16)

                def nsa_compress(self):
                    enter()

                def nsa_attend(self):
                    enter()

                def cond(self, part):
                    enter()
                    pool.dma_start(cond_rows, A["c_2"].rearrange("a (r n) -> (a r) n", r=8)).then_inc(cond_in, 16)
                    spread(mod, A["ada_b_2"][0][3072 * part:3072 * part + 3072], ada_in)
                    if part == 0:
                        pool.dma_start(hot, A["constants"][0:33, C_HOT:C_HOT + 384]).then_inc(hot_in, 16)
                        pool.dma_start(rel[0:32], A["rel_bias_2"]).then_inc(hot_in, 16)
                        pool.memset(rel[32:33], NEG).then_inc(mask_row, 1)
                        spread(lam_in, A["diff_lambda_2"][0].rearrange("a d -> (a d)"), hot_in)
                        pool.wait_ge(dist_made, 3)
                        pool.dma_start(dist_dram, dist_rows).then_inc(dist_out, 16)

                def ada(self, part):
                    enter()

                def gate_inputs(self):
                    enter()
                    for t in range(T):
                        spread(bgate[:, t, :], A["gate_b_2"][0], gate_b_in)

                def diff_inputs(self):
                    enter()
                    pool.wait_ge(dist_out, 16)
                    load_skew(0)
                    spread(subln, A["diff_subln_2"][0], row_in)
                    enter()

                def diff(self):
                    enter()

                def diff_norm(self):
                    enter()
                    pool.wait_ge(summed, 1)
                    power(ss8, rstd8, 8, P).then_inc(powered, 1)

                def sparse_inputs(self):
                    enter()
                    load_skew(1)
                    spread(kv_gain, A["dsa_kv_norm_2"][0], row_in)
                    pool.dma_start(w_uv, A["dsa_w_uv_2"][0].rearrange("h r e -> r h e")).then_inc(row_in, 16)
                    enter()

                def latent(self):
                    enter()
                    pool.wait_ge(summed, 3)
                    power(ss8[:, 0:2], rstd8[:, 0:2], 2, P).then_inc(powered, 1)

                def select(self, t):
                    enter()

                def dsa(self, t):
                    enter()

                def moba(self):
                    enter()
                    load_skew(2)
                    enter()

                def merge(self):
                    enter()

                def mlp(self):
                    enter()

                def end(self):
                    pass

            pool.memset(minus_half8, -0.5).then_inc(pool_step, 1)
            pool.wait_ge(pool_step, steps.next())
            pool.memset(minus_half, -0.5).then_inc(pool_step, 1)
            pool.memset(zero.bitcast(F32)[:, :], 0.0).then_inc(zero_made, 1)
            pool.wait_ge(pool_step, steps.next())
            load_gain(0)
            program(Pool())

        @block.scalar
        def _(act):
            stages, steps, uses, done = Count(), Count(), Uses(), Uses()
            c_sq, c_norm, c_turned, c_ffn, c_turn = Count(), Count(), Count(), Count(), Count()
            units, groups = Count(), Count()

            def enter():
                if stages.n:
                    act.wait_ge(stage_dve, stages.n)
                    act.wait_ge(stage_act, stages.n)
                stages.next()

            def leave():
                act.drain().then_inc(stage_act, 1)

            arrived = [0] * SLOTS

            def split(slot, n=None, doubled=False, transfers=2):
                if n is None:
                    n = uses.next(slot)
                if type(n) is int:
                    arrived[slot] += 16 * transfers
                    act.wait_ge(landed[slot], arrived[slot])
                else:
                    act.wait_ge(landed[slot], 32 * n + (arrived[slot] - 32 * uses.n[slot]))
                if not (type(n) is int and n == 1):
                    act.wait_ge(consumed[slot], n - 1)
                to, of = twice(slot) if doubled else (whi[:, slot, :], raw[:, slot, :])
                act.activation(to, of, ACT.Copy).then_inc(hi_ready[slot], 1)

            def chunks(count, evac, doubled=(), transfers=()):
                for c in range(count):
                    if c + 1 < count:
                        for s in range(2):
                            split(2 * ((c + 1) % 2) + s, doubled=c + 1 in doubled,
                                  transfers=dict(transfers).get(c + 1, 2))
                    pair = 2 * (c % 2)
                    done.next(pair)
                    act.wait_ge(consumed[pair + 1], done.next(pair + 1))
                    evac(c, 4 * (chunk_no.n % 2)).then_inc(act_evac, 1)
                    chunk_no.next()

            chunk_no = Count()

            def next_slabs():
                for s in range(2):
                    split(s)

            def turned(banks):
                for b in range(banks):
                    act.wait_ge(rows_turned, c_turned.next())
                    t, k = b // 2, 4 * (b % 2)
                    act.activation(aT_hi[:, k:k + 4, t * P:(t + 1) * P],
                                   ps[:, b, :].rearrange("p (k n) -> p k n", k=4), ACT.Copy).then_inc(aT_hi_made, 1)

            class Act:
                def norm(self, m, mem=False, turn=True, keep=False, modulate=False):
                    enter()
                    if mem:
                        act.wait_ge(mem_in, 32 * (m // 5 + 1))
                    src = xn if mem else x
                    for t in range(T):
                        if mem and t:
                            act.wait_ge(squared, c_sq.n)
                        junk = hs[:, :, :].rearrange("p t n -> p (t n)") if mem else xn[:, t, :]
                        act.activation(junk, src[:, t, :], ACT.Square, accum_out=ssq[:, t:t + 1])\
                           .then_inc(squared, 1)
                        c_sq.next()
                    if turn:
                        turned(4)
                    leave()

                def kv(self, l):
                    enter()

                    def evac(c, b):
                        if c < 2:
                            return act.activation(kT[:, 4 * c:4 * c + 2, :], ps[:, b, :], ACT.Copy)
                        return act.activation(vm[:, 0, 512 * (c - 2):512 * (c - 1)], ps[:, b, :], ACT.Copy)
                    chunks(4, evac)
                    leave()
                    next_slabs()

                def ffn(self, w_in, w_out):
                    enter()
                    rounds = FF // HI
                    ub, db, fb = list(uses.n), list(done.n), c_ffn.n

                    def first_half(i):
                        act.wait_ge(gate_half, fb + i + 1)
                        act.activation(hs[:, 0, 0:HI], ps[:, 4, 0:HI], ACT.Silu).then_inc(silu_made, 1)
                        act.wait_ge(consumed[1], db[1] + i + 1)
                        act.activation(hs[:, 1, 0:HI], ps[:, 5, 0:HI], ACT.Silu).then_inc(silu_made, 1)

                    def second_half(i):
                        act.wait_ge(hid_turned, fb + i + 1)
                        act.activation(hT_hi[:, 0:2, :], ps[:, 6, :], ACT.Copy).then_inc(hT_hi_made, 1)

                    with act.Fori(0, rounds) as i:
                        split(0, ub[0] + i + 1)
                        first_half(i)
                        split(1, ub[1] + i + 1)
                        second_half(i)
                        split(2, ub[2] + i + 1)
                    for s in range(3):
                        uses.n[s] += rounds
                        done.n[s] += rounds
                        arrived[s] += 32 * rounds
                    c_ffn.next(rounds)
                    leave()

                def pool(self):
                    enter()
                    split(2)
                    for b in range(4):
                        act.wait_ge(rows_turned, c_turned.next())
                        act.activation(aT_hi[:, 2 * b:2 * b + 2, :], ps[:, b, :], ACT.Copy).then_inc(aT_hi_made, 1)
                    done.next(2)
                    leave()

                def query(self, l):
                    enter()
                    chunks(2, lambda c, b: act.activation(qT[:, 4 * c:4 * c + 2, :], ps[:, b, :], ACT.Copy,
                                                          scale=1.0 / 16))
                    leave()
                    next_slabs()

                def cross(self):
                    enter()

                    def exps(u):
                        U = units.n + u
                        act.wait_ge(maxed, U + 1)
                        if u >= 2:
                            act.wait_ge(probs_turned, U - 1)
                        act.activation(Pb[u % 2][:, 0:S], ps[:, u % 2, 0:S], ACT.Exp, bias=nmx[:, 3 * (u % 2):3 * (u % 2) + 1],
                                       accum_out=den[:, 3 * (u % 2):3 * (u % 2) + 1]).then_inc(exped, 1)

                    def keep(u):
                        h, t = u // 2, u % 2
                        act.wait_ge(probs_turned, units.n + u + 1)
                        if h >= 2:
                            act.wait_ge(pv_done, groups.n + h - 1)
                        act.activation(PTc(h)[:, :, t * P:(t + 1) * P],
                                       ps[:, 2 + u % 2, 0:S].rearrange("p (m q) -> p m q", m=2),
                                       ACT.Copy).then_inc(probs_kept, 1)

                    def out_hi(h):
                        act.wait_ge(pv_done, groups.n + h + 1)
                        act.activation(aT_hi[:, 2 * h:2 * h + 2, :], ps[:, 4 + h % 2, :], ACT.Copy).then_inc(o_hi, 1)

                    exps(0)
                    for u in range(8):
                        if u + 1 < 8:
                            exps(u + 1)
                        keep(u)
                        if u % 2 == 0 and u:
                            out_hi(u // 2 - 1)
                    out_hi(3)
                    units.next(8)
                    groups.next(4)
                    leave()

                def project(self, w, gated=False):
                    enter()
                    if gated:
                        turned(4)
                    chunks(2, lambda c, b: act.drain())
                    leave()
                    next_slabs()

                def nsa_inputs(self):
                    enter()

                    def evac(c, b):
                        if c < 2:
                            return act.activation(qT[:, 4 * c:4 * c + 2, :], ps[:, b, :], ACT.Copy, scale=0.125)
                        if c < 4:
                            return act.drain()
                        if c < 6:
                            return act.activation((ksT, kwT)[c - 4][:, 0:2, :], ps[:, b, :], ACT.Copy)
                        if c == 6:
                            return act.activation(area[:, 8192:9216].rearrange("p (v t n) -> p t v n", v=2, t=2)[:, 0],
                                                  ps[:, b, :].rearrange("p (v n) -> p v n", v=2), ACT.Copy)
                        return act.activation(gates[:, :, :], ps[:, b, 0:96].rearrange("p (t n) -> p t n", t=2),
                                              ACT.Sigmoid)
                    chunks(8, evac, range(2, 6))
                    leave()
                    next_slabs()

                def nsa_compress(self):
                    enter()
                    act.activation(aTf_hi[:, 0:1920], area[:, 9344:11264], ACT.Copy).then_inc(aT_hi_made, 1)
                    split(2)
                    split(3)
                    for v in range(2):
                        done.next(2 * v)
                        act.wait_ge(consumed[2 * v + 1], done.next(2 * v + 1))
                        act.activation(hidT[:, v], ps[:, v, 0:128].rearrange("p (h n) -> p h n", h=2)[:, :, 0:60],
                                       ACT.Gelu_apprx_tanh).then_inc(gelu_made, 1)
                    act.wait_ge(cmp_made, 1)
                    act.activation(kcT, ps[:, 2, 0:60], ACT.Copy)
                    act.wait_ge(cmp_made, 2)
                    act.activation(vcmp, ps[0:15, 3, 0:256], ACT.Copy)
                    leave()
                    next_slabs()

                def nsa_attend(self):
                    enter()

                    def exps(u):
                        U, t, b = units.n + u, u // 4 % 2, 3 * (u % 2)
                        w = P * (t + 1)
                        act.wait_ge(maxed, U + 1)
                        for j, (c, n) in enumerate(((512, N_CMP), (0, w), (w, w))):
                            last = act.activation(Pb[u % 2][:, c:c + n], Pb[u % 2][:, c:c + n], ACT.Exp, scale=-1.0,
                                                  bias=nmx[:, b + j:b + j + 1], accum_out=den[:, b + j:b + j + 1])
                        last.then_inc(exped, 1)

                    def keep(u):
                        gi, t, r = u // 4, u // 4 % 2, u % 4
                        act.wait_ge(probs_turned, units.n + u + 1)
                        if gi >= 2:
                            act.wait_ge(pv_done, groups.n + gi - 1)
                        act.activation(nsaPc[gi % 2][0:N_CMP, r, :], ps[0:N_CMP, 6 + u % 2, P:2 * P], ACT.Copy)
                        act.activation(nsaP[gi % 2][:, r, 0:2 * P * (t + 1)], ps[:, 2 + u % 2, 0:2 * P * (t + 1)], ACT.Copy)\
                           .then_inc(probs_kept, 1)

                    def out_hi(gi):
                        g, t = gi // 2, gi % 2
                        act.wait_ge(pv_done, groups.n + gi + 1)
                        act.activation(aT_hi[:, 2 * g:2 * g + 2, t * P:(t + 1) * P],
                                       ps[:, 4 + gi % 2, 0:256].rearrange("p (j q) -> p j q", j=2), ACT.Copy).then_inc(o_hi, 1)

                    exps(0)
                    for u in range(32):
                        if u + 1 < 32:
                            exps(u + 1)
                        keep(u)
                        if u % 4 == 0 and u:
                            out_hi(u // 4 - 1)
                    out_hi(7)
                    units.next(32)
                    groups.next(8)
                    leave()

                def cond(self, part):
                    enter()
                    act.wait_ge(cond_turned, part + 1)
                    act.activation(condT, ps[:, 0, 0:8], ACT.Silu).then_inc(cond_made, 1)
                    act.wait_ge(cond_made, 3 * part + 1)
                    act.activation(aT_hi[:, :, 0:P], condT.unsqueeze(2).to_broadcast([P, KD, P]), ACT.Copy).then_inc(cond_made, 1)
                    if part == 0:
                        act.wait_ge(dist_made, 1)
                        act.activation(dist_rows, ps[0:12, 1, 0:384], ACT.Copy).then_inc(dist_made, 1)
                        act.wait_ge(lam_summed, 2)
                        act.activation(lam2, lam2, ACT.Exp).then_inc(dist_made, 1)
                    leave()

                def ada(self, part):
                    enter()
                    chunks(6, lambda c, b: act.drain())
                    act.wait_ge(dist_out, 16)
                    leave()
                    next_slabs()

                def gate_inputs(self):
                    enter()

                    def evac(c, b):
                        act.wait_ge(dve_evac, chunk_no.n + 1)
                        return act.activation(bgate[:, :, 512 * c:512 * c + 512], bgate[:, :, 512 * c:512 * c + 512], ACT.Sigmoid)
                    chunks(6, evac)
                    leave()
                    next_slabs()

                def keep_bias(self, b):
                    act.wait_ge(bias_turned, b + 1)
                    act.activation(bias[:, 0:2, :], ps[:, 4, :].rearrange("p (h k) -> p h k", h=2), ACT.Copy)

                def diff_inputs(self):
                    enter()

                    def evac(c, b):
                        if c < 2:
                            return act.activation((aqT, akT)[c][:, 0:2, :], ps[:, b, :], ACT.Copy, scale=(0.125, 1.0)[c])
                        return act.activation(av[:, 0, :], ps[:, b, :], ACT.Copy)
                    chunks(3, evac)
                    leave()
                    next_slabs()
                    enter()
                    self.keep_bias(0)
                    leave()

                def exps(self, u, segs, U):
                    b = 3 * (u % 2)
                    act.wait_ge(maxed, U + 1)
                    for j, (c, n) in enumerate(segs):
                        last = act.activation(Pb[u % 2][:, c:c + n], Pb[u % 2][:, c:c + n], ACT.Exp, scale=-1.0,
                                              bias=nmx[:, b + j:b + j + 1], accum_out=den[:, b + j:b + j + 1])
                    last.then_inc(exped, 1)

                def diff(self):
                    enter()

                    def exps(u):
                        w = P * (u % 2 + 1)
                        self.exps(u, ((0, w), (w, w)), units.n + u)

                    def keep(u):
                        w = P * (u % 2 + 1)
                        act.wait_ge(probs_turned, units.n + u + 1)
                        if u >= 2:
                            act.wait_ge(pv_done, groups.n + u - 1)
                        act.activation(PTu[u % 2][:, 0:w], ps[:, 4 + u % 2, 0:w], ACT.Copy).then_inc(probs_kept, 1)

                    def out(u):
                        act.wait_ge(pv_done, groups.n + u + 1)
                        act.activation(oA[:, u % 2, u // 2, :], ps[:, 6 + u % 2, 0:P], ACT.Copy).then_inc(o_hi, 1)

                    exps(0)
                    for u in range(8):
                        if u + 1 < 8:
                            exps(u + 1)
                        keep(u)
                        if u:
                            out(u - 1)
                    out(7)
                    units.next(8)
                    groups.next(8)
                    leave()

                def diff_norm(self):
                    enter()
                    act.wait_ge(branch_done, 1)
                    act.activation(yT[:, 0:2, :], ps[:, 0, :], ACT.Copy)
                    leave()

                def sparse_inputs(self):
                    enter()

                    def evac(c, b):
                        if c == 0:
                            return act.activation(bqT[:, 0:2, :], ps[:, b, :], ACT.Copy, scale=P ** -0.5)
                        if c == 1:
                            act.activation(kvn, ps[:, b, 0:256].rearrange("p (t n) -> p t n", t=T), ACT.Copy)
                            return act.activation(iqT, ps[:, b + 1, :].rearrange("p (k n) -> p k n", k=2), ACT.Copy)
                        if c == 2:
                            return act.activation(cqT, ps[:, b, :].rearrange("p (k n) -> p k n", k=2), ACT.Copy, scale=0.125)
                        return act.activation(cv, ps[:, b:b + 2, 0:256], ACT.Copy)
                    chunks(4, evac, transfers=[(1, 5)])
                    leave()
                    next_slabs()
                    enter()
                    self.keep_bias(1)
                    leave()

                def latent(self):
                    enter()
                    for t in range(T):
                        act.activation(score_part[:, P * t:P * t + P], kvn[:, t, :], ACT.Square, accum_out=ss8[:, t:t + 1]).then_inc(summed, 1)
                    leave()

                def select(self, t):
                    enter()
                    leave()

                def dsa(self, t):
                    enter()
                    w = P * (t + 1)

                    def keep(u):
                        act.wait_ge(probs_turned, units.n + u + 1)
                        act.activation(PTd[:, u, 0:t + 1, :], ps[:, 2 + u % 2, 0:w].rearrange("p (m q) -> p m q", q=P), ACT.Copy)\
                           .then_inc(probs_kept, 1)

                    self.exps(0, ((0, w),), units.n)
                    for u in range(4):
                        if u + 1 < 4:
                            self.exps(u + 1, ((0, w),), units.n + u + 1)
                        keep(u)
                    act.wait_ge(pv_done, groups.n + 1)
                    act.activation(o_lat, ps[:, 4, :], ACT.Copy).then_inc(lat_kept, 1)
                    units.next(4)
                    groups.next(1)
                    act.wait_ge(branch_done, 2 + t)
                    act.activation(yT[:, 4:6, t * P:(t + 1) * P], ps[:, 5, 0:256].rearrange("p (k q) -> p k q", k=2), ACT.Copy)
                    leave()

                def moba(self):
                    enter()
                    self.keep_bias(2)
                    leave()
                    enter()

                    def exps(u):
                        self.exps(u, ((0, P * (u % 2 + 1)),), units.n + u)

                    def keep(u):
                        w = P * (u % 2 + 1)
                        act.wait_ge(probs_turned, units.n + u + 1)
                        if u >= 2:
                            act.wait_ge(pv_done, groups.n + u - 1)
                        act.activation(PTu[u % 2][:, 0:w], ps[:, 2 + u % 2, 0:w], ACT.Copy).then_inc(probs_kept, 1)

                    exps(0)
                    for u in range(8):
                        if u + 1 < 8:
                            exps(u + 1)
                        keep(u)
                    units.next(8)
                    groups.next(8)
                    act.wait_ge(pv_done, groups.n)
                    act.activation(yT[:, 6:8, :], ps[:, 4, :].rearrange("p (k q) -> p k q", k=2), ACT.Copy)
                    leave()

                def merge(self):
                    enter()
                    act.activation(aTf_hi, yTf, ACT.Copy).then_inc(aT_hi_made, 1)
                    split(2)
                    split(3)
                    for s in range(4):
                        done.next(s)
                    leave()
                    next_slabs()

                def mlp(self):
                    enter()
                    rounds = 8
                    ub, db, fb = list(uses.n), list(done.n), c_ffn.n
                    with act.Fori(0, rounds - 1) as i:
                        split(0, ub[0] + i + 1)
                        self.mlp_round(i, db, fb)
                        split(1, ub[1] + i + 1)
                        self.mlp_turned(i, fb)
                        split(2, ub[2] + i + 1)
                        split(3, ub[3] + i + 1)
                    for s in range(4):
                        uses.n[s] += rounds - 1
                        arrived[s] += 32 * (rounds - 1)
                    self.mlp_round(rounds - 1, db, fb)
                    self.mlp_turned(rounds - 1, fb)
                    split(2)
                    split(3)
                    for s in range(4):
                        done.n[s] += rounds
                    leave()

                def mlp_round(self, i, db, fb):
                    act.wait_ge(gate_half, fb + i + 1)
                    act.activation(hs[:, 0, :], ps[:, 4, :], ACT.Relu).then_inc(silu_made, 1)
                    act.wait_ge(consumed[1], db[1] + i + 1)
                    act.activation(hs[:, 1, :], ps[:, 5, :], ACT.Relu).then_inc(silu_made, 1)

                def mlp_turned(self, i, fb):
                    act.wait_ge(hid_turned, fb + i + 1)
                    act.activation(hT_hi[:, :, :], ps[:, 6:8, :], ACT.Copy).then_inc(hT_hi_made, 1)

                def end(self):
                    pass

            next_slabs()
            act.wait_ge(x_in, 32)
            program(Act())

        @block.vector
        def _(dve):
            stages, steps, uses, done = Count(), Count(), Uses(), Uses()
            c_norm, c_turned, c_ffn, c_turn = Count(), Count(), Count(), Count()
            units, groups, chunk_no = Count(), Count(), Count()

            def enter():
                if stages.n:
                    dve.wait_ge(stage_dve, stages.n)
                    dve.wait_ge(stage_act, stages.n)
                stages.next()

            def leave():
                dve.drain().then_inc(stage_dve, 1)

            def step(ins):
                ins.then_inc(dve_step, 1)
                dve.wait_ge(dve_step, steps.next())

            def split(slot, n=None, doubled=False):
                if n is None:
                    n = uses.next(slot)
                dve.wait_ge(hi_ready[slot], n)
                if doubled:
                    hi, of = twice(slot)
                    lo = wlo[:, slot, :].rearrange("p (g a n) -> p g a n", a=2, n=64)
                else:
                    hi, of, lo = whi[:, slot, :], raw[:, slot, :], wlo[:, slot, :]
                dve.tensor_tensor(lo, of, hi, ALU.subtract).then_inc(lo_ready[slot], 1)

            def chunks(count, evac, doubled=()):
                for c in range(count):
                    if c + 1 < count:
                        for s in range(2):
                            split(2 * ((c + 1) % 2) + s, doubled=c + 1 in doubled)
                    pair = 2 * (c % 2)
                    done.next(pair)
                    dve.wait_ge(consumed[pair + 1], done.next(pair + 1))
                    evac(c, 4 * (chunk_no.n % 2)).then_inc(dve_evac, 1)
                    chunk_no.next()

            def next_slabs():
                for s in range(2):
                    split(s)

            def lower(b, dst_hi, dst_lo, src):
                dve.wait_ge(aT_hi_made, c_turned.next())
                dve.tensor_tensor(dst_lo, src, dst_hi, ALU.subtract).then_inc(aT_made, 1)

            class Dve:
                def norm(self, m, mem=False, turn=True, keep=False, modulate=False):
                    enter()
                    dve.wait_ge(gain_in[m % 2], 16 * (m // 2 + 1))
                    dve.wait_ge(rstd_made, m + 1)
                    src = xn if mem else x
                    to = x if keep else xn
                    for t in range(T):
                        last = dve.scalar_tensor_tensor(out=to[:, t, :], in0=src[:, t, :], scalar=rstd[:, t:t + 1],
                                                        in1=gain[:, m % 2, :], op0=ALU.mult, op1=ALU.mult)
                        if modulate:
                            step(last)
                            step(dve.scalar_tensor_tensor(out=xn[:, t, :], in0=mod[:, 1024:2048], scalar=1.0,
                                                          in1=xn[:, t, :], op0=ALU.add, op1=ALU.mult))
                            last = dve.tensor_tensor(xn[:, t, :], xn[:, t, :], mod[:, 0:1024], ALU.add)
                        last.then_inc(rows_normed, 1)
                    if turn:
                        for b in range(4):
                            t, k = b // 2, 4 * (b % 2)
                            at = (slice(None), slice(k, k + 4), slice(t * P, (t + 1) * P))
                            lower(b, aT_hi[at], aT_lo[at], ps[:, b, :].rearrange("p (k n) -> p k n", k=4))
                    leave()

                def kv(self, l):
                    enter()

                    def evac(c, b):
                        if c < 2:
                            return dve.tensor_copy(kT[:, 4 * c + 2:4 * c + 4, :], ps[:, b + 1, :])
                        return dve.tensor_copy(vm[:, 1, 512 * (c - 2):512 * (c - 1)], ps[:, b + 1, :])
                    chunks(4, evac)
                    leave()
                    next_slabs()

                def ffn(self, w_in, w_out):
                    enter()
                    rounds = FF // HI
                    ub, db, fb = list(uses.n), list(done.n), c_ffn.n

                    def first_half(i):
                        for t in range(T):
                            dve.wait_ge(silu_made, 2 * (fb + i) + t + 1)
                            dve.tensor_tensor(hs[:, t, HI:2 * HI], hs[:, t, 0:HI], ps[:, 4 + t, HI:2 * HI], ALU.mult)\
                               .then_inc(hid_made, 1)

                    def second_half(i):
                        dve.wait_ge(hT_hi_made, fb + i + 1)
                        dve.tensor_tensor(hT_lo[:, 0:2, :], ps[:, 6, :].rearrange("p (k n) -> p k n", k=2),
                                          hT_hi[:, 0:2, :], ALU.subtract).then_inc(hT_made, 1)

                    with dve.Fori(0, rounds) as i:
                        split(0, ub[0] + i + 1)
                        first_half(i)
                        split(1, ub[1] + i + 1)
                        second_half(i)
                        split(2, ub[2] + i + 1)
                    for s in range(3):
                        uses.n[s] += rounds
                        done.n[s] += rounds
                    c_ffn.next(rounds)
                    dve.wait_ge(consumed[2], done.n[2])
                    for b in range(4):
                        t, c = b // 2, b % 2
                        at = x[:, t, 512 * c:512 * c + 512]
                        dve.scalar_tensor_tensor(out=at, in0=ps[:, b, :], scalar=0.5, in1=at,
                                                 op0=ALU.mult, op1=ALU.add)
                    leave()

                def pool(self):
                    enter()
                    split(2)
                    for b in range(4):
                        at = (slice(None), slice(2 * b, 2 * b + 2), slice(None))
                        lower(b, aT_hi[at], aT_lo[at], ps[:, b, :].rearrange("p (k n) -> p k n", k=2))
                    dve.wait_ge(consumed[2], done.next(2))
                    dve.wait_ge(mix_in, 48)
                    for b in range(4):
                        t, c = b // 2, slice(512 * (b % 2), 512 * (b % 2) + 512)
                        step(dve.tensor_tensor(xn[:, t, c], ps[:, 4 + b, :], pool_b[:, c], ALU.add))
                        step(dve.tensor_tensor(xn[:, t, c], xn[:, t, c], pool_s[:, c], ALU.mult))
                        dve.tensor_tensor(x[:, t, c], x[:, t, c], xn[:, t, c], ALU.add)
                    leave()

                def query(self, l):
                    enter()
                    chunks(2, lambda c, b: dve.tensor_scalar(qT[:, 4 * c + 2:4 * c + 4, :],
                                                             ps[:, b + 1, :].rearrange("p (k n) -> p k n", k=2), 1.0 / 16, None, ALU.mult))
                    leave()
                    next_slabs()

                def cross(self):
                    enter()

                    def top(u):
                        U = units.n + u
                        dve.wait_ge(scored, U + 1)
                        if u >= 2:
                            dve.wait_ge(exped, U - 1)
                        dve.tensor_reduce(nmx[:, 3 * (u % 2):3 * (u % 2) + 1], ps[:, u % 2, 0:S], AX.X, ALU.max, negate=True)\
                           .then_inc(maxed, 1)

                    def weigh(u):
                        b = 3 * (u % 2)
                        dve.wait_ge(exped, units.n + u + 1)
                        step(dve.reciprocal(rec[:, b:b + 1], den[:, b:b + 1]))
                        dve.tensor_scalar(Pb[u % 2][:, 0:S], Pb[u % 2][:, 0:S], rec[:, b:b + 1], None, ALU.mult)\
                           .then_inc(weighed, 1)

                    def out_lo(h):
                        dve.wait_ge(o_hi, groups.n + h + 1)
                        dve.tensor_tensor(aT_lo[:, 2 * h:2 * h + 2, :], ps[:, 4 + h % 2, :].rearrange("p (k n) -> p k n", k=2),
                                          aT_hi[:, 2 * h:2 * h + 2, :], ALU.subtract).then_inc(o_kept, 1)

                    top(0)
                    for u in range(8):
                        if u + 1 < 8:
                            top(u + 1)
                        weigh(u)
                        if u % 2 == 0 and u:
                            out_lo(u // 2 - 1)
                    out_lo(3)
                    units.next(8)
                    groups.next(4)
                    leave()

                def project(self, w, gated=False):
                    enter()
                    if gated:
                        for b in range(4):
                            t, k = b // 2, 4 * (b % 2)
                            at = (slice(None), slice(k, k + 4), slice(t * P, (t + 1) * P))
                            lower(b, aT_hi[at], aT_lo[at], ps[:, b, :].rearrange("p (k n) -> p k n", k=4))

                    def evac(c, b):
                        for t in range(T):
                            at = x[:, t, 512 * c:512 * c + 512]
                            if gated:
                                y = hs[:, t, :]
                                step(dve.tensor_tensor(y, ps[:, b + t, :], out_gate[:, 512 * c:512 * c + 512], ALU.mult))
                                last = dve.tensor_tensor(at, at, y, ALU.add)
                                if t == 0:
                                    step(last)
                                continue
                            last = dve.tensor_tensor(at, at, ps[:, b + t, :], ALU.add)
                        return last
                    chunks(2, evac)
                    leave()
                    next_slabs()

                def nsa_inputs(self):
                    enter()

                    def evac(c, b):
                        if c < 2:
                            return dve.tensor_scalar(qT[:, 4 * c + 2:4 * c + 4, :],
                                                     ps[:, b + 1, :].rearrange("p (k n) -> p k n", k=2), 0.125, None, ALU.mult)
                        if c in (2, 3):
                            v = c - 2
                            if c == 2:
                                step(dve.tensor_copy(posT, ps[:, b + 2, 0:32]))
                            for g in range(4):
                                for a in range(2):
                                    half = slice(64 * a, 64 * a + 64)
                                    src = ps[half, b + g // 2, 256 * (g % 2) + a:256 * (g % 2) + a + 255]
                                    win = bass.AP(src.tensor, src.offset, [list(src.ap[0]), [2, 16], [16, N_CMP]])
                                    last = dve.tensor_tensor(blk[half, v, :, g, :], win,
                                                             posT[half, 16 * v:16 * v + 16].unsqueeze(2)
                                                             .to_broadcast([64, 16, N_CMP]), ALU.add)
                            return last
                        if c in (4, 5):
                            return dve.tensor_copy((ksT, kwT)[c - 4][:, 2:4, :], ps[:, b + 1, :])
                        if c == 6:
                            return dve.tensor_copy(area[:, 8192:9216].rearrange("p (v t n) -> p t v n", v=2, t=2)[:, 1],
                                                   ps[:, b + 1, :].rearrange("p (v n) -> p v n", v=2))
                        return dve.drain()
                    chunks(8, evac, range(2, 6))
                    leave()
                    next_slabs()

                def nsa_compress(self):
                    enter()
                    dve.tensor_scalar(gates[:, 0, 0:48:3], gates[:, 0, 0:48:3], cst[:, C_VIS:C_VIS + 1], None, ALU.mult)
                    dve.wait_ge(aT_hi_made, c_turned.next())
                    dve.tensor_tensor(aTf_lo[:, 0:1920], area[:, 9344:11264], aTf_hi[:, 0:1920], ALU.subtract)\
                       .then_inc(aT_made, 1)
                    split(2)
                    split(3)
                    for v in range(2):
                        done.next(2 * v)
                        done.next(2 * v + 1)
                    leave()
                    next_slabs()

                def nsa_attend(self):
                    enter()

                    def top(u):
                        U, t, b = units.n + u, u // 4 % 2, 3 * (u % 2)
                        w = P * (t + 1)
                        dve.wait_ge(scored, U + 1)
                        if u >= 2:
                            dve.wait_ge(probs_turned, U - 1)
                        causal = cst[:, C_CAUSAL + S - w:C_CAUSAL + S]
                        for j, (c, n, src, mask) in enumerate((
                                (512, N_CMP, ps[:, 6 + u % 2, 0:N_CMP], cst[:, C_CMP + 16 * t:C_CMP + 16 * t + N_CMP]),
                                (0, w, ps[:, u % 2, 0:w], causal), (w, w, ps[:, u % 2, w:2 * w], causal))):
                            last = dve.tensor_tensor_reduce(Pb[u % 2][:, c:c + n], src, mask, -1.0, BIG, ALU.add, ALU.min,
                                                            nmx[:, b + j:b + j + 1])
                        last.then_inc(maxed, 1)

                    def weigh(u):
                        t, b = u // 4 % 2, 3 * (u % 2)
                        w, h = P * (t + 1), 4 * (u // 8) + u % 4
                        dve.wait_ge(exped, units.n + u + 1)
                        step(dve.reciprocal(rec[:, b:b + 3], den[:, b:b + 3]))
                        step(dve.tensor_tensor(rec[:, b:b + 3], rec[:, b:b + 3], gates[:, t, 3 * h:3 * h + 3], ALU.mult))
                        for j, (c, n) in enumerate(((512, N_CMP), (0, w), (w, w))):
                            last = dve.tensor_scalar(Pb[u % 2][:, c:c + n], Pb[u % 2][:, c:c + n], rec[:, b + j:b + j + 1],
                                                     None, ALU.mult)
                        last.then_inc(weighed, 1)

                    def out_lo(gi):
                        g, t = gi // 2, gi % 2
                        dve.wait_ge(o_hi, groups.n + gi + 1)
                        at = (slice(None), slice(2 * g, 2 * g + 2), slice(t * P, (t + 1) * P))
                        dve.tensor_tensor(aT_lo[at], ps[:, 4 + gi % 2, 0:256].rearrange("p (j q) -> p j q", j=2),
                                          aT_hi[at], ALU.subtract).then_inc(o_kept, 1)

                    top(0)
                    for u in range(32):
                        if u + 1 < 32:
                            top(u + 1)
                        weigh(u)
                        if u % 4 == 0 and u:
                            out_lo(u // 4 - 1)
                    out_lo(7)
                    units.next(32)
                    groups.next(8)
                    leave()

                def cond(self, part):
                    enter()
                    dve.wait_ge(cond_made, 3 * part + 2)
                    dve.tensor_tensor(aT_lo[:, :, 0:P], condT.unsqueeze(2).to_broadcast([P, KD, P]), aT_hi[:, :, 0:P],
                                      ALU.subtract).then_inc(cond_made, 1)
                    if part == 0:
                        dve.wait_ge(hot_in, 48)
                        for j in range(2):
                            dve.tensor_tensor_reduce(lam_prod[:, 64 * j:64 * j + 64], lam_in[:, P * j:P * j + 64],
                                                     lam_in[:, P * j + 64:P * j + P], 1.0, 0.0, ALU.mult, ALU.add,
                                                     lam2[:, j:j + 1]).then_inc(lam_summed, 1)
                        dve.wait_ge(dist_made, 3)
                        step(dve.tensor_tensor(neg_lam, lam2[:, 1:2], lam2[:, 0:1], ALU.subtract))
                        step(dve.tensor_scalar(neg_lam, neg_lam, -LAM_INIT, None, ALU.add))
                    leave()

                def ada(self, part):
                    enter()
                    dve.wait_ge(ada_in, 16 * (part + 1))

                    def evac(c, b):
                        at = mod[:, 512 * c:512 * c + 512]
                        return dve.tensor_tensor(at, at, ps[:, b, :], ALU.add)
                    chunks(6, evac)
                    leave()
                    next_slabs()

                def gate_inputs(self):
                    enter()
                    dve.wait_ge(gate_b_in, 32)

                    def evac(c, b):
                        at = bgate[:, :, 512 * c:512 * c + 512]
                        return dve.tensor_tensor(at, at, ps[:, b:b + 2, :], ALU.add)
                    chunks(6, evac)
                    leave()
                    next_slabs()

                def keep_bias(self, b):
                    dve.wait_ge(bias_turned, b + 1)
                    dve.tensor_copy(bias[:, 2:4, :], ps[:, 5, :].rearrange("p (h k) -> p h k", h=2))

                def diff_inputs(self):
                    enter()

                    def evac(c, b):
                        if c == 0:
                            return dve.tensor_scalar(aqT[:, 2:4, :], ps[:, b + 1, :].rearrange("p (k n) -> p k n", k=2), 0.125, None, ALU.mult)
                        if c == 1:
                            return dve.tensor_copy(akT[:, 2:4, :], ps[:, b + 1, :])
                        return dve.tensor_copy(av[:, 1, :], ps[:, b + 1, :])
                    chunks(3, evac)
                    leave()
                    next_slabs()
                    enter()
                    self.keep_bias(0)
                    dve.wait_ge(row_in, 16)
                    dve.tensor_scalar(subln, subln, 1.0 - LAM_INIT, None, ALU.mult)
                    leave()

                def diff(self):
                    enter()

                    def top(u):
                        U, h, t, b = units.n + u, u // 2, u % 2, 3 * (u % 2)
                        w = P * (t + 1)
                        dve.wait_ge(scored, U + 1)
                        if u >= 2:
                            dve.wait_ge(probs_turned, U - 1)
                        for j in range(2):
                            last = dve.tensor_tensor_reduce(Pb[u % 2][:, w * j:w * j + w], ps[:, 2 * (u % 2) + j, 0:w],
                                                            bias[:, h, S - w:S], -1.0, BIG, ALU.add, ALU.min,
                                                            nmx[:, b + j:b + j + 1])
                        last.then_inc(maxed, 1)

                    def weigh(u):
                        b, w = 3 * (u % 2), P * (u % 2 + 1)
                        p0, p1 = Pb[u % 2][:, 0:w], Pb[u % 2][:, w:2 * w]
                        dve.wait_ge(exped, units.n + u + 1)
                        step(dve.reciprocal(rec[:, b:b + 2], den[:, b:b + 2]))
                        step(dve.tensor_tensor(rec[:, b + 1:b + 2], rec[:, b + 1:b + 2], neg_lam, ALU.mult))
                        step(dve.tensor_scalar(p1, p1, rec[:, b + 1:b + 2], None, ALU.mult))
                        dve.scalar_tensor_tensor(out=p0, in0=p0, scalar=rec[:, b:b + 1], in1=p1, op0=ALU.mult, op1=ALU.add)\
                           .then_inc(weighed, 1)

                    top(0)
                    for u in range(8):
                        if u + 1 < 8:
                            top(u + 1)
                        weigh(u)
                    units.next(8)
                    groups.next(8)
                    leave()

                def diff_norm(self):
                    enter()
                    sq = xnf[:, 0:1024]
                    step(dve.tensor_tensor(sq, hsf, hsf, ALU.mult))
                    dve.tensor_reduce(ss8, sq.rearrange("p (u e) -> p u e", u=8), AX.X, ALU.add).then_inc(summed, 1)
                    dve.wait_ge(powered, 1)
                    o8 = hsf.rearrange("p (u e) -> p u e", u=8)
                    step(dve.tensor_tensor(o8, o8, rstd8.unsqueeze(2).to_broadcast([P, 8, P]), ALU.mult))
                    dve.tensor_tensor(o8, o8, subln.unsqueeze(1).to_broadcast([P, 8, P]), ALU.mult).then_inc(branch_kept, 1)
                    dve.wait_ge(branch_done, 1)
                    dve.tensor_copy(yT[:, 2:4, :], ps[:, 1, :].rearrange("p (k n) -> p k n", k=2))
                    leave()

                def sparse_inputs(self):
                    enter()

                    def evac(c, b):
                        if c == 0:
                            return dve.tensor_scalar(bqT[:, 2:4, :], ps[:, b + 1, :].rearrange("p (k n) -> p k n", k=2), P ** -0.5, None, ALU.mult)
                        if c == 1:
                            return dve.tensor_copy(ikT, ps[:, b + 2, 0:256])
                        if c == 2:
                            return dve.tensor_copy(ckT, ps[:, b + 1, :].rearrange("p (k n) -> p k n", k=2))
                        dve.wait_ge(act_evac, chunk_no.n + 1)
                        return dve.tensor_scalar(iw, ps[:, b:b + 2, 256:264], 0.0625, None, ALU.mult)
                    chunks(4, evac)
                    leave()
                    next_slabs()
                    enter()
                    self.keep_bias(1)
                    leave()

                def latent(self):
                    enter()
                    dve.wait_ge(row_in, 48)
                    dve.wait_ge(powered, 2)
                    for t in range(T):
                        last = dve.scalar_tensor_tensor(out=kvn[:, t, :], in0=kvn[:, t, :], scalar=rstd8[:, t:t + 1],
                                                        in1=kv_gain, op0=ALU.mult, op1=ALU.mult)
                    last.then_inc(branch_kept, 1)
                    dve.wait_ge(branch_kept, 3)
                    dve.tensor_copy(kvT, ps[:, 0, 0:S])
                    leave()

                def select(self, t):
                    enter()
                    w = P * (t + 1)
                    wk, part = work[:, 0:w], score_part[:, 0:w]
                    dve.wait_ge(index_scored, t + 1)
                    for h in range(8):
                        src = ps[:, h % 4, w * (h // 4):w * (h // 4) + w]
                        step(dve.tensor_scalar(part if h else wk, src, 0.0, iw[:, t, h:h + 1], ALU.max, ALU.mult))
                        if h:
                            step(dve.tensor_tensor(wk, wk, part, ALU.add))
                    step(dve.tensor_tensor(wk, wk, cst[:, C_CAUSAL + S - w:C_CAUSAL + S], ALU.add))
                    for _ in range(TOPK // 8):
                        step(dve.max(top8, wk))
                        step(dve.match_replace(wk, top8, wk, -BIG))
                    dve.tensor_scalar(sel[:, 0:w], wk, -2.0e38, NEG, ALU.is_gt, ALU.mult)
                    leave()

                def dsa(self, t):
                    enter()
                    w = P * (t + 1)

                    def top(u):
                        U, b = units.n + u, 3 * (u % 2)
                        pb = Pb[u % 2][:, 0:w]
                        if u >= 2:
                            dve.wait_ge(probs_turned, U - 1)
                        step(dve.tensor_tensor(pb, bias[:, u, S - w:S], sel[:, 0:w], ALU.add))
                        dve.wait_ge(scored, U + 1)
                        dve.tensor_tensor_reduce(pb, ps[:, u % 2, 0:w], pb, -1.0, BIG, ALU.add, ALU.min,
                                                 nmx[:, b:b + 1]).then_inc(maxed, 1)

                    top(0)
                    for u in range(4):
                        if u + 1 < 4:
                            top(u + 1)
                        self.weigh_one(u, w)
                    units.next(4)
                    groups.next(1)
                    leave()

                def weigh_one(self, u, w):
                    b = 3 * (u % 2)
                    dve.wait_ge(exped, units.n + u + 1)
                    step(dve.reciprocal(rec[:, b:b + 1], den[:, b:b + 1]))
                    dve.tensor_scalar(Pb[u % 2][:, 0:w], Pb[u % 2][:, 0:w], rec[:, b:b + 1], None, ALU.mult)\
                       .then_inc(weighed, 1)

                def moba(self):
                    enter()
                    self.keep_bias(2)
                    leave()
                    enter()

                    def top(u):
                        U, h, b, w = units.n + u, u // 2, 3 * (u % 2), P * (u % 2 + 1)
                        dve.wait_ge(scored, U + 1)
                        if u >= 2:
                            dve.wait_ge(probs_turned, U - 1)
                        dve.tensor_tensor_reduce(Pb[u % 2][:, 0:w], ps[:, u % 2, 0:w], bias[:, h, S - w:S], -1.0, BIG,
                                                 ALU.add, ALU.min, nmx[:, b:b + 1]).then_inc(maxed, 1)

                    top(0)
                    for u in range(8):
                        if u + 1 < 8:
                            top(u + 1)
                        self.weigh_one(u, P * (u % 2 + 1))
                    units.next(8)
                    groups.next(8)
                    leave()

                def merge(self):
                    enter()
                    dve.wait_ge(aT_hi_made, c_turned.next())
                    dve.tensor_tensor(aTf_lo, yTf, aTf_hi, ALU.subtract).then_inc(aT_made, 1)
                    split(2)
                    split(3)
                    for s in range(4):
                        done.next(s)
                    for br in range(3):
                        dve.wait_ge(branch_done, 4 + br)
                        for t in range(T):
                            g = bgate[:, t, 1024 * br:1024 * br + 1024].rearrange("p (c n) -> p c n", c=2)
                            y = ps[:, 4 * (br % 2) + 2 * t:4 * (br % 2) + 2 * t + 2, :]
                            m = xn[:, t, :].rearrange("p (c n) -> p c n", c=2)
                            if br == 0:
                                last = dve.tensor_tensor(m, y, g, ALU.mult)
                                continue
                            last = dve.tensor_tensor(g, y, g, ALU.mult)
                        last.then_inc(branch_kept, 1)
                        if br:
                            dve.wait_ge(branch_kept, 3 + br + 1)
                            for t in range(T):
                                g = bgate[:, t, 1024 * br:1024 * br + 1024]
                                last = dve.tensor_tensor(xn[:, t, :], xn[:, t, :], g, ALU.add)
                            if br == 1:
                                step(last)
                    leave()
                    next_slabs()

                def mlp(self):
                    enter()
                    rounds = 8
                    ub, db, fb = list(uses.n), list(done.n), c_ffn.n
                    with dve.Fori(0, rounds - 1) as i:
                        split(0, ub[0] + i + 1)
                        self.mlp_round(i, fb)
                        split(1, ub[1] + i + 1)
                        self.mlp_turned(i, fb)
                        split(2, ub[2] + i + 1)
                        split(3, ub[3] + i + 1)
                    for s in range(4):
                        uses.n[s] += rounds - 1
                    self.mlp_round(rounds - 1, fb)
                    self.mlp_turned(rounds - 1, fb)
                    split(2)
                    split(3)
                    for s in range(4):
                        done.n[s] += rounds
                    dve.wait_ge(consumed[3], done.n[3])
                    for t in range(T):
                        y = xn[:, t, :]
                        step(dve.tensor_tensor(y.rearrange("p (c n) -> p c n", c=2), ps[:, 2 * t:2 * t + 2, :],
                                               out_gate.rearrange("p (c n) -> p c n", c=2), ALU.mult))
                        dve.tensor_tensor(x[:, t, :], x[:, t, :], y, ALU.add)
                    leave()

                def mlp_round(self, i, fb):
                    for t in range(T):
                        dve.wait_ge(silu_made, 2 * (fb + i) + t + 1)
                        dve.tensor_tensor(hs[:, t, :], hs[:, t, :], ps[:, 4 + t, :], ALU.mult).then_inc(hid_made, 1)

                def mlp_turned(self, i, fb):
                    dve.wait_ge(hT_hi_made, fb + i + 1)
                    dve.tensor_tensor(hT_lo[:, :, :], ps[:, 6:8, :].rearrange("p b (k n) -> p (b k) n", k=2), hT_hi[:, :, :],
                                      ALU.subtract).then_inc(hT_made, 1)

                def end(self):
                    pass

            next_slabs()
            program(Dve())

        @block.tensor
        def _(pe):
            stages, uses = Count(), Uses()
            c_norm, c_turned, c_ffn = Count(), Count(), Count()
            units, groups, chunk_no = Count(), Count(), Count()

            def enter():
                if stages.n:
                    pe.wait_ge(stage_act, stages.n)
                    pe.wait_ge(stage_dve, stages.n)
                stages.next()

            def parts(o, lh, ll, rh, rl, start, stop):
                pe.matmul(o, lh, rl, start=start, stop=False, skip_group_check=True)
                pe.matmul(o, ll, rh, start=False, stop=False, skip_group_check=True)
                return pe.matmul(o, lh, rh, start=False, stop=stop, skip_group_check=True)

            def chunk(pair, n, outs):
                before = chunk_no.next() - 2
                if before >= 0:
                    pe.wait_ge(act_evac, before)
                    pe.wait_ge(dve_evac, before)
                wh = [whi[:, pair + s, 0:4 * n].rearrange("p (k n) -> p k n", k=4) for s in range(2)]
                wl = [wlo[:, pair + s, 0:4 * n].rearrange("p (k n) -> p k n", k=4) for s in range(2)]
                for s in range(2):
                    pe.wait_ge(lo_ready[pair + s], uses.next(pair + s))
                for j, (kind, *a, o) in enumerate(outs):
                    for k in range(KD):
                        s, r = k // 4, k % 4
                        if kind == "N":
                            t, c, m = a
                            tok = slice(t * P, (t + 1) * P)
                            last = parts(o, aT_hi[:, k, tok], aT_lo[:, k, tok], wh[s][:, r, c:c + m],
                                         wl[s][:, r, c:c + m], k == 0, k == KD - 1)
                        else:
                            c, m = a
                            last = parts(o, wh[s][:, r, c:c + m], wl[s][:, r, c:c + m], aT_hi[:, k, :],
                                         aT_lo[:, k, :], k == 0, k == KD - 1)
                        if j == len(outs) - 1 and r == 3:
                            last.then_inc(consumed[pair + s], 1)

            def rows(b):
                return [("N", t, 0, 512, ps[:, b + t, :]) for t in range(T)]

            def turned(b):
                return [("T", 128 * j, 128, ps[:, b + j // 2, 256 * (j % 2):256 * (j % 2) + 256]) for j in range(4)]

            def bank():
                return 4 * (chunk_no.n % 2)

            def turn_rows():
                for b in range(4):
                    t = b // 2
                    for k in range(4):
                        f = 4 * (b % 2) + k
                        last = pe.transpose(ps[:, b, P * k:P * k + P], xn[:, t, P * f:P * f + P], ident)
                    last.then_inc(rows_turned, 1)

            class Pe:
                def norm(self, m, mem=False, turn=True, keep=False, modulate=False):
                    enter()
                    if turn:
                        pe.wait_ge(rows_normed, 2 * m + 2)
                        turn_rows()
                        pe.wait_ge(aT_made, c_turned.next(4))

                def kv(self, l):
                    enter()
                    for c in range(4):
                        chunk(2 * (c % 2), 512, turned(bank()) if c < 2 else rows(bank()))

                def ffn(self, w_in, w_out):
                    enter()
                    rounds = FF // HI
                    ub, fb = list(uses.n), c_ffn.n
                    for b in range(4):
                        pe.matmul(ps[:, b, :], zero[:, 0:P], zero[:, :], start=True, stop=False, skip_group_check=True)

                    def up(i):
                        for s in range(2):
                            pe.wait_ge(lo_ready[s], ub[s] + i + 1)
                            h, lw = (w[:, s, :].rearrange("p (k n) -> p k n", k=4) for w in (whi, wlo))
                            for t in range(T):
                                tok = slice(t * P, (t + 1) * P)
                                for r in range(4):
                                    k = 4 * s + r
                                    last = parts(ps[:, 4 + t, :], aT_hi[:, k, tok], aT_lo[:, k, tok], h[:, r, :],
                                                 lw[:, r, :], k == 0, k == KD - 1)
                                if s == 1 and t == 0:
                                    last.then_inc(gate_half, 1)
                            last.then_inc(consumed[s], 1)

                    def turn(i):
                        for t in range(T):
                            pe.wait_ge(hid_made, 2 * (fb + i) + t + 1)
                            for k in range(2):
                                last = pe.transpose(ps[:, 6, S * k + P * t:S * k + P * t + P],
                                                    hs[:, t, HI + P * k:HI + P * k + P], ident)
                        last.then_inc(hid_turned, 1)

                    def down(i, stop):
                        pe.wait_ge(lo_ready[2], ub[2] + i + 1)
                        pe.wait_ge(hT_made, fb + i + 1)
                        h, lw = (w[:, 2, :].rearrange("p (k c n) -> p k c n", k=2, c=2) for w in (whi, wlo))
                        for t in range(T):
                            tok = slice(t * P, (t + 1) * P)
                            for c in range(2):
                                for k in range(2):
                                    last = parts(ps[:, 2 * t + c, :], hT_hi[:, k, tok], hT_lo[:, k, tok],
                                                 h[:, k, c, :], lw[:, k, c, :], False, stop and k == 1)
                        last.then_inc(consumed[2], 1)

                    up(0)
                    turn(0)
                    with pe.Fori(1, rounds) as i:
                        up(i)
                        down(i - 1, False)
                        turn(i)
                    down(rounds - 1, True)
                    for s in range(3):
                        uses.n[s] += rounds
                    c_ffn.next(rounds)

                def pool(self):
                    enter()
                    pe.wait_ge(mix_in, 48)
                    for b in range(4):
                        for j in range(2):
                            k = 2 * b + j
                            o = ps[:, b, S * j:S * j + S]
                            pe.matmul(o, xn[:, 0, P * k:P * k + P], band[:, k // 2, 0:S], start=True, stop=False)
                            last = pe.matmul(o[:, P:S], xn[:, 1, P * k:P * k + P], band[:, k // 2, S:S + P],
                                             start=False, stop=True)
                        last.then_inc(rows_turned, 1)
                    pe.wait_ge(aT_made, c_turned.next(4))
                    pe.wait_ge(lo_ready[2], uses.next(2))
                    h, lw = (w[:, 2, :].rearrange("p (k n) -> p k n", n=256) for w in (whi, wlo))
                    for t in range(T):
                        tok = slice(t * P, (t + 1) * P)
                        for g in range(4):
                            o = ps[:, 4 + 2 * t + g // 2, 256 * (g % 2):256 * (g % 2) + 256]
                            for k in range(2 * g, 2 * g + 2):
                                last = parts(o, aT_hi[:, k, tok], aT_lo[:, k, tok], h[:, k, :], lw[:, k, :],
                                             k % 2 == 0, k % 2 == 1)
                    last.then_inc(consumed[2], 1)

                def query(self, l):
                    enter()
                    for c in range(2):
                        chunk(2 * c, 512, turned(bank()))

                def cross(self):
                    enter()

                    def score(u):
                        h, t = u // 2, u % 2
                        if u >= 2:
                            pe.wait_ge(exped, units.n + u - 1)
                        for j in range(2):
                            last = pe.matmul(ps[:, u % 2, 0:S], qT[:, 2 * h + j, t * P:(t + 1) * P], kT[:, 2 * h + j, :],
                                             start=j == 0, stop=j == 1)
                        last.then_inc(scored, 1)

                    def turn(u):
                        U = units.n + u
                        pe.wait_ge(weighed, U + 1)
                        if u >= 2:
                            pe.wait_ge(probs_kept, U - 1)
                        for m in range(2):
                            last = pe.transpose(ps[:, 2 + u % 2, P * m:P * m + P], Pb[u % 2][:, P * m:P * m + P], ident)
                        last.then_inc(probs_turned, 1)

                    def values(h):
                        pe.wait_ge(probs_kept, units.n + 2 * h + 2)
                        if h >= 2:
                            pe.wait_ge(o_kept, groups.n + h - 1)
                        for j in range(2):
                            for m in range(2):
                                last = pe.matmul(ps[:, 4 + h % 2, S * j:S * j + S],
                                                 vm[:, m, 256 * h + P * j:256 * h + P * j + P], PTc(h)[:, m, :],
                                                 start=m == 0, stop=m == 1)
                        last.then_inc(pv_done, 1)

                    score(0)
                    for u in range(8):
                        if u + 1 < 8:
                            score(u + 1)
                        turn(u)
                        if u % 2 == 0 and u:
                            values(u // 2 - 1)
                    values(3)
                    units.next(8)
                    groups.next(4)

                def project(self, w, gated=False):
                    enter()
                    if gated:
                        turn_rows()
                        pe.wait_ge(aT_made, c_turned.next(4))
                    for c in range(2):
                        chunk(2 * c, 512, rows(bank()))

                def nsa_inputs(self):
                    enter()

                    for c in range(6):
                        b = bank()
                        if c == 2:
                            pe.wait_ge(pos_in, 16)
                            pe.wait_ge(dve_evac, chunk_no.n - 1)
                            pe.transpose(ps[:, b + 2, 0:32], pos_rows, ident[0:32, 0:32])
                        chunk(2 * (c % 2), 512, turned(b))
                    chunk(0, 512, rows(bank()))
                    b = bank()
                    chunk(2, 48, [("N", t, 0, 48, ps[:, b, 48 * t:48 * t + 48]) for t in range(T)])

                def nsa_compress(self):
                    enter()
                    pe.wait_ge(aT_made, c_turned.next())
                    for v in range(2):
                        for s in range(2):
                            pe.wait_ge(lo_ready[2 * v + s], uses.next(2 * v + s))
                        for h in range(2):
                            for j in range(16):
                                s = 2 * v + j // 8
                                c = 256 * (j % 8) + P * h
                                r = slice(960 * v + 60 * j, 960 * v + 60 * j + 60)
                                last = parts(ps[:, v, 64 * h:64 * h + 60], whi[:, s, c:c + P], wlo[:, s, c:c + P],
                                             aTf_hi[:, r], aTf_lo[:, r], j == 0, j == 15)
                                if h == 1 and j % 8 == 7:
                                    last.then_inc(consumed[s], 1)
                    pe.wait_ge(w2_in, 48)
                    pe.wait_ge(gelu_made, 1)
                    for h in range(2):
                        last = pe.matmul(ps[:, 2, 0:60], w2k[:, h, :], hidT[:, 0, h, :], start=h == 0, stop=h == 1)
                    last.then_inc(cmp_made, 1)
                    pe.wait_ge(gelu_made, 2)
                    for g in range(4):
                        for h in range(2):
                            last = pe.matmul(ps[0:N_CMP, 3, 64 * g:64 * g + 64], hidT[:, 1, h, N_CMP * g:N_CMP * g + N_CMP],
                                             w2v[:, h, :], start=h == 0, stop=h == 1)
                    last.then_inc(cmp_made, 1)

                def nsa_attend(self):
                    enter()

                    def score(u):
                        g, t, r = u // 8, u // 4 % 2, u % 4
                        half, w = slice(64 * (r % 2), 64 * (r % 2) + 64), P * (t + 1)
                        if u >= 2:
                            pe.wait_ge(maxed, units.n + u - 1)
                            pe.wait_ge(probs_kept, units.n + u - 1)
                        q = qT[half, 2 * g + r // 2, t * P:(t + 1) * P]
                        pe.matmul(ps[:, 6 + u % 2, 0:N_CMP], q, kcT[half, N_CMP * g:N_CMP * g + N_CMP],
                                  start=True, stop=True)
                        pe.matmul(ps[:, u % 2, 0:w], q, ksT[half, g, 0:w], start=True, stop=True)
                        pe.matmul(ps[:, u % 2, w:2 * w], q, kwT[half, g, 0:w], start=True, stop=True).then_inc(scored, 1)

                    def turn(u):
                        U, t = units.n + u, u // 4 % 2
                        pe.wait_ge(weighed, U + 1)
                        if u >= 2:
                            pe.wait_ge(probs_kept, U - 1)
                        pe.transpose(ps[0:N_CMP, 6 + u % 2, P:2 * P], Pb[u % 2][:, 512:512 + N_CMP], ident)
                        for m in range(2 * (t + 1)):
                            last = pe.transpose(ps[:, 2 + u % 2, P * m:P * m + P], Pb[u % 2][:, P * m:P * m + P], ident)
                        last.then_inc(probs_turned, 1)

                    def values(gi):
                        g, t = gi // 2, gi % 2
                        pe.wait_ge(probs_kept, units.n + 4 * gi + 4)
                        if gi >= 2:
                            pe.wait_ge(o_kept, groups.n + gi - 1)
                        for par in range(2):
                            o = ps[64 * par:64 * par + 64, 4 + gi % 2, 0:256]
                            pe.matmul(o, vcmp[:, 64 * g:64 * g + 64], nsaPc[gi % 2][0:N_CMP, par::2, :], start=True, stop=False)
                            for j, v in enumerate((vs, vw)):
                                for m in range(t + 1):
                                    c = P * (j * (t + 1) + m)
                                    last = pe.matmul(o, v[:, m, 64 * g:64 * g + 64], nsaP[gi % 2][:, par::2, c:c + P],
                                                     start=False, stop=j == 1 and m == t)
                        last.then_inc(pv_done, 1)

                    score(0)
                    for u in range(32):
                        if u + 1 < 32:
                            score(u + 1)
                        turn(u)
                        if u % 4 == 0 and u:
                            values(u // 4 - 1)
                    values(7)
                    units.next(32)
                    groups.next(8)

                def cond(self, part):
                    enter()
                    pe.wait_ge(cond_in, 16 * (part + 1))
                    pe.transpose(ps[:, 0, 0:8], cond_rows, ident[0:8, 0:8]).then_inc(cond_turned, 1)
                    if part == 0:
                        pe.wait_ge(hot_in, 48)
                        pe.wait_ge(mask_row, 1)
                        pe.matmul(ps[0:12, 1, 0:384], rel, hot, start=True, stop=True).then_inc(dist_made, 1)

                def ada(self, part):
                    enter()
                    pe.wait_ge(cond_made, 3 * part + 3)
                    for c in range(6):
                        chunk(2 * (c % 2), 512, [("N", 0, 0, 512, ps[:, bank(), :])])

                def gate_inputs(self):
                    enter()
                    for c in range(6):
                        chunk(2 * (c % 2), 512, rows(bank()))

                def turn_bias(self, b):
                    enter()
                    pe.wait_ge(skew_in, 16 * (b + 1))
                    for j in range(2):
                        last = pe.matmul(ps[:, 4 + j, :], cst[:, C_FLIP:C_FLIP + P], skew[:, 2 * j:2 * j + 2, :],
                                         start=True, stop=True)
                    last.then_inc(bias_turned, 1)

                def diff_inputs(self):
                    enter()
                    for c in range(3):
                        chunk(2 * (c % 2), 512, turned(bank()) if c < 2 else rows(bank()))
                    self.turn_bias(0)

                def turn_probs(self, u, t, b, src=None):
                    U = units.n + u
                    pe.wait_ge(weighed, U + 1)
                    if u >= 2:
                        pe.wait_ge(probs_kept, U - 1)
                    for m in range(t + 1):
                        last = pe.transpose(ps[:, b, P * m:P * m + P], Pb[u % 2][:, P * m:P * m + P], ident)
                    last.then_inc(probs_turned, 1)

                def diff(self):
                    enter()

                    def score(u):
                        h, t = u // 2, u % 2
                        if u >= 2:
                            pe.wait_ge(maxed, units.n + u - 1)
                        for j in range(2):
                            half = slice(64 * j, 64 * j + 64)
                            last = pe.matmul(ps[:, 2 * (u % 2) + j, 0:P * (t + 1)], aqT[half, h, t * P:(t + 1) * P],
                                             akT[half, h, 0:P * (t + 1)], start=True, stop=True)
                        last.then_inc(scored, 1)

                    def values(u):
                        h, t = u // 2, u % 2
                        pe.wait_ge(probs_kept, units.n + u + 1)
                        if u >= 2:
                            pe.wait_ge(o_hi, 16 + u - 1)
                        for m in range(t + 1):
                            last = pe.matmul(ps[:, 6 + u % 2, 0:P], PTu[u % 2][:, P * m:P * m + P], av[:, m, P * h:P * h + P],
                                             start=m == 0, stop=m == t)
                        last.then_inc(pv_done, 1)

                    score(0)
                    for u in range(8):
                        if u + 1 < 8:
                            score(u + 1)
                        self.turn_probs(u, u % 2, 4 + u % 2)
                        if u:
                            values(u - 1)
                    values(7)
                    units.next(8)
                    groups.next(8)

                def diff_norm(self):
                    enter()
                    pe.wait_ge(branch_kept, 1)
                    for h in range(4):
                        for t in range(T):
                            c = S * (h % 2) + P * t
                            last = pe.transpose(ps[:, h // 2, c:c + P], oA[:, t, h, :], ident)
                    last.then_inc(branch_done, 1)

                def sparse_inputs(self):
                    enter()
                    chunk(0, 512, turned(bank()))
                    b = bank()
                    chunk(2, 512, [("N", t, 0, P, ps[:, b, P * t:P * t + P]) for t in range(T)]
                          + [("T", P + P * j, P, ps[:, b + 1, S * j:S * j + S]) for j in range(2)]
                          + [("T", 384, P, ps[:, b + 2, 0:S])])
                    chunk(0, 512, turned(bank()))
                    b = bank()
                    chunk(2, 264, [("N", t, 0, 264, ps[:, b + t, 0:264]) for t in range(T)])
                    self.turn_bias(1)

                def latent(self):
                    enter()
                    pe.wait_ge(branch_kept, 2)
                    for t in range(T):
                        last = pe.transpose(ps[:, 0, P * t:P * t + P], kvn[:, t, :], ident)
                    last.then_inc(branch_kept, 1)

                def select(self, t):
                    enter()
                    w = P * (t + 1)
                    for h in range(8):
                        r = slice(32 * (h % 4), 32 * (h % 4) + 32)
                        last = pe.matmul(ps[:, h % 4, w * (h // 4):w * (h // 4) + w], iqT[r, h // 4, t * P:(t + 1) * P],
                                         ikT[r, 0:w], start=True, stop=True, tile_position=(32 * (h % 4), 0))
                    last.then_inc(index_scored, 1)

                def dsa(self, t):
                    enter()
                    w = P * (t + 1)

                    def score(u):
                        if u >= 2:
                            pe.wait_ge(maxed, units.n + u - 1)
                        pe.matmul(ps[:, u % 2, 0:w], bqT[:, u, t * P:(t + 1) * P], kvT[:, 0:w], start=True, stop=True)\
                          .then_inc(scored, 1)

                    score(0)
                    for u in range(4):
                        if u + 1 < 4:
                            score(u + 1)
                        self.turn_probs(u, t, 2 + u % 2)
                    units.next(4)
                    pe.wait_ge(probs_kept, units.n)
                    for m in range(t + 1):
                        last = pe.matmul(ps[:, 4, :], kvn[:, m, :], PTd[:, :, m, :], start=m == 0, stop=m == t)
                    last.then_inc(pv_done, 1)
                    groups.next(1)
                    pe.wait_ge(lat_kept, t + 1)
                    for h in range(4):
                        last = pe.matmul(ps[64 * (h % 2):64 * (h % 2) + 64, 5, P * (h // 2):P * (h // 2) + P],
                                         w_uv[:, h, :], o_lat[:, P * h:P * h + P], start=True, stop=True)
                    last.then_inc(branch_done, 1)

                def moba(self):
                    self.turn_bias(2)
                    enter()

                    def score(u):
                        h, t = u // 2, u % 2
                        r, w = slice(64 * (h % 2), 64 * (h % 2) + 64), P * (t + 1)
                        if u >= 2:
                            pe.wait_ge(maxed, units.n + u - 1)
                        pe.matmul(ps[:, u % 2, 0:w], cqT[r, h // 2, t * P:(t + 1) * P], ckT[r, h // 2, 0:w],
                                  start=True, stop=True).then_inc(scored, 1)

                    def values(u):
                        h, t = u // 2, u % 2
                        pe.wait_ge(probs_kept, units.n + u + 1)
                        for m in range(t + 1):
                            c = S * (h // 2) + P * t
                            last = pe.matmul(ps[64 * (h % 2):64 * (h % 2) + 64, 4, c:c + P], cv[:, m, 64 * h:64 * h + 64],
                                             PTu[u % 2][:, P * m:P * m + P], start=m == 0, stop=m == t)
                        last.then_inc(pv_done, 1)

                    score(0)
                    for u in range(8):
                        if u + 1 < 8:
                            score(u + 1)
                        self.turn_probs(u, u % 2, 2 + u % 2)
                        if u:
                            values(u - 1)
                    values(7)
                    units.next(8)
                    groups.next(8)

                def merge(self):
                    enter()
                    pe.wait_ge(aT_made, c_turned.next())
                    for br in range(3):
                        if br == 2:
                            pe.wait_ge(branch_kept, 4)
                        for s in ((0, 1), (2,), (3,))[br]:
                            pe.wait_ge(lo_ready[s], uses.next(s))
                        for c in range(2):
                            for t in range(T):
                                o, tok = ps[:, 4 * (br % 2) + 2 * t + c, :], slice(t * P, (t + 1) * P)
                                n = (4, 2, 2)[br]
                                for k in range(n):
                                    kk = (0, 4, 6)[br] + k
                                    s, at = (c, 512 * k) if br == 0 else (br + 1, 1024 * k + 512 * c)
                                    last = parts(o, aT_hi[:, kk, tok], aT_lo[:, kk, tok], whi[:, s, at:at + 512],
                                                 wlo[:, s, at:at + 512], k == 0, k == n - 1)
                            if br == 0:
                                last.then_inc(consumed[c], 1)
                        if br:
                            last.then_inc(consumed[br + 1], 1)
                        pe.drain().then_inc(branch_done, 1)

                def mlp(self):
                    enter()
                    rounds = 8
                    ub, fb = list(uses.n), c_ffn.n
                    for b in range(4):
                        pe.matmul(ps[:, b, :], zero[:, 0:P], zero[:, :], start=True, stop=False, skip_group_check=True)

                    def up(i):
                        for s in range(2):
                            pe.wait_ge(lo_ready[s], ub[s] + i + 1)
                            h, lw = (w[:, s, :].rearrange("p (k n) -> p k n", k=4) for w in (whi, wlo))
                            for t in range(T):
                                tok = slice(t * P, (t + 1) * P)
                                for r in range(4):
                                    k = 4 * s + r
                                    last = parts(ps[:, 4 + t, :], aT_hi[:, k, tok], aT_lo[:, k, tok], h[:, r, :],
                                                 lw[:, r, :], k == 0, k == KD - 1)
                                if s == 1 and t == 0:
                                    last.then_inc(gate_half, 1)
                            last.then_inc(consumed[s], 1)

                    def turn(i):
                        for t in range(T):
                            pe.wait_ge(hid_made, 2 * (fb + i) + t + 1)
                            for k in range(4):
                                c = S * (k % 2) + P * t
                                last = pe.transpose(ps[:, 6 + k // 2, c:c + P], hs[:, t, P * k:P * k + P], ident)
                        last.then_inc(hid_turned, 1)

                    def down(i, stop):
                        pe.wait_ge(hT_made, fb + i + 1)
                        for s in (2, 3):
                            pe.wait_ge(lo_ready[s], ub[s] + i + 1)
                            h, lw = (w[:, s, :].rearrange("p (k c n) -> p k c n", k=2, c=2) for w in (whi, wlo))
                            for t in range(T):
                                tok = slice(t * P, (t + 1) * P)
                                for c in range(2):
                                    for k in range(2):
                                        kk = 2 * (s - 2) + k
                                        last = parts(ps[:, 2 * t + c, :], hT_hi[:, kk, tok], hT_lo[:, kk, tok],
                                                     h[:, k, c, :], lw[:, k, c, :], False, stop and kk == 3)
                            last.then_inc(consumed[s], 1)

                    up(0)
                    turn(0)
                    with pe.Fori(1, rounds) as i:
                        up(i)
                        down(i - 1, False)
                        turn(i)
                    down(rounds - 1, True)

                def end(self):
                    pass

            pe.wait_ge(const_in, 16)
            pe.wait_ge(zero_made, 1)
            program(Pe())


_NAMES = ["x", "mem", "ffn1_norm", "ffn1_w_in", "ffn1_w_out", "mix_norm", "xattn_norm", "mem_norm", "xattn_w_q",
          "xattn_w_kv", "xattn_w_o", "ffn2_norm", "ffn2_w_in", "ffn2_w_out", "pool_w", "pool_b", "pool_scale",
          "nsa_w_in", "nsa_cmp_pos", "nsa_cmp_w1", "nsa_cmp_w2", "nsa_w_o", "final_norm", "c_2", "rel_bias_2",
          "ada_w_2", "ada_b_2", "norm_mix_2", "w_in_2", "gate_b_2", "diff_lambda_2", "diff_subln_2",
          "dsa_kv_norm_2", "dsa_w_uv_2", "w_br_a_2", "w_br_b_2", "w_br_c_2", "w_o_2", "norm_mlp_2", "w_ff1_2",
          "w_ff2_2", "norm_final_2"]


def kernel(**inputs):
    import concourse.bacc as bacc
    from concourse.bass_utils import run_bass_kernel_spmd

    arrays = {n: np.ascontiguousarray(inputs[n]) for n in _NAMES}
    arrays["constants"] = constant_table()
    nc = bacc.Bacc("TRN2", target_bir_lowering=False, num_devices=1)
    A = {n: nc.dram_tensor(f"in_{n}", a.shape, F32, kind="ExternalInput").ap() for n, a in arrays.items()}
    out = nc.dram_tensor("out_x", (1, S, D), F32, kind="ExternalOutput").ap()
    build(nc, A, out)
    r = run_bass_kernel_spmd(nc, [{f"in_{n}": a for n, a in arrays.items()}], core_ids=[0])
    return r.results[0]["out_x"]
```

```python
import math
from contextlib import ExitStack

import numpy as np

import concourse.bass as bass
from concourse import mybir

F32 = mybir.dt.float32
F32R = mybir.dt.float32r
ALU = mybir.AluOpType
ACT = mybir.ActivationFunctionType
AX = mybir.AxisListType.X

P = 128
D = 1024
S = 256
T = S // P
KD = D // P
FF = 2816
HI = 256
EPS = 1e-6
NEG = -1e30
BIG = 3.0e38

SLOTS = 4
SLAB = 2048

NSA_H, NSA_G, NSA_R, NSA_DH = 16, 4, 4, 64
N_CMP, CMP_BLOCK, CMP_STRIDE, CMP_HID = 15, 32, 16, 256
COLS = dict(aq=0, ak=512, av=1024, bq=1536, bkv=2048, biq=2176, bik=2432, biw=2464,
            cq=2472, ck=2728, cv=2984, g=3240)
N_BUCKETS, MAX_DISTANCE = 32, 128
TOPK = 64
LAM_INIT = 0.8 - 0.6 * math.exp(-0.3 * 0)
POOL_WINDOWS = (2, 4, 8, 16)

C_IDENT, C_FLIP, C_CAUSAL, C_CMP, C_VIS = 0, 128, 256, 512, 544
C_HOT, C_BAND, C_END = 546, 930, 930 + 4 * 384


def constant_table():
    c = np.zeros((P, C_END), np.float32)
    i = np.arange(P)
    c[i, C_IDENT + i] = 1.0
    c[i, C_FLIP + 127 - i] = 1.0
    q, k = i[:, None], i[None, :]
    c[:, C_CAUSAL + 128:C_CAUSAL + 256] = np.where(k <= q, 0.0, NEG)
    n = np.arange(N_CMP)
    for t in range(T):
        end = n * CMP_STRIDE + CMP_BLOCK - 1
        c[:, C_CMP + 16 * t:C_CMP + 16 * t + N_CMP] = np.where(end[None, :] <= 128 * t + q, 0.0, NEG)
    c[:, C_VIS] = i >= CMP_BLOCK - 1
    dist = 255 - np.arange(384)
    half = N_BUCKETS // 2
    nf = np.maximum(dist, 1).astype(np.float32)
    large = half + (np.log(nf / np.float32(half)) / np.float32(math.log(MAX_DISTANCE / half))
                    * np.float32(N_BUCKETS - half)).astype(np.int32)
    bucket = np.where(dist < half, dist, np.minimum(large, N_BUCKETS - 1))
    bucket = np.where(dist < 0, N_BUCKETS, bucket)
    c[bucket, C_HOT + np.arange(384)] = 1.0
    for w, win in enumerate(POOL_WINDOWS):
        for tile, to in ((0, np.arange(S)), (1, np.arange(P, S))):
            frm = tile * P + i
            gap = to[None, :] - frm[:, None]
            cnt = np.minimum(to + 1, win).astype(np.float32)
            m = np.where((gap >= 0) & (gap < win), np.float32(1) / cnt[None, :], 0) - (gap == 0)
            at = C_BAND + 384 * w + 256 * tile
            c[:, at:at + len(to)] = m
    return c


class Uses:

    def __init__(self):
        self.n = [0] * SLOTS

    def next(self, slot):
        self.n[slot] += 1
        return self.n[slot]


class Count:

    def __init__(self):
        self.n = 0

    def next(self, k=1):
        self.n += k
        return self.n


def build(nc, A, out):
    ds = bass.ds
    with ExitStack() as ctx:
        def sb(name, shape, dt=F32):
            return ctx.enter_context(nc.sbuf_tensor(name, shape, dt))

        def sem(name):
            return ctx.enter_context(nc.semaphore(name))

        raw = sb("raw", [P, SLOTS, SLAB])
        whi = sb("whi", [P, SLOTS, SLAB], F32R)
        wlo = sb("wlo", [P, SLOTS, SLAB], F32R)
        x = sb("x", [P, T, D])
        xn = sb("xn", [P, T, D])
        aT_hi = sb("aT_hi", [P, KD, S], F32R)
        aT_lo = sb("aT_lo", [P, KD, S], F32R)
        hs = sb("hs", [P, T, 512])
        hT_hi = sb("hT_hi", [P, 4, S], F32R)
        hT_lo = sb("hT_lo", [P, 4, S], F32R)
        gain = sb("gain", [P, 2, D])
        cst = sb("cst", [P, C_HOT])
        area = sb("area", [P, 14000])
        zero = sb("zero", [P, 512], F32R)
        small = sb("small", [P, 64])
        ps = ctx.enter_context(nc.psum_tensor("ps", [P, 8, 512], F32))

        ident = cst[:, C_IDENT:C_IDENT + 128]
        ssq, var, rstd = small[:, 0:2], small[:, 2:4], small[:, 4:6]
        minus_half = small[:, 6:8]
        nmx, den, rec = small[:, 8:14], small[:, 14:20], small[:, 20:26]

        landed = [sem(f"landed{s}") for s in range(SLOTS)]
        hi_ready = [sem(f"hi_ready{s}") for s in range(SLOTS)]
        lo_ready = [sem(f"lo_ready{s}") for s in range(SLOTS)]
        consumed = [sem(f"consumed{s}") for s in range(SLOTS)]
        stage_act, stage_dve = sem("stage_act"), sem("stage_dve")
        x_half = sem("x_half")
        x_in, mem_in, const_in, gain_in = sem("x_in"), sem("mem_in"), sem("const_in"), [sem(f"gain_in{b}") for b in range(2)]
        zero_made, mix_in = sem("zero_made"), sem("mix_in")
        squared, rstd_made, rows_normed = sem("squared"), sem("rstd_made"), sem("rows_normed")
        rows_turned, aT_hi_made, aT_made = sem("rows_turned"), sem("aT_hi_made"), sem("aT_made")
        pool_step, act_step, dve_step = sem("pool_step"), sem("act_step"), sem("dve_step")
        act_evac, dve_evac = sem("act_evac"), sem("dve_evac")
        gate_half, silu_made, hid_made = sem("gate_half"), sem("silu_made"), sem("hid_made")
        hid_turned, hT_hi_made, hT_made = sem("hid_turned"), sem("hT_hi_made"), sem("hT_made")
        scored, maxed, exped, weighed = sem("scored"), sem("maxed"), sem("exped"), sem("weighed")
        probs_turned, probs_kept, pv_done = sem("probs_turned"), sem("probs_kept"), sem("pv_done")
        o_hi, o_kept = sem("o_hi"), sem("o_kept")
        cmp_scored, cmp_centred, cmp_exped, cmp_weighed = (sem(f"cmp_{n}") for n in ("scored", "centred", "exped", "weighed"))
        cmp_turned, cmp_kept = sem("cmp_turned"), sem("cmp_kept")
        pos_in, pos_made, w2_in, gelu_made, cmp_made = (sem(n) for n in ("pos_in", "pos_made", "w2_in", "gelu_made", "cmp_made"))
        cond_in, cond_made = sem("cond_in"), sem("cond_made")
        ada_landed, ada_used, ada_out = ([sem(f"{n}{b}") for b in range(2)] for n in ("ada_landed", "ada_used", "ada_out"))
        ada_in, ada_summed, ones_made = sem("ada_in"), sem("ada_summed"), sem("ones_made")
        hot_in, dist_made, dist_out, skew_in = (sem(n) for n in ("hot_in", "dist_made", "dist_out", "skew_in"))
        lam_summed, row_in, gate_b_in, bias_turned = (sem(n) for n in ("lam_summed", "row_in", "gate_b_in", "bias_turned"))
        summed, powered, index_scored, lat_kept = (sem(n) for n in ("summed", "powered", "index_scored", "lat_kept"))
        branch_done, branch_kept, mask_row = sem("branch_done"), sem("branch_kept"), sem("mask_row")
        stored, relu_made = sem("stored"), sem("relu_made")

        kT = area[:, 0:2048].rearrange("p (k s) -> p k s", k=KD)
        vm = area[:, 2048:4096].rearrange("p (t d) -> p t d", t=T)
        qT = area[:, 4096:6144].rearrange("p (k s) -> p k s", k=KD)
        PT = area[:, 6144:8192]
        pool_b = area[:, 6144:7168]
        pool_s = area[:, 7168:8192]
        band = area[:, 8192:8192 + 4 * 384].rearrange("p (w c) -> p w c", w=4)
        xnf = xn[:, :, :].rearrange("p t n -> p (t n)")
        hsf = hs[:, :, :].rearrange("p t n -> p (t n)")
        Pb = [xnf[:, 512 * b:512 * b + 512] for b in range(3)]
        ksT = area[:, 6144:7168].rearrange("p (g s) -> p g s", g=4)
        kwT = area[:, 7168:8192].rearrange("p (g s) -> p g s", g=4)
        vs = area[:, 8192:8704].rearrange("p (t n) -> p t n", t=T)
        vw = area[:, 8704:9216].rearrange("p (t n) -> p t n", t=T)
        gates = area[:, 9216:9312].rearrange("p (t n) -> p t n", t=T)
        blk = area[:, 9344:11264].rearrange("p (v j g n) -> p v j g n", v=2, j=16, g=4)
        nsaP = [area[:, 9344 + 2048 * b:11392 + 2048 * b].rearrange("p (r n) -> p r n", r=4) for b in range(2)]
        nsaPc = [a.rearrange("p (r n) -> p r n", r=4) for a in (area[:, 13440:13952], hsf[:, 512:1024])]
        cmpP = hsf[:, 0:512].rearrange("p (t h n) -> p t h n", t=T, h=NSA_H)[:, :, :, 0:N_CMP]
        cmp_max, cmp_rec = (xnf[:, c:c + 32].rearrange("p (t h) -> p t h", t=T) for c in (1888, 1920))
        pos_rows, posT = hsf[0:32, 0:128], hsf[:, 128:160]
        hidT = hsf[:, 160:400].rearrange("p (v h n) -> p v h n", v=2, h=2)
        w2k = hsf[:, 400:656].rearrange("p (h n) -> p h n", h=2)
        w2v = hsf[:, 656:784].rearrange("p (h n) -> p h n", h=2)
        kcT = xnf[:, 1568:1628]
        vcmp = xnf[0:15, 1628:1884]
        aTf_hi = aT_hi[:, :, :].rearrange("p k s -> p (k s)")
        aTf_lo = aT_lo[:, :, :].rearrange("p k s -> p (k s)")

        yT = area[:, 0:2048].rearrange("p (k s) -> p k s", k=KD)
        yTf = area[:, 0:2048]
        mod = area[:, 0:3072]
        out_gate = area[:, 2048:3072]
        bgate = area[:, 3072:9216].rearrange("p (t n) -> p t n", t=T)
        aqT = area[:, 9216:10240].rearrange("p (k s) -> p k s", k=4)
        akT = area[:, 10240:11264].rearrange("p (k s) -> p k s", k=4)
        av = area[:, 11264:12288].rearrange("p (t n) -> p t n", t=T)
        bqT = area[:, 9216:10240].rearrange("p (k s) -> p k s", k=4)
        kvn = area[:, 10240:10496].rearrange("p (t n) -> p t n", t=T)
        iqT = area[:, 10496:11008].rearrange("p (k s) -> p k s", k=2)
        ikT = area[:, 11008:11264]
        cqT = area[:, 11264:11776].rearrange("p (k s) -> p k s", k=2)
        ckT = area[:, 11776:12288].rearrange("p (k s) -> p k s", k=2)
        cv = area[:, 12288:12800].rearrange("p (t n) -> p t n", t=T)
        iw = area[:, 12800:12816].rearrange("p (t n) -> p t n", t=T)
        bias = area[:, 12816:13840].rearrange("p (h k) -> p h k", h=4)
        kvT = area[:, 1536:1792]
        w_uv = area[:, 1792:2048].rearrange("p (h e) -> p h e", h=4)
        oA = hsf.rearrange("p (t h e) -> p t h e", t=T, h=4)
        PTd = hsf.rearrange("p (h m q) -> p h m q", h=4, m=2)
        skew = gain[:, 1, :].rearrange("p (h k) -> p h k", h=4)
        PTu = [xnf[:, 1056 + 256 * b:1312 + 256 * b] for b in range(2)]
        o_lat, score_part = xnf[:, 1056:1568], xnf[:, 1568:1824]
        sel = [Pb[1][:, 256:384], Pb[0][:, 256:512]]
        work = [xnf[:, 1056:1184], xnf[:, 1184:1440]]
        top8 = [xnf[:, 1824:1832], xnf[:, 1960:1968]]
        subln, kv_gain = xnf[:, 1568:1696], xnf[:, 1832:1960]
        condT = area[:, 13952:13960]
        ada_turns = [(range(0, 4), 1), (range(4, 8), 1), (range(8, 12), 0)]

        def ada_acc(c, buf):
            return gain[:, buf, 512 * (c % 2):512 * (c % 2) + 512]

        ada_parts = area[:, 3072:6144].rearrange("p (c n) -> p c n", c=6)
        ada_bias = area[:, 6144:9216]
        ones = hsf[:, 0:P]
        hot, rel, dist_rows = area[0:33, 9216:9600], area[0:33, 9600:9612], area[0:12, 9728:10112]
        lam_in, lam_prod = area[:, 10240:10496], area[:, 10496:10624]
        neg_lam, lam2 = small[:, 60:61], small[:, 58:60]
        ss8, var8, rstd8, minus_half8 = (small[:, c:c + 8] for c in (26, 34, 42, 50))
        dist_dram = nc.dram_tensor("dist_rows", (12, 384), F32, kind="Internal").ap()
        ada_dram = nc.dram_tensor("ada_sums", (12, P, 512), F32, kind="Internal").ap()

        def twice(slot):
            return (whi[:, slot, :].rearrange("p (g a n) -> p g a n", a=2, n=64),
                    raw[:, slot, 0:SLAB // 2].rearrange("p (g n) -> p g n", n=64).unsqueeze(2)
                    .to_broadcast([P, SLAB // 128, 2, 64]))

        def PTc(h):
            return PT[:, 512 * (h % 2):512 * (h % 2) + 512].rearrange("p (m q) -> p m q", m=2)

        L = range(2)
        gains = []
        for l in L:
            gains += [A["mem_norm"][l], A["ffn1_norm"][l], A["mix_norm"][l], A["xattn_norm"][l], A["ffn2_norm"][l]]

        gains += [A["final_norm"], A["norm_mix_2"][0], A["norm_mlp_2"][0], A["norm_final_2"]]

        block = ctx.enter_context(nc.Block())

        def program(e):
            for l in L:
                e.norm(5 * l, mem=True)
                e.kv(l)
                e.norm(5 * l + 1)
                e.ffn(A["ffn1_w_in"][l], A["ffn1_w_out"][l])
                e.norm(5 * l + 2, turn=l > 0)
                if l == 0:
                    e.pool()
                else:
                    e.nsa_inputs()
                    e.nsa_compress()
                    e.nsa_attend()
                    e.project(A["nsa_w_o"][0])
                e.norm(5 * l + 3)
                e.query(l)
                e.cross(l)
                e.project(A["xattn_w_o"][l])
                e.norm(5 * l + 4)
                e.ffn(A["ffn2_w_in"][l], A["ffn2_w_out"][l])
            e.norm(10, turn=False, keep=True)
            e.ada(0)
            e.norm(11, modulate=True)
            e.gate_inputs()
            e.diff_inputs()
            e.diff()
            e.diff_norm()
            e.sparse_inputs()
            e.latent()
            e.select()
            e.dsa(0)
            e.dsa(1)
            e.moba()
            e.merge()
            e.project(A["w_o_2"][0], gated=True)
            e.ada(1)
            e.norm(12, modulate=True)
            e.mlp()
            e.norm(13, turn=False, keep=True)
            e.end()

        @block.sync
        def _(sp):
            uses = Uses()
            stages = Count()

            def slab(slot, halves, n=None):
                if n is None:
                    n = uses.next(slot)
                if not (type(n) is int and n == 1):
                    sp.wait_ge(lo_ready[slot], n - 1)
                for dst, src in halves:
                    sp.dma_start(dst, src).then_inc(landed[slot], 16)

            def pieces(w, cols, n, pair):
                wv = w.rearrange("(k p) n -> p k n", p=P)
                for s in range(2):
                    d = raw[:, pair + s, 0:4 * n].rearrange("p (k n) -> p k n", k=4)
                    slab(pair + s, [(d[:, :, to:to + m], wv[:, 4 * s:4 * s + 4, c:c + m]) for to, c, m in cols])

            def chunk(w, c0, n, pair):
                wv = w.rearrange("(k p) n -> p k n", p=P)
                for s in range(2):
                    d = raw[:, pair + s, 0:4 * n].rearrange("p (k n) -> p k n", k=4)
                    slab(pair + s, [(d[:, 2 * j:2 * j + 2, :],
                                     wv[:, 4 * s + 2 * j:4 * s + 2 * j + 2, c0:c0 + n]) for j in range(2)])

            def ada_slabs(turn):
                w = A["ada_w_2"][0].rearrange("(k p) n -> p k n", p=P)
                for c in ada_turns[turn][0]:
                    for s in range(2):
                        if c == ada_turns[turn][0][0]:
                            sp.wait_ge(lo_ready[2 + s], uses.n[2 + s])
                        else:
                            sp.wait_ge(ada_used[s], c)
                        d = raw[:, 2 + s, :].rearrange("p (k n) -> p k n", k=4)
                        for j in range(2):
                            sp.dma_start(d[:, 2 * j:2 * j + 2, :], w[:, 4 * s + 2 * j:4 * s + 2 * j + 2, 512 * c:512 * c + 512])\
                              .then_inc(ada_landed[s], 16)
                for s in range(2):
                    ada_seen[s] = ada_turns[turn][0][-1] + 1

            ada_seen = [0, 0]

            class Sp:
                def norm(self, m, mem=False, turn=True, keep=False, modulate=False):
                    stages.next()

                def kv(self, l):
                    stages.next()
                    for c in range(4):
                        chunk(A["xattn_w_kv"][l], 512 * c, 512, 2 * (c % 2))
                        if l == 0 and c < T:
                            sp.dma_start(x[:, c, :], A["x"][0, c * P:(c + 1) * P, :]).then_inc(x_in, 16)

                def ffn(self, w_in, w_out):
                    stages.next()
                    rounds = FF // HI
                    wi = w_in.rearrange("(k p) n -> p k n", p=P)
                    wo = w_out.rearrange("(k p) n -> p k n", p=P)

                    def up(i, base):
                        for s in range(2):
                            d = raw[:, s, :].rearrange("p (k h n) -> p k h n", k=4, h=2)
                            slab(s, [(d[:, :, h, :], wi[:, 4 * s:4 * s + 4, ds(FF * h + i * HI, HI)])
                                     for h in range(2)], base[s] + i + 1)

                    def down(i, base, slot=2):
                        d = raw[:, slot, :].rearrange("p (k n) -> p k n", k=2)
                        slab(slot, [(d[:, j:j + 1, :], wo[:, ds(2 * i + j, 1), :]) for j in range(2)],
                             base[2] + i + 1 if slot == 2 else None)

                    base = list(uses.n)
                    up(0, base)
                    with sp.Fori(1, rounds) as i:
                        up(i, base)
                        down(i - 1, base)
                    down(rounds - 1, base, 3)
                    for s in range(3):
                        uses.n[s] += rounds - s // 2

                def pool(self):
                    stages.next()
                    chunk(A["xattn_w_q"][0], 0, 512, 0)
                    w = A["pool_w"][0].rearrange("g (k p) n -> p (g k) n", p=P)
                    d = raw[:, 2, :].rearrange("p (k n) -> p k n", n=256)
                    slab(2, [(d[:, 4 * j:4 * j + 4, :], w[:, 4 * j:4 * j + 4, :]) for j in range(2)])

                def query(self, l):
                    stages.next()
                    for c in range(1 if l == 0 else 0, 2):
                        chunk(A["xattn_w_q"][l], 512 * c, 512, 2 * c)

                def cross(self, l):
                    stages.next()
                    chunk(A["xattn_w_o"][l], 0, 512, 0)
                    ada_slabs(2 * l)

                def project(self, w, gated=False):
                    stages.next()
                    if not gated:
                        for s in range(2):
                            sp.wait_ge(ada_used[s], ada_seen[s])
                    for c in range(0 if gated else 1, 2):
                        chunk(w, 512 * c, 512, 2 * c)

                def nsa_inputs(self):
                    stages.next()
                    w = A["nsa_w_in"][0]
                    for c in range(2):
                        chunk(w, 512 * c, 512, 2 * c)
                    for c, c0 in enumerate((1024, 1280, 1536, 2048)):
                        chunk(w, c0, 256, 2 * (c % 2))
                    wv = w.rearrange("(k p) n -> p k n", p=P)
                    for s in range(2):
                        d = raw[:, s, :].rearrange("p (k h n) -> p k h n", k=4, h=2)
                        slab(s, [(d[:, :, h, :], wv[:, 4 * s:4 * s + 4, c0:c0 + 256]) for h, c0 in enumerate((1792, 2304))])
                    chunk(w, 2560, 48, 2)

                def nsa_compress(self):
                    stages.next()
                    for v in range(2):
                        w = A["nsa_cmp_w1"][0, v].rearrange("(j p) n -> p j n", p=P)
                        for s in range(2):
                            d = raw[:, 2 * v + s, :].rearrange("p (j n) -> p j n", j=8)
                            slab(2 * v + s, [(d[:, 4 * j:4 * j + 4, :], w[:, 8 * s + 4 * j:8 * s + 4 * j + 4, :])
                                             for j in range(2)])

                def nsa_attend(self):
                    stages.next()
                    chunk(A["nsa_w_o"][0], 0, 512, 0)
                    ada_slabs(1)

                def skip(self, *_):
                    stages.next()

                ada = diff = diff_norm = latent = select = dsa = skip

                def moba(self):
                    stages.next(2)

                def gate_inputs(self):
                    stages.next()
                    for c in range(6):
                        chunk(A["w_in_2"][0], COLS["g"] + 512 * c, 512, 2 * (c % 2))

                def diff_inputs(self):
                    stages.next(2)
                    for c, n in enumerate(("aq", "ak", "av")):
                        chunk(A["w_in_2"][0], COLS[n], 512, 2 * (c % 2))

                def sparse_inputs(self):
                    stages.next(2)
                    w = A["w_in_2"][0]
                    chunk(w, COLS["bq"], 512, 0)
                    pieces(w, [(0, COLS["bkv"], 384)] + [(384 + 32 * j, COLS["bik"], 32) for j in range(4)], 512, 2)
                    chunk(w, COLS["cq"], 512, 0)
                    pieces(w, [(0, COLS["cv"], 256), (256, COLS["biw"], 8)], 264, 2)

                def merge(self):
                    stages.next()
                    a = A["w_br_a_2"][0].rearrange("(k p) n -> p k n", p=P)
                    for s in range(2):
                        d = raw[:, s, :].rearrange("p (k n) -> p k n", k=4)
                        slab(s, [(d[:, 2 * j:2 * j + 2, :], a[:, 2 * j:2 * j + 2, 512 * s:512 * s + 512]) for j in range(2)])
                    for s, n in ((2, "w_br_b_2"), (3, "w_br_c_2")):
                        w = A[n][0].rearrange("(k p) n -> p k n", p=P)
                        d = raw[:, s, :].rearrange("p (k n) -> p k n", k=2)
                        slab(s, [(d[:, j:j + 1, :], w[:, j:j + 1, :]) for j in range(2)])

                def mlp(self):
                    stages.next()
                    rounds = 8
                    wi = A["w_ff1_2"][0].rearrange("(k p) n -> p k n", p=P)
                    wo = A["w_ff2_2"][0].rearrange("(k p) n -> p k n", p=P)
                    base = list(uses.n)

                    def up(i):
                        for s in range(2):
                            d = raw[:, s, :].rearrange("p (k n) -> p k n", k=4)
                            slab(s, [(d[:, 2 * j:2 * j + 2, :], wi[:, 4 * s + 2 * j:4 * s + 2 * j + 2, ds(512 * i, 512)])
                                     for j in range(2)], base[s] + i + 1)

                    def down(i):
                        for s in range(2):
                            d = raw[:, 2 + s, :].rearrange("p (k n) -> p k n", k=2)
                            slab(2 + s, [(d[:, j:j + 1, :], wo[:, ds(4 * i + 2 * s + j, 1), :]) for j in range(2)],
                                 base[2 + s] + i + 1)

                    up(0)
                    with sp.Fori(1, rounds) as i:
                        up(i)
                        down(i - 1)
                    down(rounds - 1)
                    for s in range(4):
                        uses.n[s] += rounds

                def end(self):
                    sp.wait_ge(stage_act, stages.n)
                    sp.wait_ge(stage_dve, stages.n)

            sp.dma_start(cst[:, :], A["constants"][:, 0:C_HOT]).then_inc(const_in, 16)
            program(Sp())
            for t in range(T):
                sp.dma_start(out[0, t * P:(t + 1) * P, :], x[:, t, :]).then_inc(stored, 16)
            sp.wait_ge(stored, 16 * T)

        @block.gpsimd
        def _(pool):
            stages, steps = Count(), Count()
            squares = Count()

            def enter():
                if stages.n:
                    pool.wait_ge(stage_act, stages.n)
                    pool.wait_ge(stage_dve, stages.n)
                stages.next()

            def load_gain(m):
                pool.dma_start(gain[:, m % 2, :], gains[m].unsqueeze(0).to_broadcast([P, D])).then_inc(gain_in[m % 2], 16)

            def power(src, dst, n, mean):
                pool.tensor_scalar(var8[:, 0:n], src, 1.0 / mean, EPS, ALU.mult, ALU.add).then_inc(pool_step, 1)
                pool.wait_ge(pool_step, steps.next())
                return pool.tensor_tensor(dst, var8[:, 0:n], minus_half8[:, 0:n], ALU.pow)

            def spread(to, row, done):
                pool.dma_start(to, row.unsqueeze(0).to_broadcast([P, row.shape[0]])).then_inc(done, 16)

            def load_skew(b):
                pool.dma_start(skew, bass.AP(dist_dram.tensor, 4 * 384 * b, [[1, P], [384, 4], [1, S]])).then_inc(skew_in, 16)

            def store_ada(turn):
                cs, buf = ada_turns[turn]
                for c in cs:
                    pool.wait_ge(ada_used[1], c + 1)
                    pool.dma_start(ada_dram[c], ada_acc(c, buf)).then_inc(ada_out[c % 2], 16)
                for b in range(2):
                    pool.wait_ge(ada_out[b], 16 * (cs[-1] + 1) // 2)

            def load_mem():
                for t in range(T):
                    pool.dma_start(xn[:, t, :], A["mem"][0, t * P:(t + 1) * P, :]).then_inc(mem_in, 16)

            class Pool:
                def norm(self, m, mem=False, turn=True, keep=False, modulate=False):
                    enter()
                    if m == 9:
                        self.load_ada(0)
                        pool.dma_start(hot, A["constants"][0:33, C_HOT:C_HOT + 384]).then_inc(hot_in, 16)
                        pool.dma_start(rel[0:32], A["rel_bias_2"]).then_inc(hot_in, 16)
                        pool.memset(rel[32:33], NEG).then_inc(mask_row, 1)
                        pool.wait_ge(mask_row, 1)
                        spread(lam_in, A["diff_lambda_2"][0].rearrange("a d -> (a d)"), hot_in)
                    for t in range(T):
                        pool.wait_ge(squared, squares.next())
                        power(ssq[:, t:t + 1], rstd[:, t:t + 1], 1, D).then_inc(rstd_made, 1)
                        pool.wait_ge(rstd_made, 2 * m + t + 1)
                    if m + 1 < len(gains):
                        load_gain(m + 1)
                    self.norms = m + 1

                def kv(self, l):
                    enter()
                    if l == 0:
                        pool.dma_start(condT, A["c_2"].rearrange("a (k p) -> p (a k)", p=P), allow_slow_non_contiguous=True)\
                            .then_inc(cond_in, 16)

                def ffn(self, w_in, w_out):
                    enter()
                    if self.norms == 2:
                        pool.dma_start(pool_b, A["pool_b"][0].unsqueeze(0).to_broadcast([P, D])).then_inc(mix_in, 16)
                        pool.dma_start(pool_s, A["pool_scale"][0].unsqueeze(0).to_broadcast([P, D])).then_inc(mix_in, 16)
                        pool.dma_start(area[:, 8192:8192 + 4 * 384], A["constants"][:, C_BAND:C_END]).then_inc(mix_in, 16)
                    if self.norms == 5:
                        load_mem()


                def pool(self):
                    enter()

                def query(self, l):
                    enter()

                def cross(self, l):
                    enter()
                    store_ada(2 * l)

                def project(self, w, gated=False):
                    enter()
                    if gated:
                        self.load_ada(1)

                def load_ada(self, part):
                    pool.dma_start(ada_parts, ada_dram[6 * part:6 * part + 6].rearrange("c p n -> p c n")).then_inc(ada_in, 16)
                    spread(ada_bias, A["ada_b_2"][0][3072 * part:3072 * part + 3072], ada_in)

                def nsa_inputs(self):
                    enter()
                    pool.dma_start(pos_rows, A["nsa_cmp_pos"][0].rearrange("v (j a) d -> (v j) (a d)", a=2))\
                        .then_inc(pos_in, 16)
                    for to, v in ((w2k[:, :, 0:64], 0), (w2k[:, :, 64:128], 0), (w2v, 1)):
                        pool.dma_start(to, A["nsa_cmp_w2"][0, v].rearrange("(h p) n -> p h n", p=P)).then_inc(w2_in, 16)

                def nsa_compress(self):
                    enter()

                def nsa_attend(self):
                    enter()
                    store_ada(1)

                def ada(self, part):
                    enter()
                    pool.memset(ones, 1.0).then_inc(ones_made, 1)
                    pool.wait_ge(ones_made, part + 1)
                    if part == 0:
                        pool.wait_ge(dist_made, 2)
                        pool.dma_start(dist_dram, dist_rows).then_inc(dist_out, 16)

                def gate_inputs(self):
                    enter()
                    for t in range(T):
                        spread(bgate[:, t, :], A["gate_b_2"][0], gate_b_in)

                def diff_inputs(self):
                    enter()
                    pool.wait_ge(dist_out, 16)
                    load_skew(0)
                    spread(subln, A["diff_subln_2"][0], row_in)
                    enter()

                def diff(self):
                    enter()
                    load_skew(1)

                def diff_norm(self):
                    enter()
                    pool.wait_ge(summed, 1)
                    power(ss8, rstd8, 8, P).then_inc(powered, 1)

                def sparse_inputs(self):
                    enter()
                    spread(kv_gain, A["dsa_kv_norm_2"][0], row_in)
                    pool.dma_start(w_uv, A["dsa_w_uv_2"][0].rearrange("h r e -> r h e")).then_inc(row_in, 16)
                    enter()

                def latent(self):
                    enter()
                    load_skew(2)
                    pool.wait_ge(summed, 3)
                    power(ss8[:, 0:2], rstd8[:, 0:2], 2, P).then_inc(powered, 1)

                def select(self):
                    enter()

                def dsa(self, t):
                    enter()

                def moba(self):
                    enter()
                    enter()

                def merge(self):
                    enter()

                def mlp(self):
                    enter()

                def end(self):
                    pass

            load_mem()
            load_gain(0)
            pool.memset(minus_half8, -0.5).then_inc(pool_step, 1)
            pool.wait_ge(pool_step, steps.next())
            pool.memset(minus_half, -0.5).then_inc(pool_step, 1)
            pool.memset(zero.bitcast(F32)[:, :], 0.0).then_inc(zero_made, 1)
            pool.wait_ge(pool_step, steps.next())
            program(Pool())

        @block.scalar
        def _(act):
            stages, steps, uses, done = Count(), Count(), Uses(), Uses()
            c_sq, c_norm, c_turned, c_ffn, c_turn = Count(), Count(), Count(), Count(), Count()
            units, groups = Count(), Count()

            def enter(updates_x=False):
                if stages.n:
                    act.wait_ge(stage_dve, stages.n)
                    act.wait_ge(stage_act, stages.n)
                stages.next()
                fresh[0] = updates_x
                x_updates.next(int(updates_x))

            fresh, x_updates = [False], Count()

            def leave():
                act.drain().then_inc(stage_act, 1)

            arrived = [0] * SLOTS

            def split(slot, n=None, doubled=False, transfers=2):
                if n is None:
                    n = uses.next(slot)
                if type(n) is int:
                    arrived[slot] += 16 * transfers
                    act.wait_ge(landed[slot], arrived[slot])
                else:
                    act.wait_ge(landed[slot], 32 * n + (arrived[slot] - 32 * uses.n[slot]))
                if not (type(n) is int and n == 1):
                    act.wait_ge(consumed[slot], n - 1)
                to, of = twice(slot) if doubled else (whi[:, slot, :], raw[:, slot, :])
                act.activation(to, of, ACT.Copy).then_inc(hi_ready[slot], 1)

            def chunks(count, evac, doubled=(), transfers=()):
                for c in range(count):
                    if c + 1 == count and count % 2 == 0:
                        next_slabs()
                    if c + 1 < count:
                        for s in range(2):
                            split(2 * ((c + 1) % 2) + s, doubled=c + 1 in doubled,
                                  transfers=dict(transfers).get(c + 1, 2))
                    pair = 2 * (c % 2)
                    done.next(pair)
                    act.wait_ge(consumed[pair + 1], done.next(pair + 1))
                    evac(c, 4 * (chunk_no.n % 2)).then_inc(act_evac, 1)
                    chunk_no.next()

            chunk_no = Count()

            def next_slabs():
                for s in range(2):
                    split(s)

            def turned(banks):
                for b in range(banks):
                    act.wait_ge(rows_turned, c_turned.next())
                    t, k = b // 2, 4 * (b % 2)
                    act.activation(aT_hi[:, k:k + 4, t * P:(t + 1) * P],
                                   ps[:, b, :].rearrange("p (k n) -> p k n", k=4), ACT.Copy).then_inc(aT_hi_made, 1)

            class Act:
                def norm(self, m, mem=False, turn=True, keep=False, modulate=False):
                    early = fresh[0]
                    if early:
                        act.wait_ge(x_half, x_updates.n)
                        act.wait_ge(stage_act, stages.n)
                        stages.next()
                        fresh[0] = False
                    else:
                        enter()
                    if mem:
                        act.wait_ge(mem_in, 32 * (m // 5 + 1))
                    if m == 1:
                        act.wait_ge(x_in, 16 * T)
                    src = xn if mem else x
                    for t in range(T):
                        if early and t:
                            act.wait_ge(stage_dve, stages.n - 1)
                        if mem and t:
                            act.wait_ge(squared, c_sq.n)
                        junk = hs[:, :, :].rearrange("p t n -> p (t n)") if mem else xn[:, t, :]
                        act.activation(junk, src[:, t, :], ACT.Square, accum_out=ssq[:, t:t + 1])\
                           .then_inc(squared, 1)
                        c_sq.next()
                    if m == 0:
                        next_slabs()
                    if turn:
                        turned(4)
                    leave()

                def kv(self, l):
                    enter()

                    def evac(c, b):
                        if c < 2:
                            return act.activation(kT[:, 4 * c:4 * c + 2, :], ps[:, b, :], ACT.Copy)
                        return act.activation(vm[:, 0, 512 * (c - 2):512 * (c - 1)], ps[:, b, :], ACT.Copy)
                    chunks(4, evac)
                    leave()

                def ffn(self, w_in, w_out):
                    enter(updates_x=True)
                    rounds = FF // HI
                    ub, db, fb = list(uses.n), list(done.n), c_ffn.n

                    def first_half(i):
                        act.wait_ge(gate_half, fb + i + 1)
                        act.activation(hs[:, 0, 0:HI], ps[:, 4, 0:HI], ACT.Silu).then_inc(silu_made, 1)
                        act.wait_ge(consumed[1], db[1] + i + 1)
                        act.activation(hs[:, 1, 0:HI], ps[:, 5, 0:HI], ACT.Silu).then_inc(silu_made, 1)

                    def second_half(i):
                        act.wait_ge(hid_turned, fb + i + 1)
                        act.activation(hT_hi[:, 0:2, :], ps[:, 6, :], ACT.Copy).then_inc(hT_hi_made, 1)

                    with act.Fori(0, rounds - 1) as i:
                        split(0, ub[0] + i + 1)
                        first_half(i)
                        split(1, ub[1] + i + 1)
                        second_half(i)
                        split(2, ub[2] + i + 1)
                    for s in range(3):
                        uses.n[s] += rounds - 1
                        arrived[s] += 32 * (rounds - 1)
                    split(3)
                    first_half(rounds - 1)
                    second_half(rounds - 1)
                    for s in range(4):
                        done.n[s] += (rounds, rounds, rounds - 1, 1)[s]
                    next_slabs()
                    c_ffn.next(rounds)
                    leave()

                def pool(self):
                    enter(updates_x=True)
                    act.wait_ge(cond_in, 16)
                    act.activation(condT, condT, ACT.Silu).then_inc(cond_made, 1)
                    split(2)
                    for b in range(4):
                        act.wait_ge(rows_turned, c_turned.next())
                        act.activation(aT_hi[:, 2 * b:2 * b + 2, :], ps[:, b, :], ACT.Copy).then_inc(aT_hi_made, 1)
                    done.next(2)
                    leave()

                def query(self, l):
                    enter()
                    chunks(2, lambda c, b: act.activation(qT[:, 4 * c:4 * c + 2, :], ps[:, b, :], ACT.Copy,
                                                          scale=1.0 / 16))
                    leave()

                def cross(self, l):
                    enter()

                    def exps(u):
                        U = units.n + u
                        act.wait_ge(maxed, U + 1)
                        if u >= 3:
                            act.wait_ge(probs_turned, U - 2)
                        act.activation(Pb[u % 3][:, 0:S], ps[:, u % 3, 0:S], ACT.Exp, bias=nmx[:, 2 * (u % 3):2 * (u % 3) + 1],
                                       accum_out=den[:, 2 * (u % 3):2 * (u % 3) + 1]).then_inc(exped, 1)

                    def keep(u):
                        h, t = u // 2, u % 2
                        act.wait_ge(probs_turned, units.n + u + 1)
                        if h >= 2:
                            act.wait_ge(pv_done, groups.n + h - 1)
                        act.activation(PTc(h)[:, :, t * P:(t + 1) * P],
                                       ps[:, 3 + u % 2, 0:S].rearrange("p (m q) -> p m q", m=2),
                                       ACT.Copy).then_inc(probs_kept, 1)

                    def out_hi(h):
                        act.wait_ge(pv_done, groups.n + h + 1)
                        act.activation(aT_hi[:, 2 * h:2 * h + 2, :], ps[:, 6 + h % 2, :], ACT.Copy).then_inc(o_hi, 1)

                    exps(0)
                    exps(1)
                    for u in range(8):
                        keep(u)
                        if u + 2 < 8:
                            exps(u + 2)
                        if u % 2 == 0 and u:
                            out_hi(u // 2 - 1)
                    out_hi(3)
                    units.next(8)
                    groups.next(4)
                    leave()

                def project(self, w, gated=False):
                    enter(updates_x=True)
                    if gated:
                        turned(4)
                    chunks(2, lambda c, b: act.drain())
                    leave()

                def nsa_inputs(self):
                    enter()

                    def evac(c, b):
                        if c < 2:
                            return act.activation(qT[:, 4 * c:4 * c + 2, :], ps[:, b, :], ACT.Copy, scale=0.125)
                        if c < 4:
                            return act.drain()
                        if c < 6:
                            return act.activation((ksT, kwT)[c - 4][:, 0:2, :], ps[:, b, :], ACT.Copy)
                        if c == 6:
                            return act.activation(area[:, 8192:9216].rearrange("p (v t n) -> p t v n", v=2, t=2)[:, 0],
                                                  ps[:, b, :].rearrange("p (v n) -> p v n", v=2), ACT.Copy)
                        return act.activation(gates[:, :, :], ps[:, b, 0:96].rearrange("p (t n) -> p t n", t=2),
                                              ACT.Sigmoid)
                    chunks(8, evac, range(2, 6))
                    leave()

                def nsa_compress(self):
                    enter()
                    act.activation(aTf_hi[:, 0:1920], area[:, 9344:11264], ACT.Copy).then_inc(aT_hi_made, 1)
                    split(2)
                    split(3)
                    for v in range(2):
                        done.next(2 * v)
                        act.wait_ge(consumed[2 * v + 1], done.next(2 * v + 1))
                        act.activation(hidT[:, v], ps[:, v, 0:128].rearrange("p (h n) -> p h n", h=2)[:, :, 0:60],
                                       ACT.Gelu_apprx_tanh).then_inc(gelu_made, 1)
                    act.wait_ge(cmp_made, 1)
                    act.activation(kcT, ps[:, 2, 0:60], ACT.Copy)
                    act.wait_ge(cmp_made, 2)
                    act.activation(vcmp, ps[0:15, 3, 0:256], ACT.Copy)
                    leave()
                    next_slabs()

                def nsa_attend(self):
                    enter()

                    def exps(u):
                        U, t, b = units.n + u, u // 4 % 2, 2 * (u % 3)
                        w = P * (t + 1)
                        act.wait_ge(maxed, U + 1)
                        for j, (c, n) in enumerate(((0, w), (w, w))):
                            last = act.activation(Pb[u % 3][:, c:c + n], Pb[u % 3][:, c:c + n], ACT.Exp, scale=-1.0,
                                                  bias=nmx[:, b + j:b + j + 1], accum_out=den[:, b + j:b + j + 1])
                        last.then_inc(exped, 1)

                    def keep(u):
                        gi, t, r = u // 4, u // 4 % 2, u % 4
                        act.wait_ge(probs_turned, units.n + u + 1)
                        if gi >= 2:
                            act.wait_ge(pv_done, groups.n + gi - 1)
                        act.activation(nsaP[gi % 2][:, r, 0:2 * P * (t + 1)], ps[:, 3 + u % 2, 0:2 * P * (t + 1)], ACT.Copy)\
                           .then_inc(probs_kept, 1)

                    def out_hi(gi):
                        g, t = gi // 2, gi % 2
                        act.wait_ge(pv_done, groups.n + gi + 1)
                        act.activation(aT_hi[:, 2 * g:2 * g + 2, t * P:(t + 1) * P],
                                       ps[:, 6 + gi % 2, 0:256].rearrange("p (j q) -> p j q", j=2), ACT.Copy).then_inc(o_hi, 1)

                    def keep_cmp(gi):
                        act.wait_ge(cmp_turned, gi + 1)
                        if gi >= 2:
                            act.wait_ge(pv_done, groups.n + gi - 1)
                        act.activation(nsaPc[gi % 2][0:N_CMP], ps[0:N_CMP, 5, :].rearrange("p (r q) -> p r q", r=4), ACT.Copy)\
                           .then_inc(cmp_kept, 1)

                    act.wait_ge(cmp_centred, 1)
                    act.activation(cmpP, cmpP, ACT.Exp).then_inc(cmp_exped, 1)
                    exps(0)
                    exps(1)
                    for u in range(32):
                        keep(u)
                        if u + 2 < 32:
                            exps(u + 2)
                        if u % 4 == 1:
                            keep_cmp(u // 4)
                        if u % 4 == 0 and u:
                            out_hi(u // 4 - 1)
                    out_hi(7)
                    units.next(32)
                    groups.next(8)
                    leave()

                def ada(self, part):
                    enter()
                    if part == 0:
                        act.wait_ge(dist_made, 1)
                        act.activation(dist_rows, ps[0:12, 6, 0:384], ACT.Copy).then_inc(dist_made, 1)
                        act.wait_ge(lam_summed, 2)
                        act.activation(lam2, lam2, ACT.Exp).then_inc(dist_made, 1)
                    leave()

                def gate_inputs(self):
                    enter()

                    def evac(c, b):
                        act.wait_ge(dve_evac, chunk_no.n + 1)
                        return act.activation(bgate[:, :, 512 * c:512 * c + 512], bgate[:, :, 512 * c:512 * c + 512], ACT.Sigmoid)
                    chunks(6, evac)
                    leave()

                def keep_bias(self, b):
                    act.wait_ge(bias_turned, b + 1)
                    act.activation(bias[:, 0:2, :], ps[:, 4, :].rearrange("p (h k) -> p h k", h=2), ACT.Copy)

                def diff_inputs(self):
                    enter()

                    def evac(c, b):
                        if c < 2:
                            return act.activation((aqT, akT)[c][:, 0:2, :], ps[:, b, :], ACT.Copy, scale=(0.125, 1.0)[c])
                        return act.activation(av[:, 0, :], ps[:, b, :], ACT.Copy)
                    chunks(3, evac)
                    leave()
                    next_slabs()
                    enter()
                    self.keep_bias(0)
                    leave()

                def exps(self, u, segs, U):
                    b = 2 * (u % 2)
                    act.wait_ge(maxed, U + 1)
                    for j, (c, n) in enumerate(segs):
                        last = act.activation(Pb[u % 2][:, c:c + n], Pb[u % 2][:, c:c + n], ACT.Exp, scale=-1.0,
                                              bias=nmx[:, b + j:b + j + 1], accum_out=den[:, b + j:b + j + 1])
                    last.then_inc(exped, 1)

                def diff(self):
                    enter()

                    def exps(u):
                        w = P * (u % 2 + 1)
                        self.exps(u, ((0, w), (w, w)), units.n + u)

                    def keep(u):
                        w = P * (u % 2 + 1)
                        act.wait_ge(probs_turned, units.n + u + 1)
                        if u >= 2:
                            act.wait_ge(pv_done, groups.n + u - 1)
                        act.activation(PTu[u % 2][:, 0:w], ps[:, 4 + u % 2, 0:w], ACT.Copy).then_inc(probs_kept, 1)

                    def out(u):
                        act.wait_ge(pv_done, groups.n + u + 1)
                        act.activation(oA[:, u % 2, u // 2, :], ps[:, 6 + u % 2, 0:P], ACT.Copy).then_inc(o_hi, 1)

                    exps(0)
                    for u in range(8):
                        if u + 1 < 8:
                            exps(u + 1)
                        keep(u)
                        if u:
                            out(u - 1)
                    out(7)
                    units.next(8)
                    groups.next(8)
                    leave()

                def diff_norm(self):
                    enter()
                    act.wait_ge(branch_done, 1)
                    act.activation(yT[:, 0:2, :], ps[:, 0, :], ACT.Copy)
                    leave()

                def sparse_inputs(self):
                    enter()

                    def evac(c, b):
                        if c == 0:
                            return act.activation(bqT[:, 0:2, :], ps[:, b, :], ACT.Copy, scale=P ** -0.5)
                        if c == 1:
                            act.activation(kvn, ps[:, b, 0:256].rearrange("p (t n) -> p t n", t=T), ACT.Copy)
                            return act.activation(iqT, ps[:, b + 1, :].rearrange("p (k n) -> p k n", k=2), ACT.Copy)
                        if c == 2:
                            return act.activation(cqT, ps[:, b, :].rearrange("p (k n) -> p k n", k=2), ACT.Copy, scale=0.125)
                        return act.activation(cv, ps[:, b:b + 2, 0:256], ACT.Copy)
                    chunks(4, evac, transfers=[(1, 5)])
                    leave()
                    enter()
                    self.keep_bias(1)
                    leave()

                def latent(self):
                    enter()
                    for t in range(T):
                        act.activation(score_part[:, P * t:P * t + P], kvn[:, t, :], ACT.Square, accum_out=ss8[:, t:t + 1]).then_inc(summed, 1)
                    leave()

                def select(self):
                    enter()
                    act.wait_ge(index_scored, 2)
                    for j in range(4):
                        for t in range(T):
                            o = ps[:, 4 * t + j, 0:2 * P * (t + 1)]
                            last = act.activation(o, o, ACT.Relu)
                        last.then_inc(relu_made, 1)
                    leave()

                def dsa(self, t):
                    enter()
                    w = P * (t + 1)

                    def keep(u):
                        act.wait_ge(probs_turned, units.n + u + 1)
                        act.activation(PTd[:, u, 0:t + 1, :], ps[:, 2 + u % 2, 0:w].rearrange("p (m q) -> p m q", q=P), ACT.Copy)\
                           .then_inc(probs_kept, 1)

                    self.exps(0, ((0, w),), units.n)
                    for u in range(4):
                        if u + 1 < 4:
                            self.exps(u + 1, ((0, w),), units.n + u + 1)
                        keep(u)
                    act.wait_ge(pv_done, groups.n + 1)
                    act.activation(o_lat, ps[:, 4, :], ACT.Copy).then_inc(lat_kept, 1)
                    units.next(4)
                    groups.next(1)
                    act.wait_ge(branch_done, 2 + t)
                    act.activation(yT[:, 4:6, t * P:(t + 1) * P], ps[:, 5, 0:256].rearrange("p (k q) -> p k q", k=2), ACT.Copy)
                    leave()

                def moba(self):
                    enter()
                    self.keep_bias(2)
                    leave()
                    enter()

                    def exps(u):
                        self.exps(u, ((0, P * (u % 2 + 1)),), units.n + u)

                    def keep(u):
                        w = P * (u % 2 + 1)
                        act.wait_ge(probs_turned, units.n + u + 1)
                        if u >= 2:
                            act.wait_ge(pv_done, groups.n + u - 1)
                        act.activation(PTu[u % 2][:, 0:w], ps[:, 2 + u % 2, 0:w], ACT.Copy).then_inc(probs_kept, 1)

                    exps(0)
                    for u in range(8):
                        if u + 1 < 8:
                            exps(u + 1)
                        keep(u)
                    units.next(8)
                    groups.next(8)
                    act.wait_ge(pv_done, groups.n)
                    act.activation(yT[:, 6:8, :], ps[:, 4, :].rearrange("p (k q) -> p k q", k=2), ACT.Copy)
                    leave()

                def merge(self):
                    enter()
                    act.activation(aTf_hi, yTf, ACT.Copy).then_inc(aT_hi_made, 1)
                    split(2)
                    split(3)
                    for s in range(4):
                        done.next(s)
                    leave()
                    next_slabs()

                def mlp(self):
                    enter(updates_x=True)
                    rounds = 8
                    ub, db, fb = list(uses.n), list(done.n), c_ffn.n
                    with act.Fori(0, rounds - 1) as i:
                        split(0, ub[0] + i + 1)
                        self.mlp_round(i, db, fb)
                        split(1, ub[1] + i + 1)
                        self.mlp_turned(i, fb)
                        split(2, ub[2] + i + 1)
                        split(3, ub[3] + i + 1)
                    for s in range(4):
                        uses.n[s] += rounds - 1
                        arrived[s] += 32 * (rounds - 1)
                    self.mlp_round(rounds - 1, db, fb)
                    self.mlp_turned(rounds - 1, fb)
                    split(2)
                    split(3)
                    for s in range(4):
                        done.n[s] += rounds
                    leave()

                def mlp_round(self, i, db, fb):
                    act.wait_ge(gate_half, fb + i + 1)
                    act.activation(hs[:, 0, :], ps[:, 4, :], ACT.Relu).then_inc(silu_made, 1)
                    act.wait_ge(consumed[1], db[1] + i + 1)
                    act.activation(hs[:, 1, :], ps[:, 5, :], ACT.Relu).then_inc(silu_made, 1)

                def mlp_turned(self, i, fb):
                    act.wait_ge(hid_turned, fb + i + 1)
                    act.activation(hT_hi[:, :, :], ps[:, 6:8, :], ACT.Copy).then_inc(hT_hi_made, 1)

                def end(self):
                    pass

            program(Act())

        @block.vector
        def _(dve):
            stages, steps, uses, done = Count(), Count(), Uses(), Uses()
            c_norm, c_turned, c_ffn, c_turn = Count(), Count(), Count(), Count()
            units, groups, chunk_no = Count(), Count(), Count()

            def enter():
                if stages.n:
                    dve.wait_ge(stage_dve, stages.n)
                    dve.wait_ge(stage_act, stages.n)
                stages.next()

            def leave():
                dve.drain().then_inc(stage_dve, 1)

            def step(ins):
                ins.then_inc(dve_step, 1)
                dve.wait_ge(dve_step, steps.next())

            def split(slot, n=None, doubled=False):
                if n is None:
                    n = uses.next(slot)
                dve.wait_ge(hi_ready[slot], n)
                if doubled:
                    hi, of = twice(slot)
                    lo = wlo[:, slot, :].rearrange("p (g a n) -> p g a n", a=2, n=64)
                else:
                    hi, of, lo = whi[:, slot, :], raw[:, slot, :], wlo[:, slot, :]
                dve.tensor_tensor(lo, of, hi, ALU.subtract).then_inc(lo_ready[slot], 1)

            def chunks(count, evac, doubled=()):
                for c in range(count):
                    if c + 1 == count and count % 2 == 0:
                        next_slabs()
                    if c + 1 < count:
                        for s in range(2):
                            split(2 * ((c + 1) % 2) + s, doubled=c + 1 in doubled)
                    pair = 2 * (c % 2)
                    done.next(pair)
                    dve.wait_ge(consumed[pair + 1], done.next(pair + 1))
                    evac(c, 4 * (chunk_no.n % 2)).then_inc(dve_evac, 1)
                    chunk_no.next()

            def next_slabs():
                for s in range(2):
                    split(s)

            def lower(b, dst_hi, dst_lo, src):
                dve.wait_ge(aT_hi_made, c_turned.next())
                dve.tensor_tensor(dst_lo, src, dst_hi, ALU.subtract).then_inc(aT_made, 1)

            def ada_slab(turn, n):
                cs, buf = ada_turns[turn]
                c, s = cs[n // 2], n % 2
                if turn == 0 and n == 0:
                    dve.wait_ge(cond_made, 1)
                if s == 0 and c >= 2:
                    dve.wait_ge(ada_out[c % 2], 16 * (c // 2))
                dve.wait_ge(ada_landed[s], 32 * (c + 1))
                acc = ada_acc(c, buf)
                for r in range(4):
                    w, k = raw[:, 2 + s, 512 * r:512 * r + 512], 4 * s + r
                    if k == 0:
                        last = dve.tensor_scalar(acc, w, condT[:, 0:1], None, ALU.mult)
                    else:
                        last = dve.scalar_tensor_tensor(out=acc, in0=w, scalar=condT[:, k:k + 1], in1=acc,
                                                        op0=ALU.mult, op1=ALU.add)
                    if r < 3:
                        step(last)
                last.then_inc(ada_used[s], 1)
                dve.wait_ge(ada_used[s], c + 1)

            class Dve:
                def norm(self, m, mem=False, turn=True, keep=False, modulate=False):
                    enter()
                    dve.wait_ge(gain_in[m % 2], 16 * (m // 2 + 1))
                    src = xn if mem else x
                    to = x if keep else xn
                    if modulate:
                        step(dve.scalar_tensor_tensor(out=gain[:, m % 2, :], in0=mod[:, 1024:2048], scalar=1.0,
                                                      in1=gain[:, m % 2, :], op0=ALU.add, op1=ALU.mult))
                    for t in range(T):
                        dve.wait_ge(rstd_made, 2 * m + t + 1)
                        last = dve.scalar_tensor_tensor(out=to[:, t, :], in0=src[:, t, :], scalar=rstd[:, t:t + 1],
                                                        in1=gain[:, m % 2, :], op0=ALU.mult, op1=ALU.mult)
                        if modulate:
                            step(last)
                            last = dve.tensor_tensor(xn[:, t, :], xn[:, t, :], mod[:, 0:1024], ALU.add)
                        last.then_inc(rows_normed, 1)
                    if m == 0:
                        next_slabs()
                    if turn:
                        for b in range(4):
                            t, k = b // 2, 4 * (b % 2)
                            at = (slice(None), slice(k, k + 4), slice(t * P, (t + 1) * P))
                            lower(b, aT_hi[at], aT_lo[at], ps[:, b, :].rearrange("p (k n) -> p k n", k=4))
                    leave()

                def kv(self, l):
                    enter()

                    def evac(c, b):
                        if c < 2:
                            return dve.tensor_copy(kT[:, 4 * c + 2:4 * c + 4, :], ps[:, b + 1, :])
                        return dve.tensor_copy(vm[:, 1, 512 * (c - 2):512 * (c - 1)], ps[:, b + 1, :])
                    chunks(4, evac)
                    leave()

                def ffn(self, w_in, w_out):
                    enter()
                    rounds = FF // HI
                    ub, db, fb = list(uses.n), list(done.n), c_ffn.n

                    def first_half(i):
                        for t in range(T):
                            dve.wait_ge(silu_made, 2 * (fb + i) + t + 1)
                            dve.tensor_tensor(hs[:, t, HI:2 * HI], hs[:, t, 0:HI], ps[:, 4 + t, HI:2 * HI], ALU.mult)\
                               .then_inc(hid_made, 1)

                    def second_half(i):
                        dve.wait_ge(hT_hi_made, fb + i + 1)
                        dve.tensor_tensor(hT_lo[:, 0:2, :], ps[:, 6, :].rearrange("p (k n) -> p k n", k=2),
                                          hT_hi[:, 0:2, :], ALU.subtract).then_inc(hT_made, 1)

                    with dve.Fori(0, rounds - 1) as i:
                        split(0, ub[0] + i + 1)
                        first_half(i)
                        split(1, ub[1] + i + 1)
                        second_half(i)
                        split(2, ub[2] + i + 1)
                    for s in range(3):
                        uses.n[s] += rounds - 1
                    split(3)
                    first_half(rounds - 1)
                    second_half(rounds - 1)
                    for s in range(4):
                        done.n[s] += (rounds, rounds, rounds - 1, 1)[s]
                    next_slabs()
                    c_ffn.next(rounds)
                    dve.wait_ge(consumed[3], done.n[3])
                    for b in range(4):
                        t, c = b // 2, b % 2
                        at = x[:, t, 512 * c:512 * c + 512]
                        last = dve.scalar_tensor_tensor(out=at, in0=ps[:, b, :], scalar=0.5, in1=at,
                                                        op0=ALU.mult, op1=ALU.add)
                        if b == 1:
                            last.then_inc(x_half, 1)
                    leave()

                def pool(self):
                    enter()
                    split(2)
                    for b in range(4):
                        at = (slice(None), slice(2 * b, 2 * b + 2), slice(None))
                        lower(b, aT_hi[at], aT_lo[at], ps[:, b, :].rearrange("p (k n) -> p k n", k=2))
                    dve.wait_ge(consumed[2], done.next(2))
                    dve.wait_ge(mix_in, 48)
                    for b in range(4):
                        t, c = b // 2, slice(512 * (b % 2), 512 * (b % 2) + 512)
                        step(dve.tensor_tensor(xn[:, t, c], ps[:, 4 + b, :], pool_b[:, c], ALU.add))
                        step(dve.tensor_tensor(xn[:, t, c], xn[:, t, c], pool_s[:, c], ALU.mult))
                        last = dve.tensor_tensor(x[:, t, c], x[:, t, c], xn[:, t, c], ALU.add)
                        if b == 1:
                            last.then_inc(x_half, 1)
                    leave()

                def query(self, l):
                    enter()
                    chunks(2, lambda c, b: dve.tensor_scalar(qT[:, 4 * c + 2:4 * c + 4, :],
                                                             ps[:, b + 1, :].rearrange("p (k n) -> p k n", k=2), 1.0 / 16, None, ALU.mult))
                    leave()

                def cross(self, l):
                    enter()

                    def top(u):
                        U = units.n + u
                        dve.wait_ge(scored, U + 1)
                        if u >= 3:
                            dve.wait_ge(exped, U - 2)
                        dve.tensor_reduce(nmx[:, 2 * (u % 3):2 * (u % 3) + 1], ps[:, u % 3, 0:S], AX.X, ALU.max, negate=True)\
                           .then_inc(maxed, 1)

                    def weigh(u):
                        b = 2 * (u % 3)
                        dve.wait_ge(exped, units.n + u + 1)
                        step(dve.reciprocal(rec[:, b:b + 1], den[:, b:b + 1]))
                        dve.tensor_scalar(Pb[u % 3][:, 0:S], Pb[u % 3][:, 0:S], rec[:, b:b + 1], None, ALU.mult)\
                           .then_inc(weighed, 1)

                    def out_lo(h):
                        dve.wait_ge(o_hi, groups.n + h + 1)
                        dve.tensor_tensor(aT_lo[:, 2 * h:2 * h + 2, :], ps[:, 6 + h % 2, :].rearrange("p (k n) -> p k n", k=2),
                                          aT_hi[:, 2 * h:2 * h + 2, :], ALU.subtract).then_inc(o_kept, 1)

                    top(0)
                    top(1)
                    for u in range(8):
                        weigh(u)
                        if u + 2 < 8:
                            top(u + 2)
                        ada_slab(2 * l, u)
                        if u % 2 == 0 and u:
                            out_lo(u // 2 - 1)
                    out_lo(3)
                    units.next(8)
                    groups.next(4)
                    leave()

                def project(self, w, gated=False):
                    enter()
                    if gated:
                        for b in range(4):
                            t, k = b // 2, 4 * (b % 2)
                            at = (slice(None), slice(k, k + 4), slice(t * P, (t + 1) * P))
                            lower(b, aT_hi[at], aT_lo[at], ps[:, b, :].rearrange("p (k n) -> p k n", k=4))

                    def evac(c, b):
                        for t in range(T):
                            at = x[:, t, 512 * c:512 * c + 512]
                            if gated:
                                y = hs[:, t, :]
                                step(dve.tensor_tensor(y, ps[:, b + t, :], out_gate[:, 512 * c:512 * c + 512], ALU.mult))
                                last = dve.tensor_tensor(at, at, y, ALU.add)
                            else:
                                last = dve.tensor_tensor(at, at, ps[:, b + t, :], ALU.add)
                            if t == 0 and c == 1:
                                last.then_inc(x_half, 1)
                        return last
                    chunks(2, evac)
                    leave()

                def nsa_inputs(self):
                    enter()

                    def evac(c, b):
                        if c < 2:
                            return dve.tensor_scalar(qT[:, 4 * c + 2:4 * c + 4, :],
                                                     ps[:, b + 1, :].rearrange("p (k n) -> p k n", k=2), 0.125, None, ALU.mult)
                        if c in (2, 3):
                            v = c - 2
                            if c == 2:
                                step(dve.tensor_copy(posT, ps[:, b + 2, 0:32]))
                            for g in range(4):
                                for a in range(2):
                                    half = slice(64 * a, 64 * a + 64)
                                    src = ps[half, b + g // 2, 256 * (g % 2) + a:256 * (g % 2) + a + 255]
                                    win = bass.AP(src.tensor, src.offset, [list(src.ap[0]), [2, 16], [16, N_CMP]])
                                    last = dve.tensor_tensor(blk[half, v, :, g, :], win,
                                                             posT[half, 16 * v:16 * v + 16].unsqueeze(2)
                                                             .to_broadcast([64, 16, N_CMP]), ALU.add)
                            return last
                        if c in (4, 5):
                            return dve.tensor_copy((ksT, kwT)[c - 4][:, 2:4, :], ps[:, b + 1, :])
                        if c == 6:
                            return dve.tensor_copy(area[:, 8192:9216].rearrange("p (v t n) -> p t v n", v=2, t=2)[:, 1],
                                                   ps[:, b + 1, :].rearrange("p (v n) -> p v n", v=2))
                        return dve.drain()
                    chunks(8, evac, range(2, 6))
                    leave()

                def nsa_compress(self):
                    enter()
                    dve.tensor_scalar(gates[:, 0, 0:48:3], gates[:, 0, 0:48:3], cst[:, C_VIS:C_VIS + 1], None, ALU.mult)
                    dve.wait_ge(aT_hi_made, c_turned.next())
                    dve.tensor_tensor(aTf_lo[:, 0:1920], area[:, 9344:11264], aTf_hi[:, 0:1920], ALU.subtract)\
                       .then_inc(aT_made, 1)
                    split(2)
                    split(3)
                    for v in range(2):
                        done.next(2 * v)
                        done.next(2 * v + 1)
                    leave()
                    next_slabs()

                def nsa_attend(self):
                    enter()

                    def top(u):
                        U, t, b = units.n + u, u // 4 % 2, 2 * (u % 3)
                        w = P * (t + 1)
                        dve.wait_ge(scored, U + 1)
                        if u >= 3:
                            dve.wait_ge(probs_turned, U - 2)
                        for j in range(2):
                            last = dve.tensor_tensor_reduce(Pb[u % 3][:, w * j:w * j + w], ps[:, u % 3, w * j:w * j + w],
                                                            cst[:, C_CAUSAL + S - w:C_CAUSAL + S], -1.0, BIG, ALU.add, ALU.min,
                                                            nmx[:, b + j:b + j + 1])
                        last.then_inc(maxed, 1)

                    def weigh(u):
                        t, b = u // 4 % 2, 2 * (u % 3)
                        w, h = P * (t + 1), 4 * (u // 8) + u % 4
                        dve.wait_ge(exped, units.n + u + 1)
                        step(dve.reciprocal(rec[:, b:b + 2], den[:, b:b + 2]))
                        for j in range(2):
                            p = Pb[u % 3][:, w * j:w * j + w]
                            last = dve.tensor_scalar(p, p, rec[:, b + j:b + j + 1], gates[:, t, 3 * h + 1 + j:3 * h + 2 + j],
                                                     ALU.mult, ALU.mult)
                        last.then_inc(weighed, 1)

                    def out_lo(gi):
                        g, t = gi // 2, gi % 2
                        dve.wait_ge(o_hi, groups.n + gi + 1)
                        at = (slice(None), slice(2 * g, 2 * g + 2), slice(t * P, (t + 1) * P))
                        dve.tensor_tensor(aT_lo[at], ps[:, 6 + gi % 2, 0:256].rearrange("p (j q) -> p j q", j=2),
                                          aT_hi[at], ALU.subtract).then_inc(o_kept, 1)

                    mask = cst[:, C_CMP:C_CMP + 32].rearrange("p (t n) -> p t n", t=T)[:, :, 0:N_CMP]
                    every = [P, T, NSA_H, N_CMP]
                    dve.wait_ge(cmp_scored, 2)
                    for par in range(2):
                        scores = ps[:, 6 + par, 0:256].rearrange("p (t h n) -> p t h n", t=T, h=NSA_H // 2)[:, :, :, 0:N_CMP]
                        step(dve.tensor_tensor(cmpP[:, :, par::2, :], scores,
                                               mask.unsqueeze(2).to_broadcast([P, T, NSA_H // 2, N_CMP]), ALU.add))
                    step(dve.tensor_reduce(cmp_max, cmpP, AX.X, ALU.max))
                    dve.tensor_tensor(cmpP, cmpP, cmp_max.unsqueeze(3).to_broadcast(every), ALU.subtract).then_inc(cmp_centred, 1)
                    top(0)
                    top(1)
                    dve.wait_ge(cmp_exped, 1)
                    step(dve.tensor_reduce(cmp_rec, cmpP, AX.X, ALU.add))
                    step(dve.reciprocal(cmp_rec, cmp_rec))
                    step(dve.tensor_tensor(cmp_rec, cmp_rec, gates[:, :, 0::3], ALU.mult))
                    dve.tensor_tensor(cmpP, cmpP, cmp_rec.unsqueeze(3).to_broadcast(every), ALU.mult).then_inc(cmp_weighed, 1)
                    for u in range(32):
                        weigh(u)
                        if u + 2 < 32:
                            top(u + 2)
                        if u % 4 == 3:
                            ada_slab(1, u // 4)
                        if u % 4 == 0 and u:
                            out_lo(u // 4 - 1)
                    out_lo(7)
                    units.next(32)
                    groups.next(8)
                    leave()

                def ada(self, part):
                    enter()
                    if part == 0:
                        dve.wait_ge(hot_in, 48)
                        for j in range(2):
                            dve.tensor_tensor_reduce(lam_prod[:, 64 * j:64 * j + 64], lam_in[:, P * j:P * j + 64],
                                                     lam_in[:, P * j + 64:P * j + P], 1.0, 0.0, ALU.mult, ALU.add,
                                                     lam2[:, j:j + 1]).then_inc(lam_summed, 1)
                        dve.wait_ge(dist_made, 3)
                        step(dve.tensor_tensor(neg_lam, lam2[:, 1:2], lam2[:, 0:1], ALU.subtract))
                        step(dve.tensor_scalar(neg_lam, neg_lam, -LAM_INIT, None, ALU.add))
                    for c in range(6):
                        dve.wait_ge(ada_summed, 6 * part + c + 1)
                        dve.tensor_tensor(mod[:, 512 * c:512 * c + 512], ps[:, c, :], ada_bias[:, 512 * c:512 * c + 512], ALU.add)
                    leave()

                def gate_inputs(self):
                    enter()
                    dve.wait_ge(gate_b_in, 32)

                    def evac(c, b):
                        at = bgate[:, :, 512 * c:512 * c + 512]
                        return dve.tensor_tensor(at, at, ps[:, b:b + 2, :], ALU.add)
                    chunks(6, evac)
                    leave()

                def keep_bias(self, b):
                    dve.wait_ge(bias_turned, b + 1)
                    dve.tensor_copy(bias[:, 2:4, :], ps[:, 5, :].rearrange("p (h k) -> p h k", h=2))

                def diff_inputs(self):
                    enter()

                    def evac(c, b):
                        if c == 0:
                            return dve.tensor_scalar(aqT[:, 2:4, :], ps[:, b + 1, :].rearrange("p (k n) -> p k n", k=2), 0.125, None, ALU.mult)
                        if c == 1:
                            return dve.tensor_copy(akT[:, 2:4, :], ps[:, b + 1, :])
                        return dve.tensor_copy(av[:, 1, :], ps[:, b + 1, :])
                    chunks(3, evac)
                    leave()
                    next_slabs()
                    enter()
                    self.keep_bias(0)
                    dve.wait_ge(row_in, 16)
                    dve.tensor_scalar(subln, subln, 1.0 - LAM_INIT, None, ALU.mult)
                    leave()

                def diff(self):
                    enter()

                    def top(u):
                        U, h, t, b = units.n + u, u // 2, u % 2, 2 * (u % 2)
                        w = P * (t + 1)
                        dve.wait_ge(scored, U + 1)
                        if u >= 2:
                            dve.wait_ge(probs_turned, U - 1)
                        for j in range(2):
                            last = dve.tensor_tensor_reduce(Pb[u % 2][:, w * j:w * j + w], ps[:, 2 * (u % 2) + j, 0:w],
                                                            bias[:, h, S - w:S], -1.0, BIG, ALU.add, ALU.min,
                                                            nmx[:, b + j:b + j + 1])
                        last.then_inc(maxed, 1)

                    def weigh(u):
                        b, w = 2 * (u % 2), P * (u % 2 + 1)
                        p0, p1 = Pb[u % 2][:, 0:w], Pb[u % 2][:, w:2 * w]
                        dve.wait_ge(exped, units.n + u + 1)
                        step(dve.reciprocal(rec[:, b:b + 2], den[:, b:b + 2]))
                        step(dve.tensor_tensor(rec[:, b + 1:b + 2], rec[:, b + 1:b + 2], neg_lam, ALU.mult))
                        step(dve.tensor_scalar(p1, p1, rec[:, b + 1:b + 2], None, ALU.mult))
                        dve.scalar_tensor_tensor(out=p0, in0=p0, scalar=rec[:, b:b + 1], in1=p1, op0=ALU.mult, op1=ALU.add)\
                           .then_inc(weighed, 1)

                    top(0)
                    for u in range(8):
                        if u + 1 < 8:
                            top(u + 1)
                        weigh(u)
                    units.next(8)
                    groups.next(8)
                    leave()

                def diff_norm(self):
                    enter()
                    sq = xnf[:, 0:1024]
                    step(dve.tensor_tensor(sq, hsf, hsf, ALU.mult))
                    dve.tensor_reduce(ss8, sq.rearrange("p (u e) -> p u e", u=8), AX.X, ALU.add).then_inc(summed, 1)
                    dve.wait_ge(powered, 1)
                    o8 = hsf.rearrange("p (u e) -> p u e", u=8)
                    step(dve.tensor_tensor(o8, o8, rstd8.unsqueeze(2).to_broadcast([P, 8, P]), ALU.mult))
                    dve.tensor_tensor(o8, o8, subln.unsqueeze(1).to_broadcast([P, 8, P]), ALU.mult).then_inc(branch_kept, 1)
                    dve.wait_ge(branch_done, 1)
                    dve.tensor_copy(yT[:, 2:4, :], ps[:, 1, :].rearrange("p (k n) -> p k n", k=2))
                    leave()

                def sparse_inputs(self):
                    enter()

                    def evac(c, b):
                        if c == 0:
                            return dve.tensor_scalar(bqT[:, 2:4, :], ps[:, b + 1, :].rearrange("p (k n) -> p k n", k=2), P ** -0.5, None, ALU.mult)
                        if c == 1:
                            return dve.tensor_copy(ikT, ps[:, b + 2, 0:256])
                        if c == 2:
                            return dve.tensor_copy(ckT, ps[:, b + 1, :].rearrange("p (k n) -> p k n", k=2))
                        dve.wait_ge(act_evac, chunk_no.n + 1)
                        return dve.tensor_scalar(iw, ps[:, b:b + 2, 256:264], 0.0625, None, ALU.mult)
                    chunks(4, evac)
                    leave()
                    enter()
                    self.keep_bias(1)
                    leave()

                def latent(self):
                    enter()
                    dve.wait_ge(row_in, 48)
                    dve.wait_ge(powered, 2)
                    for t in range(T):
                        last = dve.scalar_tensor_tensor(out=kvn[:, t, :], in0=kvn[:, t, :], scalar=rstd8[:, t:t + 1],
                                                        in1=kv_gain, op0=ALU.mult, op1=ALU.mult)
                    last.then_inc(branch_kept, 1)
                    dve.wait_ge(branch_kept, 3)
                    dve.tensor_copy(kvT, ps[:, 0, 0:S])
                    leave()

                def select(self):
                    enter()
                    base = steps.n
                    at = [0]

                    def each(make):
                        for t in range(T):
                            if at[0] >= T:
                                dve.wait_ge(dve_step, base + at[0] - 1)
                            make(t, P * (t + 1)).then_inc(dve_step, 1)
                            at[0] += 1

                    dve.wait_ge(index_scored, 2)
                    for h in (0, 4, 1, 5, 2, 6, 3, 7):
                        if h < 4:
                            dve.wait_ge(relu_made, h + 1)

                        def weigh(t, w):
                            src = ps[:, 4 * t + h % 4, w * (h // 4):w * (h // 4) + w]
                            wk = work[t]
                            if h == 0:
                                return dve.tensor_scalar(wk, src, iw[:, t, h:h + 1], None, ALU.mult)
                            return dve.scalar_tensor_tensor(out=wk, in0=src, scalar=iw[:, t, h:h + 1], in1=wk,
                                                            op0=ALU.mult, op1=ALU.add)
                        each(weigh)
                    each(lambda t, w: dve.tensor_tensor(work[t], work[t], cst[:, C_CAUSAL + S - w:C_CAUSAL + S], ALU.add))
                    for _ in range(TOPK // 8):
                        each(lambda t, w: dve.max(top8[t], work[t]))
                        each(lambda t, w: dve.match_replace(work[t], top8[t], work[t], -BIG))
                    each(lambda t, w: dve.tensor_scalar(sel[t], work[t], -2.0e38, NEG, ALU.is_gt, ALU.mult))
                    steps.next(at[0])
                    leave()

                def dsa(self, t):
                    enter()
                    w = P * (t + 1)

                    def top(u):
                        U, b = units.n + u, 2 * (u % 2)
                        pb = Pb[u % 2][:, 0:w]
                        if u >= 2:
                            dve.wait_ge(probs_turned, U - 1)
                        step(dve.tensor_tensor(pb, bias[:, u, S - w:S], sel[t], ALU.add))
                        dve.wait_ge(scored, U + 1)
                        dve.tensor_tensor_reduce(pb, ps[:, u % 2, 0:w], pb, -1.0, BIG, ALU.add, ALU.min,
                                                 nmx[:, b:b + 1]).then_inc(maxed, 1)

                    top(0)
                    for u in range(4):
                        if u + 1 < 4:
                            top(u + 1)
                        self.weigh_one(u, w)
                    units.next(4)
                    groups.next(1)
                    leave()

                def weigh_one(self, u, w):
                    b = 2 * (u % 2)
                    dve.wait_ge(exped, units.n + u + 1)
                    step(dve.reciprocal(rec[:, b:b + 1], den[:, b:b + 1]))
                    dve.tensor_scalar(Pb[u % 2][:, 0:w], Pb[u % 2][:, 0:w], rec[:, b:b + 1], None, ALU.mult)\
                       .then_inc(weighed, 1)

                def moba(self):
                    enter()
                    self.keep_bias(2)
                    leave()
                    enter()

                    def top(u):
                        U, h, b, w = units.n + u, u // 2, 2 * (u % 2), P * (u % 2 + 1)
                        dve.wait_ge(scored, U + 1)
                        if u >= 2:
                            dve.wait_ge(probs_turned, U - 1)
                        dve.tensor_tensor_reduce(Pb[u % 2][:, 0:w], ps[:, u % 2, 0:w], bias[:, h, S - w:S], -1.0, BIG,
                                                 ALU.add, ALU.min, nmx[:, b:b + 1]).then_inc(maxed, 1)

                    top(0)
                    for u in range(8):
                        if u + 1 < 8:
                            top(u + 1)
                        self.weigh_one(u, P * (u % 2 + 1))
                    units.next(8)
                    groups.next(8)
                    leave()

                def merge(self):
                    enter()
                    dve.wait_ge(aT_hi_made, c_turned.next())
                    dve.tensor_tensor(aTf_lo, yTf, aTf_hi, ALU.subtract).then_inc(aT_made, 1)
                    split(2)
                    split(3)
                    for s in range(4):
                        done.next(s)
                    for br in range(3):
                        dve.wait_ge(branch_done, 4 + br)
                        for t in range(T):
                            g = bgate[:, t, 1024 * br:1024 * br + 1024].rearrange("p (c n) -> p c n", c=2)
                            y = ps[:, 4 * (br % 2) + 2 * t:4 * (br % 2) + 2 * t + 2, :]
                            m = xn[:, t, :].rearrange("p (c n) -> p c n", c=2)
                            if br == 0:
                                last = dve.tensor_tensor(m, y, g, ALU.mult)
                                continue
                            last = dve.tensor_tensor(g, y, g, ALU.mult)
                        last.then_inc(branch_kept, 1)
                        if br:
                            dve.wait_ge(branch_kept, 3 + br + 1)
                            for t in range(T):
                                g = bgate[:, t, 1024 * br:1024 * br + 1024]
                                last = dve.tensor_tensor(xn[:, t, :], xn[:, t, :], g, ALU.add)
                            if br == 1:
                                step(last)
                    leave()
                    next_slabs()

                def mlp(self):
                    enter()
                    rounds = 8
                    ub, db, fb = list(uses.n), list(done.n), c_ffn.n
                    with dve.Fori(0, rounds - 1) as i:
                        split(0, ub[0] + i + 1)
                        self.mlp_round(i, fb)
                        split(1, ub[1] + i + 1)
                        self.mlp_turned(i, fb)
                        split(2, ub[2] + i + 1)
                        split(3, ub[3] + i + 1)
                    for s in range(4):
                        uses.n[s] += rounds - 1
                    self.mlp_round(rounds - 1, fb)
                    self.mlp_turned(rounds - 1, fb)
                    split(2)
                    split(3)
                    for s in range(4):
                        done.n[s] += rounds
                    dve.wait_ge(consumed[3], done.n[3])
                    for t in range(T):
                        y = xn[:, t, :]
                        step(dve.tensor_tensor(y.rearrange("p (c n) -> p c n", c=2), ps[:, 2 * t:2 * t + 2, :],
                                               out_gate.rearrange("p (c n) -> p c n", c=2), ALU.mult))
                        last = dve.tensor_tensor(x[:, t, :], x[:, t, :], y, ALU.add)
                        if t == 0:
                            last.then_inc(x_half, 1)
                    leave()

                def mlp_round(self, i, fb):
                    for t in range(T):
                        dve.wait_ge(silu_made, 2 * (fb + i) + t + 1)
                        dve.tensor_tensor(hs[:, t, :], hs[:, t, :], ps[:, 4 + t, :], ALU.mult).then_inc(hid_made, 1)

                def mlp_turned(self, i, fb):
                    dve.wait_ge(hT_hi_made, fb + i + 1)
                    dve.tensor_tensor(hT_lo[:, :, :], ps[:, 6:8, :].rearrange("p b (k n) -> p (b k) n", k=2), hT_hi[:, :, :],
                                      ALU.subtract).then_inc(hT_made, 1)

                def end(self):
                    pass

            program(Dve())

        @block.tensor
        def _(pe):
            stages, uses = Count(), Uses()
            c_norm, c_turned, c_ffn = Count(), Count(), Count()
            units, groups, chunk_no = Count(), Count(), Count()

            def enter():
                if stages.n:
                    pe.wait_ge(stage_act, stages.n)
                    pe.wait_ge(stage_dve, stages.n)
                stages.next()

            def parts(o, lh, ll, rh, rl, start, stop):
                pe.matmul(o, lh, rl, start=start, stop=False, skip_group_check=True)
                pe.matmul(o, ll, rh, start=False, stop=False, skip_group_check=True)
                return pe.matmul(o, lh, rh, start=False, stop=stop, skip_group_check=True)

            def chunk(pair, n, outs):
                before = chunk_no.next() - 2
                if before >= 0:
                    pe.wait_ge(act_evac, before)
                    pe.wait_ge(dve_evac, before)
                wh = [whi[:, pair + s, 0:4 * n].rearrange("p (k n) -> p k n", k=4) for s in range(2)]
                wl = [wlo[:, pair + s, 0:4 * n].rearrange("p (k n) -> p k n", k=4) for s in range(2)]
                for s in range(2):
                    pe.wait_ge(lo_ready[pair + s], uses.next(pair + s))
                for j, (kind, *a, o) in enumerate(outs):
                    for k in range(KD):
                        s, r = k // 4, k % 4
                        if kind == "N":
                            t, c, m = a
                            tok = slice(t * P, (t + 1) * P)
                            last = parts(o, aT_hi[:, k, tok], aT_lo[:, k, tok], wh[s][:, r, c:c + m],
                                         wl[s][:, r, c:c + m], k == 0, k == KD - 1)
                        else:
                            c, m = a
                            last = parts(o, wh[s][:, r, c:c + m], wl[s][:, r, c:c + m], aT_hi[:, k, :],
                                         aT_lo[:, k, :], k == 0, k == KD - 1)
                        if j == len(outs) - 1 and r == 3:
                            last.then_inc(consumed[pair + s], 1)

            def rows(b):
                return [("N", t, 0, 512, ps[:, b + t, :]) for t in range(T)]

            def turned(b):
                return [("T", 128 * j, 128, ps[:, b + j // 2, 256 * (j % 2):256 * (j % 2) + 256]) for j in range(4)]

            def bank():
                return 4 * (chunk_no.n % 2)

            def turn_rows(normed=None):
                for b in range(4):
                    t = b // 2
                    if normed is not None and b % 2 == 0:
                        pe.wait_ge(rows_normed, normed + t + 1)
                    for k in range(4):
                        f = 4 * (b % 2) + k
                        last = pe.transpose(ps[:, b, P * k:P * k + P], xn[:, t, P * f:P * f + P], ident)
                    last.then_inc(rows_turned, 1)

            class Pe:
                def norm(self, m, mem=False, turn=True, keep=False, modulate=False):
                    enter()
                    if turn:
                        turn_rows(2 * m)
                        pe.wait_ge(aT_made, c_turned.next(4))

                def kv(self, l):
                    enter()
                    for c in range(4):
                        chunk(2 * (c % 2), 512, turned(bank()) if c < 2 else rows(bank()))

                def ffn(self, w_in, w_out):
                    enter()
                    rounds = FF // HI
                    ub, fb = list(uses.n), c_ffn.n
                    for b in range(4):
                        pe.matmul(ps[:, b, :], zero[:, 0:P], zero[:, :], start=True, stop=False, skip_group_check=True)

                    def up(i):
                        for s in range(2):
                            pe.wait_ge(lo_ready[s], ub[s] + i + 1)
                            h, lw = (w[:, s, :].rearrange("p (k n) -> p k n", k=4) for w in (whi, wlo))
                            for t in range(T):
                                tok = slice(t * P, (t + 1) * P)
                                for r in range(4):
                                    k = 4 * s + r
                                    last = parts(ps[:, 4 + t, :], aT_hi[:, k, tok], aT_lo[:, k, tok], h[:, r, :],
                                                 lw[:, r, :], k == 0, k == KD - 1)
                                if s == 1 and t == 0:
                                    last.then_inc(gate_half, 1)
                            last.then_inc(consumed[s], 1)

                    def turn(i):
                        for t in range(T):
                            pe.wait_ge(hid_made, 2 * (fb + i) + t + 1)
                            for k in range(2):
                                last = pe.transpose(ps[:, 6, S * k + P * t:S * k + P * t + P],
                                                    hs[:, t, HI + P * k:HI + P * k + P], ident)
                        last.then_inc(hid_turned, 1)

                    def down(i, stop, slot=2):
                        pe.wait_ge(lo_ready[slot], ub[2] + i + 1 if slot == 2 else uses.next(3))
                        pe.wait_ge(hT_made, fb + i + 1)
                        h, lw = (w[:, slot, :].rearrange("p (k c n) -> p k c n", k=2, c=2) for w in (whi, wlo))
                        for t in range(T):
                            tok = slice(t * P, (t + 1) * P)
                            for c in range(2):
                                for k in range(2):
                                    last = parts(ps[:, 2 * t + c, :], hT_hi[:, k, tok], hT_lo[:, k, tok],
                                                 h[:, k, c, :], lw[:, k, c, :], False, stop and k == 1)
                        last.then_inc(consumed[slot], 1)

                    up(0)
                    turn(0)
                    with pe.Fori(1, rounds) as i:
                        up(i)
                        down(i - 1, False)
                        turn(i)
                    down(rounds - 1, True, 3)
                    for s in range(3):
                        uses.n[s] += rounds - s // 2
                    c_ffn.next(rounds)

                def pool(self):
                    enter()
                    pe.wait_ge(mix_in, 48)
                    for b in range(4):
                        for j in range(2):
                            k = 2 * b + j
                            o = ps[:, b, S * j:S * j + S]
                            pe.matmul(o, xn[:, 0, P * k:P * k + P], band[:, k // 2, 0:S], start=True, stop=False)
                            last = pe.matmul(o[:, P:S], xn[:, 1, P * k:P * k + P], band[:, k // 2, S:S + P],
                                             start=False, stop=True)
                        last.then_inc(rows_turned, 1)
                    pe.wait_ge(aT_made, c_turned.next(4))
                    pe.wait_ge(lo_ready[2], uses.next(2))
                    h, lw = (w[:, 2, :].rearrange("p (k n) -> p k n", n=256) for w in (whi, wlo))
                    for t in range(T):
                        tok = slice(t * P, (t + 1) * P)
                        for g in range(4):
                            o = ps[:, 4 + 2 * t + g // 2, 256 * (g % 2):256 * (g % 2) + 256]
                            for k in range(2 * g, 2 * g + 2):
                                last = parts(o, aT_hi[:, k, tok], aT_lo[:, k, tok], h[:, k, :], lw[:, k, :],
                                             k % 2 == 0, k % 2 == 1)
                    last.then_inc(consumed[2], 1)

                def query(self, l):
                    enter()
                    for c in range(2):
                        chunk(2 * c, 512, turned(bank()))

                def cross(self, l):
                    enter()

                    def score(u):
                        h, t = u // 2, u % 2
                        if u >= 3:
                            pe.wait_ge(exped, units.n + u - 2)
                        for j in range(2):
                            last = pe.matmul(ps[:, u % 3, 0:S], qT[:, 2 * h + j, t * P:(t + 1) * P], kT[:, 2 * h + j, :],
                                             start=j == 0, stop=j == 1)
                        last.then_inc(scored, 1)

                    def turn(u):
                        U = units.n + u
                        pe.wait_ge(weighed, U + 1)
                        if u >= 2:
                            pe.wait_ge(probs_kept, U - 1)
                        for m in range(2):
                            last = pe.transpose(ps[:, 3 + u % 2, P * m:P * m + P], Pb[u % 3][:, P * m:P * m + P], ident)
                        last.then_inc(probs_turned, 1)

                    def values(h):
                        pe.wait_ge(probs_kept, units.n + 2 * h + 2)
                        if h >= 2:
                            pe.wait_ge(o_kept, groups.n + h - 1)
                        for j in range(2):
                            for m in range(2):
                                last = pe.matmul(ps[:, 6 + h % 2, S * j:S * j + S],
                                                 vm[:, m, 256 * h + P * j:256 * h + P * j + P], PTc(h)[:, m, :],
                                                 start=m == 0, stop=m == 1)
                        last.then_inc(pv_done, 1)

                    score(0)
                    score(1)
                    for u in range(8):
                        if u + 2 < 8:
                            score(u + 2)
                        turn(u)
                        if u % 2 == 0 and u:
                            values(u // 2 - 1)
                    values(3)
                    units.next(8)
                    groups.next(4)

                def project(self, w, gated=False):
                    enter()
                    if gated:
                        turn_rows()
                        pe.wait_ge(aT_made, c_turned.next(4))
                    for c in range(2):
                        chunk(2 * c, 512, rows(bank()))

                def nsa_inputs(self):
                    enter()

                    for c in range(6):
                        b = bank()
                        if c == 2:
                            pe.wait_ge(pos_in, 16)
                            pe.wait_ge(dve_evac, chunk_no.n - 1)
                            pe.transpose(ps[:, b + 2, 0:32], pos_rows, ident[0:32, 0:32])
                        chunk(2 * (c % 2), 512, turned(b))
                    chunk(0, 512, rows(bank()))
                    b = bank()
                    chunk(2, 48, [("N", t, 0, 48, ps[:, b, 48 * t:48 * t + 48]) for t in range(T)])

                def nsa_compress(self):
                    enter()
                    pe.wait_ge(aT_made, c_turned.next())
                    for v in range(2):
                        for s in range(2):
                            pe.wait_ge(lo_ready[2 * v + s], uses.next(2 * v + s))
                        for h in range(2):
                            for j in range(16):
                                s = 2 * v + j // 8
                                c = 256 * (j % 8) + P * h
                                r = slice(960 * v + 60 * j, 960 * v + 60 * j + 60)
                                last = parts(ps[:, v, 64 * h:64 * h + 60], whi[:, s, c:c + P], wlo[:, s, c:c + P],
                                             aTf_hi[:, r], aTf_lo[:, r], j == 0, j == 15)
                                if h == 1 and j % 8 == 7:
                                    last.then_inc(consumed[s], 1)
                    pe.wait_ge(w2_in, 48)
                    pe.wait_ge(gelu_made, 1)
                    for h in range(2):
                        last = pe.matmul(ps[:, 2, 0:60], w2k[:, h, :], hidT[:, 0, h, :], start=h == 0, stop=h == 1)
                    last.then_inc(cmp_made, 1)
                    pe.wait_ge(gelu_made, 2)
                    for g in range(4):
                        for h in range(2):
                            last = pe.matmul(ps[0:N_CMP, 3, 64 * g:64 * g + 64], hidT[:, 1, h, N_CMP * g:N_CMP * g + N_CMP],
                                             w2v[:, h, :], start=h == 0, stop=h == 1)
                    last.then_inc(cmp_made, 1)

                def nsa_attend(self):
                    enter()

                    def score(u):
                        g, t, r = u // 8, u // 4 % 2, u % 4
                        half, w = slice(64 * (r % 2), 64 * (r % 2) + 64), P * (t + 1)
                        if u >= 3:
                            pe.wait_ge(maxed, units.n + u - 2)
                        q = qT[half, 2 * g + r // 2, t * P:(t + 1) * P]
                        pe.matmul(ps[:, u % 3, 0:w], q, ksT[half, g, 0:w], start=True, stop=True)
                        pe.matmul(ps[:, u % 3, w:2 * w], q, kwT[half, g, 0:w], start=True, stop=True).then_inc(scored, 1)

                    def turn(u):
                        U, t = units.n + u, u // 4 % 2
                        pe.wait_ge(weighed, U + 1)
                        if u >= 2:
                            pe.wait_ge(probs_kept, U - 1)
                        for m in range(2 * (t + 1)):
                            last = pe.transpose(ps[:, 3 + u % 2, P * m:P * m + P], Pb[u % 3][:, P * m:P * m + P], ident)
                        last.then_inc(probs_turned, 1)

                    def values(gi):
                        g, t = gi // 2, gi % 2
                        pe.wait_ge(probs_kept, units.n + 4 * gi + 4)
                        pe.wait_ge(cmp_kept, gi + 1)
                        if gi >= 2:
                            pe.wait_ge(o_kept, groups.n + gi - 1)
                        for par in range(2):
                            o = ps[64 * par:64 * par + 64, 6 + gi % 2, 0:256]
                            pe.matmul(o, vcmp[:, 64 * g:64 * g + 64], nsaPc[gi % 2][0:N_CMP, par::2, :], start=True, stop=False)
                            for j, v in enumerate((vs, vw)):
                                for m in range(t + 1):
                                    c = P * (j * (t + 1) + m)
                                    last = pe.matmul(o, v[:, m, 64 * g:64 * g + 64], nsaP[gi % 2][:, par::2, c:c + P],
                                                     start=False, stop=j == 1 and m == t)
                        last.then_inc(pv_done, 1)

                    def turn_cmp(gi):
                        g, t = gi // 2, gi % 2
                        pe.wait_ge(cmp_weighed, 1)
                        if gi:
                            pe.wait_ge(cmp_kept, gi)
                        for r in range(4):
                            last = pe.transpose(ps[0:N_CMP, 5, P * r:P * r + P], cmpP[:, t, 4 * g + r, :], ident)
                        last.then_inc(cmp_turned, 1)

                    for t in range(T):
                        for h in range(NSA_H):
                            half, c = slice(64 * (h % 2), 64 * (h % 2) + 64), 16 * (NSA_H // 2 * t + h // 2)
                            last = pe.matmul(ps[:, 6 + h % 2, c:c + N_CMP], qT[half, h // 2, t * P:(t + 1) * P],
                                             kcT[half, N_CMP * (h // 4):N_CMP * (h // 4) + N_CMP], start=True, stop=True)
                            if t == T - 1 and h >= NSA_H - 2:
                                last.then_inc(cmp_scored, 1)
                    score(0)
                    score(1)
                    for u in range(32):
                        if u + 2 < 32:
                            score(u + 2)
                        turn(u)
                        if u % 4 == 0:
                            turn_cmp(u // 4)
                        if u % 4 == 0 and u:
                            values(u // 4 - 1)
                    values(7)
                    units.next(32)
                    groups.next(8)

                def ada(self, part):
                    enter()
                    if part == 0:
                        pe.wait_ge(hot_in, 48)
                        pe.wait_ge(mask_row, 1)
                        pe.matmul(ps[0:12, 6, 0:384], rel, hot, start=True, stop=True).then_inc(dist_made, 1)
                    pe.wait_ge(ones_made, part + 1)
                    pe.wait_ge(ada_in, 32 * (part + 1))
                    for c in range(6):
                        pe.matmul(ps[:, c, :], ones, ada_parts[:, c, :], start=True, stop=True).then_inc(ada_summed, 1)

                def gate_inputs(self):
                    enter()
                    for c in range(6):
                        chunk(2 * (c % 2), 512, rows(bank()))

                def turn_bias(self, b):
                    enter()
                    pe.wait_ge(skew_in, 16 * (b + 1))
                    for j in range(2):
                        last = pe.matmul(ps[:, 4 + j, :], cst[:, C_FLIP:C_FLIP + P], skew[:, 2 * j:2 * j + 2, :],
                                         start=True, stop=True)
                    last.then_inc(bias_turned, 1)

                def diff_inputs(self):
                    enter()
                    for c in range(3):
                        chunk(2 * (c % 2), 512, turned(bank()) if c < 2 else rows(bank()))
                    self.turn_bias(0)

                def turn_probs(self, u, t, b, src=None):
                    U = units.n + u
                    pe.wait_ge(weighed, U + 1)
                    if u >= 2:
                        pe.wait_ge(probs_kept, U - 1)
                    for m in range(t + 1):
                        last = pe.transpose(ps[:, b, P * m:P * m + P], Pb[u % 2][:, P * m:P * m + P], ident)
                    last.then_inc(probs_turned, 1)

                def diff(self):
                    enter()

                    def score(u):
                        h, t = u // 2, u % 2
                        if u >= 2:
                            pe.wait_ge(maxed, units.n + u - 1)
                        for j in range(2):
                            half = slice(64 * j, 64 * j + 64)
                            last = pe.matmul(ps[:, 2 * (u % 2) + j, 0:P * (t + 1)], aqT[half, h, t * P:(t + 1) * P],
                                             akT[half, h, 0:P * (t + 1)], start=True, stop=True)
                        last.then_inc(scored, 1)

                    def values(u):
                        h, t = u // 2, u % 2
                        pe.wait_ge(probs_kept, units.n + u + 1)
                        if u >= 2:
                            pe.wait_ge(o_hi, 16 + u - 1)
                        for m in range(t + 1):
                            last = pe.matmul(ps[:, 6 + u % 2, 0:P], PTu[u % 2][:, P * m:P * m + P], av[:, m, P * h:P * h + P],
                                             start=m == 0, stop=m == t)
                        last.then_inc(pv_done, 1)

                    score(0)
                    for u in range(8):
                        if u + 1 < 8:
                            score(u + 1)
                        self.turn_probs(u, u % 2, 4 + u % 2)
                        if u:
                            values(u - 1)
                    values(7)
                    units.next(8)
                    groups.next(8)

                def diff_norm(self):
                    enter()
                    pe.wait_ge(branch_kept, 1)
                    for h in range(4):
                        for t in range(T):
                            c = S * (h % 2) + P * t
                            last = pe.transpose(ps[:, h // 2, c:c + P], oA[:, t, h, :], ident)
                    last.then_inc(branch_done, 1)

                def sparse_inputs(self):
                    enter()
                    chunk(0, 512, turned(bank()))
                    b = bank()
                    chunk(2, 512, [("N", t, 0, P, ps[:, b, P * t:P * t + P]) for t in range(T)]
                          + [("T", P + P * j, P, ps[:, b + 1, S * j:S * j + S]) for j in range(2)]
                          + [("T", 384, P, ps[:, b + 2, 0:S])])
                    chunk(0, 512, turned(bank()))
                    b = bank()
                    chunk(2, 264, [("N", t, 0, 264, ps[:, b + t, 0:264]) for t in range(T)])
                    self.turn_bias(1)

                def latent(self):
                    enter()
                    pe.wait_ge(branch_kept, 2)
                    for t in range(T):
                        last = pe.transpose(ps[:, 0, P * t:P * t + P], kvn[:, t, :], ident)
                    last.then_inc(branch_kept, 1)

                def select(self):
                    enter()
                    for t in range(T):
                        w = P * (t + 1)
                        for h in range(8):
                            r = slice(32 * (h % 4), 32 * (h % 4) + 32)
                            last = pe.matmul(ps[:, 4 * t + h % 4, w * (h // 4):w * (h // 4) + w],
                                             iqT[r, h // 4, t * P:(t + 1) * P], ikT[r, 0:w], start=True, stop=True,
                                             tile_position=(32 * (h % 4), 0))
                    pe.drain().then_inc(index_scored, 2)

                def dsa(self, t):
                    enter()
                    w = P * (t + 1)

                    def score(u):
                        if u >= 2:
                            pe.wait_ge(maxed, units.n + u - 1)
                        pe.matmul(ps[:, u % 2, 0:w], bqT[:, u, t * P:(t + 1) * P], kvT[:, 0:w], start=True, stop=True)\
                          .then_inc(scored, 1)

                    score(0)
                    for u in range(4):
                        if u + 1 < 4:
                            score(u + 1)
                        self.turn_probs(u, t, 2 + u % 2)
                    units.next(4)
                    pe.wait_ge(probs_kept, units.n)
                    for m in range(t + 1):
                        last = pe.matmul(ps[:, 4, :], kvn[:, m, :], PTd[:, :, m, :], start=m == 0, stop=m == t)
                    last.then_inc(pv_done, 1)
                    groups.next(1)
                    pe.wait_ge(lat_kept, t + 1)
                    for h in range(4):
                        last = pe.matmul(ps[64 * (h % 2):64 * (h % 2) + 64, 5, P * (h // 2):P * (h // 2) + P],
                                         w_uv[:, h, :], o_lat[:, P * h:P * h + P], start=True, stop=True)
                    last.then_inc(branch_done, 1)

                def moba(self):
                    self.turn_bias(2)
                    enter()

                    def score(u):
                        h, t = u // 2, u % 2
                        r, w = slice(64 * (h % 2), 64 * (h % 2) + 64), P * (t + 1)
                        if u >= 2:
                            pe.wait_ge(maxed, units.n + u - 1)
                        pe.matmul(ps[:, u % 2, 0:w], cqT[r, h // 2, t * P:(t + 1) * P], ckT[r, h // 2, 0:w],
                                  start=True, stop=True).then_inc(scored, 1)

                    def values(u):
                        h, t = u // 2, u % 2
                        pe.wait_ge(probs_kept, units.n + u + 1)
                        for m in range(t + 1):
                            c = S * (h // 2) + P * t
                            last = pe.matmul(ps[64 * (h % 2):64 * (h % 2) + 64, 4, c:c + P], cv[:, m, 64 * h:64 * h + 64],
                                             PTu[u % 2][:, P * m:P * m + P], start=m == 0, stop=m == t)
                        last.then_inc(pv_done, 1)

                    score(0)
                    for u in range(8):
                        if u + 1 < 8:
                            score(u + 1)
                        self.turn_probs(u, u % 2, 2 + u % 2)
                        if u:
                            values(u - 1)
                    values(7)
                    units.next(8)
                    groups.next(8)

                def merge(self):
                    enter()
                    pe.wait_ge(aT_made, c_turned.next())
                    for br in range(3):
                        if br == 2:
                            pe.wait_ge(branch_kept, 4)
                        for s in ((0, 1), (2,), (3,))[br]:
                            pe.wait_ge(lo_ready[s], uses.next(s))
                        for c in range(2):
                            for t in range(T):
                                o, tok = ps[:, 4 * (br % 2) + 2 * t + c, :], slice(t * P, (t + 1) * P)
                                n = (4, 2, 2)[br]
                                for k in range(n):
                                    kk = (0, 4, 6)[br] + k
                                    s, at = (c, 512 * k) if br == 0 else (br + 1, 1024 * k + 512 * c)
                                    last = parts(o, aT_hi[:, kk, tok], aT_lo[:, kk, tok], whi[:, s, at:at + 512],
                                                 wlo[:, s, at:at + 512], k == 0, k == n - 1)
                            if br == 0:
                                last.then_inc(consumed[c], 1)
                        if br:
                            last.then_inc(consumed[br + 1], 1)
                        pe.drain().then_inc(branch_done, 1)

                def mlp(self):
                    enter()
                    rounds = 8
                    ub, fb = list(uses.n), c_ffn.n
                    for b in range(4):
                        pe.matmul(ps[:, b, :], zero[:, 0:P], zero[:, :], start=True, stop=False, skip_group_check=True)

                    def up(i):
                        for s in range(2):
                            pe.wait_ge(lo_ready[s], ub[s] + i + 1)
                            h, lw = (w[:, s, :].rearrange("p (k n) -> p k n", k=4) for w in (whi, wlo))
                            for t in range(T):
                                tok = slice(t * P, (t + 1) * P)
                                for r in range(4):
                                    k = 4 * s + r
                                    last = parts(ps[:, 4 + t, :], aT_hi[:, k, tok], aT_lo[:, k, tok], h[:, r, :],
                                                 lw[:, r, :], k == 0, k == KD - 1)
                                if s == 1 and t == 0:
                                    last.then_inc(gate_half, 1)
                            last.then_inc(consumed[s], 1)

                    def turn(i):
                        for t in range(T):
                            pe.wait_ge(hid_made, 2 * (fb + i) + t + 1)
                            for k in range(4):
                                c = S * (k % 2) + P * t
                                last = pe.transpose(ps[:, 6 + k // 2, c:c + P], hs[:, t, P * k:P * k + P], ident)
                        last.then_inc(hid_turned, 1)

                    def down(i, stop):
                        pe.wait_ge(hT_made, fb + i + 1)
                        for s in (2, 3):
                            pe.wait_ge(lo_ready[s], ub[s] + i + 1)
                            h, lw = (w[:, s, :].rearrange("p (k c n) -> p k c n", k=2, c=2) for w in (whi, wlo))
                            for t in range(T):
                                tok = slice(t * P, (t + 1) * P)
                                for c in range(2):
                                    for k in range(2):
                                        kk = 2 * (s - 2) + k
                                        last = parts(ps[:, 2 * t + c, :], hT_hi[:, kk, tok], hT_lo[:, kk, tok],
                                                     h[:, k, c, :], lw[:, k, c, :], False, stop and kk == 3)
                            last.then_inc(consumed[s], 1)

                    up(0)
                    turn(0)
                    with pe.Fori(1, rounds) as i:
                        up(i)
                        down(i - 1, False)
                        turn(i)
                    down(rounds - 1, True)

                def end(self):
                    pass

            pe.wait_ge(const_in, 16)
            pe.wait_ge(zero_made, 1)
            program(Pe())


_NAMES = ["x", "mem", "ffn1_norm", "ffn1_w_in", "ffn1_w_out", "mix_norm", "xattn_norm", "mem_norm", "xattn_w_q",
          "xattn_w_kv", "xattn_w_o", "ffn2_norm", "ffn2_w_in", "ffn2_w_out", "pool_w", "pool_b", "pool_scale",
          "nsa_w_in", "nsa_cmp_pos", "nsa_cmp_w1", "nsa_cmp_w2", "nsa_w_o", "final_norm", "c_2", "rel_bias_2",
          "ada_w_2", "ada_b_2", "norm_mix_2", "w_in_2", "gate_b_2", "diff_lambda_2", "diff_subln_2",
          "dsa_kv_norm_2", "dsa_w_uv_2", "w_br_a_2", "w_br_b_2", "w_br_c_2", "w_o_2", "norm_mlp_2", "w_ff1_2",
          "w_ff2_2", "norm_final_2"]


def kernel(**inputs):
    import concourse.bacc as bacc
    from concourse.bass_utils import run_bass_kernel_spmd

    arrays = {n: np.ascontiguousarray(inputs[n]) for n in _NAMES}
    arrays["constants"] = constant_table()
    nc = bacc.Bacc("TRN2", target_bir_lowering=False, num_devices=1)
    A = {n: nc.dram_tensor(f"in_{n}", a.shape, F32, kind="ExternalInput").ap() for n, a in arrays.items()}
    out = nc.dram_tensor("out_x", (1, S, D), F32, kind="ExternalOutput").ap()
    build(nc, A, out)
    r = run_bass_kernel_spmd(nc, [{f"in_{n}": a for n, a in arrays.items()}], core_ids=[0])
    return r.results[0]["out_x"]
```

```python
import math
from contextlib import ExitStack

import numpy as np

import concourse.bass as bass
from concourse import mybir

F32 = mybir.dt.float32
F32R = mybir.dt.float32r
ALU = mybir.AluOpType
ACT = mybir.ActivationFunctionType
AX = mybir.AxisListType.X

P = 128
D = 1024
S = 256
T = S // P
KD = D // P
FF = 2816
HI = 256
EPS = 1e-6
NEG = -1e30
BIG = 3.0e38

SLOTS = 4
SLAB = 2048

NSA_H, NSA_G, NSA_R, NSA_DH = 16, 4, 4, 64
N_CMP, CMP_BLOCK, CMP_STRIDE, CMP_HID = 15, 32, 16, 256
COLS = dict(aq=0, ak=512, av=1024, bq=1536, bkv=2048, biq=2176, bik=2432, biw=2464,
            cq=2472, ck=2728, cv=2984, g=3240)
N_BUCKETS, MAX_DISTANCE = 32, 128
TOPK = 64
LAM_INIT = 0.8 - 0.6 * math.exp(-0.3 * 0)
POOL_WINDOWS = (2, 4, 8, 16)

C_IDENT, C_FLIP, C_CAUSAL, C_CMP, C_VIS = 0, 128, 256, 512, 544
C_HOT, C_BAND, C_END = 546, 930, 930 + 4 * 384


def constant_table():
    c = np.zeros((P, C_END), np.float32)
    i = np.arange(P)
    c[i, C_IDENT + i] = 1.0
    c[i, C_FLIP + 127 - i] = 1.0
    q, k = i[:, None], i[None, :]
    c[:, C_CAUSAL + 128:C_CAUSAL + 256] = np.where(k <= q, 0.0, NEG)
    n = np.arange(N_CMP)
    for t in range(T):
        end = n * CMP_STRIDE + CMP_BLOCK - 1
        c[:, C_CMP + 16 * t:C_CMP + 16 * t + N_CMP] = np.where(end[None, :] <= 128 * t + q, 0.0, NEG)
    c[:, C_VIS] = i >= CMP_BLOCK - 1
    dist = 255 - np.arange(384)
    half = N_BUCKETS // 2
    nf = np.maximum(dist, 1).astype(np.float32)
    large = half + (np.log(nf / np.float32(half)) / np.float32(math.log(MAX_DISTANCE / half))
                    * np.float32(N_BUCKETS - half)).astype(np.int32)
    bucket = np.where(dist < half, dist, np.minimum(large, N_BUCKETS - 1))
    bucket = np.where(dist < 0, N_BUCKETS, bucket)
    c[bucket, C_HOT + np.arange(384)] = 1.0
    for w, win in enumerate(POOL_WINDOWS):
        for tile, to in ((0, np.arange(S)), (1, np.arange(P, S))):
            frm = tile * P + i
            gap = to[None, :] - frm[:, None]
            cnt = np.minimum(to + 1, win).astype(np.float32)
            m = np.where((gap >= 0) & (gap < win), np.float32(1) / cnt[None, :], 0) - (gap == 0)
            at = C_BAND + 384 * w + 256 * tile
            c[:, at:at + len(to)] = m
    return c


class Uses:

    def __init__(self):
        self.n = [0] * SLOTS

    def next(self, slot):
        self.n[slot] += 1
        return self.n[slot]


class Count:

    def __init__(self):
        self.n = 0

    def next(self, k=1):
        self.n += k
        return self.n


def build(nc, A, out):
    ds = bass.ds
    with ExitStack() as ctx:
        def sb(name, shape, dt=F32):
            return ctx.enter_context(nc.sbuf_tensor(name, shape, dt))

        def sem(name):
            return ctx.enter_context(nc.semaphore(name))

        raw = sb("raw", [P, SLOTS, SLAB])
        whi = sb("whi", [P, SLOTS, SLAB], F32R)
        wlo = sb("wlo", [P, SLOTS, SLAB], F32R)
        x = sb("x", [P, T, D])
        xn = sb("xn", [P, T, D])
        aT_hi = sb("aT_hi", [P, KD, S], F32R)
        aT_lo = sb("aT_lo", [P, KD, S], F32R)
        hs = sb("hs", [P, T, 512])
        hT_hi = sb("hT_hi", [P, 4, S], F32R)
        hT_lo = sb("hT_lo", [P, 4, S], F32R)
        gain = sb("gain", [P, 2, D])
        cst = sb("cst", [P, C_HOT])
        area = sb("area", [P, 14000])
        zero = sb("zero", [P, 512], F32R)
        small = sb("small", [P, 64])
        ps = ctx.enter_context(nc.psum_tensor("ps", [P, 8, 512], F32))

        ident = cst[:, C_IDENT:C_IDENT + 128]
        ssq, rstd = small[:, 0:2], small[:, 4:6]
        minus_half = small[:, 6:8]
        nmx, den, rec = small[:, 8:14], small[:, 14:20], small[:, 20:26]

        landed = [sem(f"landed{s}") for s in range(SLOTS)]
        hi_ready = [sem(f"hi_ready{s}") for s in range(SLOTS)]
        lo_ready = [sem(f"lo_ready{s}") for s in range(SLOTS)]
        consumed = [sem(f"consumed{s}") for s in range(SLOTS)]
        stage_act, stage_dve = sem("stage_act"), sem("stage_dve")
        x_half = sem("x_half")
        x_in, mem_in, const_in, gain_in = sem("x_in"), [sem(f"mem_in{l}") for l in range(2)], sem("const_in"), [sem(f"gain_in{b}") for b in range(2)]
        zero_made, mix_in = sem("zero_made"), sem("mix_in")
        squared, rstd_made, rows_normed = sem("squared"), sem("rstd_made"), sem("rows_normed")
        rows_turned, aT_hi_made, aT_made = sem("rows_turned"), sem("aT_hi_made"), sem("aT_made")
        pool_step, dve_step = sem("pool_step"), sem("dve_step")
        act_evac, dve_evac = sem("act_evac"), sem("dve_evac")
        gate_half, silu_made, hid_made = sem("gate_half"), sem("silu_made"), sem("hid_made")
        hid_turned, hT_hi_made, hT_made = sem("hid_turned"), sem("hT_hi_made"), sem("hT_made")
        scored, maxed, exped, weighed = sem("scored"), sem("maxed"), sem("exped"), sem("weighed")
        probs_turned, probs_kept, pv_done = sem("probs_turned"), sem("probs_kept"), sem("pv_done")
        o_hi, o_kept = sem("o_hi"), sem("o_kept")
        cmp_scored, cmp_centred, cmp_exped, cmp_weighed = (sem(f"cmp_{n}") for n in ("scored", "centred", "exped", "weighed"))
        cmp_turned, cmp_kept = sem("cmp_turned"), sem("cmp_kept")
        cmp_hid_turned, cmp_hid_kept = sem("cmp_hid_turned"), sem("cmp_hid_kept")
        pos_in, w2_in, gelu_made, cmp_made = (sem(n) for n in ("pos_in", "w2_in", "gelu_made", "cmp_made"))
        cond_in, cond_made = sem("cond_in"), sem("cond_made")
        ada_landed, ada_used, ada_out = ([sem(f"{n}{b}") for b in range(2)] for n in ("ada_landed", "ada_used", "ada_out"))
        ada_in, ada_summed, ones_made = sem("ada_in"), sem("ada_summed"), sem("ones_made")
        hot_in, dist_made, dist_out, skew_in = (sem(n) for n in ("hot_in", "dist_made", "dist_out", "skew_in"))
        lam_summed, row_in, gate_b_in, bias_turned = (sem(n) for n in ("lam_summed", "row_in", "gate_b_in", "bias_turned"))
        summed, powered, index_scored, lat_kept = (sem(n) for n in ("summed", "powered", "index_scored", "lat_kept"))
        branch_done, branch_kept, mask_row = sem("branch_done"), sem("branch_kept"), sem("mask_row")
        stored, relu_made, index_read = sem("stored"), sem("relu_made"), sem("index_read")

        kT = area[:, 0:2048].rearrange("p (k s) -> p k s", k=KD)
        vm = area[:, 2048:4096].rearrange("p (t d) -> p t d", t=T)
        qT = area[:, 4096:6144].rearrange("p (k s) -> p k s", k=KD)
        PT = area[:, 6144:8192]
        pool_b = area[:, 6144:7168]
        pool_s = area[:, 7168:8192]
        band = area[:, 8192:8192 + 4 * 384].rearrange("p (w c) -> p w c", w=4)
        xnf = xn[:, :, :].rearrange("p t n -> p (t n)")
        hsf = hs[:, :, :].rearrange("p t n -> p (t n)")
        Pb = [xnf[:, 512 * b:512 * b + 512] for b in range(3)]
        ksT = area[:, 6144:7168].rearrange("p (g s) -> p g s", g=4)
        kwT = area[:, 7168:8192].rearrange("p (g s) -> p g s", g=4)
        vs = area[:, 8192:8704].rearrange("p (t n) -> p t n", t=T)
        vw = area[:, 8704:9216].rearrange("p (t n) -> p t n", t=T)
        gates = area[:, 9216:9312].rearrange("p (t n) -> p t n", t=T)
        blk = area[:, 9344:11264].rearrange("p (v j g n) -> p v j g n", v=2, j=16, g=4)
        nsaP = [area[:, 9344 + 2048 * b:11392 + 2048 * b].rearrange("p (r n) -> p r n", r=4) for b in range(2)]
        nsaPc = [a.rearrange("p (r n) -> p r n", r=4) for a in (area[:, 13440:13952], hsf[:, 512:1024])]
        cmpP = hsf[:, 0:512].rearrange("p (t h n) -> p t h n", t=T, h=NSA_H)[:, :, :, 0:N_CMP]
        cmp_max, cmp_rec = (xnf[:, c:c + 32].rearrange("p (t h) -> p t h", t=T) for c in (1888, 1920))
        pos_rows, posT = hsf[0:32, 0:128], hsf[:, 128:160]
        hidT = hsf[:, 160:400].rearrange("p (v h n) -> p v h n", v=2, h=2)
        cmp_pieces = ((0, 900 + P), (900 + P, 1920 - 900 - P))
        hid_rows = [xnf[0:4 * N_CMP, 256 * v:256 * v + 256] for v in range(2)]
        w2k = hsf[:, 400:656].rearrange("p (h n) -> p h n", h=2)
        w2v = hsf[:, 656:784].rearrange("p (h n) -> p h n", h=2)
        kcT = xnf[:, 1568:1628]
        vcmp = xnf[0:15, 1628:1884]
        aTf_hi = aT_hi[:, :, :].rearrange("p k s -> p (k s)")
        aTf_lo = aT_lo[:, :, :].rearrange("p k s -> p (k s)")

        yT = area[:, 0:2048].rearrange("p (k s) -> p k s", k=KD)
        yTf = area[:, 0:2048]
        mod = area[:, 0:3072]
        out_gate = area[:, 2048:3072]
        bgate = area[:, 3072:9216].rearrange("p (t n) -> p t n", t=T)
        aqT = area[:, 9216:10240].rearrange("p (k s) -> p k s", k=4)
        akT = area[:, 10240:11264].rearrange("p (k s) -> p k s", k=4)
        av = area[:, 11264:12288].rearrange("p (t n) -> p t n", t=T)
        bqT = area[:, 9216:10240].rearrange("p (k s) -> p k s", k=4)
        kvn = area[:, 10240:10496].rearrange("p (t n) -> p t n", t=T)
        iqT = area[:, 10496:11008].rearrange("p (k s) -> p k s", k=2)
        ikT = area[:, 11008:11264]
        cqT = area[:, 11264:11776].rearrange("p (k s) -> p k s", k=2)
        ckT = area[:, 11776:12288].rearrange("p (k s) -> p k s", k=2)
        cv = area[:, 12288:12800].rearrange("p (t n) -> p t n", t=T)
        iw = area[:, 12800:12816].rearrange("p (t n) -> p t n", t=T)
        bias = area[:, 12816:13840].rearrange("p (h k) -> p h k", h=4)
        kvT = area[:, 1536:1792]
        w_uv = area[:, 1792:2048].rearrange("p (h e) -> p h e", h=4)
        oA = hsf.rearrange("p (t h e) -> p t h e", t=T, h=4)
        PTd = hsf.rearrange("p (h m q) -> p h m q", h=4, m=2)
        skew = gain[:, 1, :].rearrange("p (h k) -> p h k", h=4)
        diff_PT = [area[:, 12288 + 256 * b:12544 + 256 * b] for b in range(2)]
        moba_PT = [xnf[:, 1536 + 256 * b:1792 + 256 * b] for b in range(2)]
        o_lat, score_part = xnf[:, 1056:1568], xnf[:, 1568:1824]
        sel = [yT[:, 4:5 + t, P * t:P * t + P] for t in range(T)]
        index_bank = (2, 3, 6, 7)
        work = [xnf[:, 1056:1184], xnf[:, 1184:1440]]
        top8 = [xnf[:, 1824:1832], xnf[:, 1960:1968]]
        subln, kv_gain = xnf[:, 1568:1696], xnf[:, 1832:1960]
        condT = area[:, 13952:13960]
        ada_turns = [(range(0, 2), 1), (range(2, 10), 1), (range(10, 12), 0)]

        def ada_acc(c, buf):
            return gain[:, buf, 512 * (c % 2):512 * (c % 2) + 512]

        ada_parts = area[:, 3072:6144].rearrange("p (c n) -> p c n", c=6)
        ada_bias = area[:, 6144:9216]
        ones = hsf[:, 0:P]
        hot, rel, dist_rows = area[0:33, 9216:9600], area[0:33, 9600:9612], area[0:12, 9728:10112]
        lam_in, lam_prod = area[:, 10240:10496], area[:, 10496:10624]
        neg_lam, lam2 = small[:, 60:61], small[:, 58:60]
        ss8, var8, rstd8, minus_half8 = (small[:, c:c + 8] for c in (26, 34, 42, 50))
        dist_dram = nc.dram_tensor("dist_rows", (12, 384), F32, kind="Internal").ap()
        ada_dram = nc.dram_tensor("ada_sums", (12, P, 512), F32, kind="Internal").ap()

        def twice(slot):
            return (whi[:, slot, :].rearrange("p (g a n) -> p g a n", a=2, n=64),
                    raw[:, slot, 0:SLAB // 2].rearrange("p (g n) -> p g n", n=64).unsqueeze(2)
                    .to_broadcast([P, SLAB // 128, 2, 64]))

        def PTc(h):
            return PT[:, 512 * (h % 2):512 * (h % 2) + 512].rearrange("p (m q) -> p m q", m=2)

        L = range(2)
        gains = []
        for l in L:
            gains += [A["mem_norm"][l], A["ffn1_norm"][l], A["mix_norm"][l], A["xattn_norm"][l], A["ffn2_norm"][l]]

        gains += [A["final_norm"], A["norm_mix_2"][0], A["norm_mlp_2"][0], A["norm_final_2"]]

        block = ctx.enter_context(nc.Block())

        def program(e):
            for l in L:
                e.norm(5 * l, mem=True)
                e.kv(l)
                e.norm(5 * l + 1)
                e.ffn(A["ffn1_w_in"][l], A["ffn1_w_out"][l])
                e.norm(5 * l + 2, turn=l > 0)
                if l == 0:
                    e.pool()
                else:
                    e.nsa_inputs()
                    e.nsa_compress()
                    e.nsa_attend()
                    e.project(A["nsa_w_o"][0])
                e.norm(5 * l + 3)
                e.query(l)
                e.cross(l)
                e.project(A["xattn_w_o"][l])
                e.norm(5 * l + 4)
                e.ffn(A["ffn2_w_in"][l], A["ffn2_w_out"][l])
            e.norm(10, turn=False, keep=True)
            e.ada(0)
            e.norm(11, modulate=True)
            e.wide_inputs()
            e.diff_bias()
            e.diff()
            e.sparse_inputs()
            e.latent()
            e.dsa(0)
            e.dsa(1)
            e.moba()
            e.merge()
            e.project(A["w_o_2"][0], gated=True)
            e.ada(1)
            e.norm(12, modulate=True)
            e.mlp()
            e.norm(13, turn=False, keep=True)

        @block.sync
        def _(sp):
            uses = Uses()
            stages = Count()

            def slab(slot, halves, n=None):
                if n is None:
                    n = uses.next(slot)
                if not (type(n) is int and n == 1):
                    sp.wait_ge(lo_ready[slot], n - 1)
                for dst, src in halves:
                    sp.dma_start(dst, src).then_inc(landed[slot], 16)

            def pieces(w, cols, n, pair):
                wv = w.rearrange("(k p) n -> p k n", p=P)
                for s in range(2):
                    d = raw[:, pair + s, 0:4 * n].rearrange("p (k n) -> p k n", k=4)
                    slab(pair + s, [(d[:, :, to:to + m], wv[:, 4 * s:4 * s + 4, c:c + m]) for to, c, m in cols])

            def chunk(w, c0, n, pair):
                wv = w.rearrange("(k p) n -> p k n", p=P)
                for s in range(2):
                    d = raw[:, pair + s, 0:4 * n].rearrange("p (k n) -> p k n", k=4)
                    slab(pair + s, [(d[:, 2 * j:2 * j + 2, :],
                                     wv[:, 4 * s + 2 * j:4 * s + 2 * j + 2, c0:c0 + n]) for j in range(2)])

            def ada_slabs(turn):
                w = A["ada_w_2"][0].rearrange("(k p) n -> p k n", p=P)
                for c in ada_turns[turn][0]:
                    for s in range(2):
                        if c == ada_turns[turn][0][0]:
                            sp.wait_ge(lo_ready[2 + s], uses.n[2 + s])
                        else:
                            sp.wait_ge(ada_used[s], c)
                        d = raw[:, 2 + s, :].rearrange("p (k n) -> p k n", k=4)
                        for j in range(2):
                            sp.dma_start(d[:, 2 * j:2 * j + 2, :], w[:, 4 * s + 2 * j:4 * s + 2 * j + 2, 512 * c:512 * c + 512])\
                              .then_inc(ada_landed[s], 16)
                for s in range(2):
                    ada_seen[s] = ada_turns[turn][0][-1] + 1

            ada_seen = [0, 0]

            class Sp:
                def norm(self, m, mem=False, turn=True, keep=False, modulate=False):
                    stages.next()

                def kv(self, l):
                    stages.next()
                    for c in range(4):
                        chunk(A["xattn_w_kv"][l], 512 * c, 512, 2 * (c % 2))
                        if l == 0 and c < T:
                            sp.dma_start(x[:, c, :], A["x"][0, c * P:(c + 1) * P, :]).then_inc(x_in, 16)

                def ffn(self, w_in, w_out):
                    stages.next()
                    rounds = FF // HI
                    wi = w_in.rearrange("(k p) n -> p k n", p=P)
                    wo = w_out.rearrange("(k p) n -> p k n", p=P)

                    def up(i, base):
                        for s in range(2):
                            d = raw[:, s, :].rearrange("p (k h n) -> p k h n", k=4, h=2)
                            slab(s, [(d[:, :, h, :], wi[:, 4 * s:4 * s + 4, ds(FF * h + i * HI, HI)])
                                     for h in range(2)], base[s] + i + 1)

                    def down(i, base, slot=2):
                        d = raw[:, slot, :].rearrange("p (k n) -> p k n", k=2)
                        slab(slot, [(d[:, j:j + 1, :], wo[:, ds(2 * i + j, 1), :]) for j in range(2)],
                             base[2] + i + 1 if slot == 2 else None)

                    base = list(uses.n)
                    up(0, base)
                    with sp.Fori(1, rounds) as i:
                        up(i, base)
                        down(i - 1, base)
                    down(rounds - 1, base, 3)
                    for s in range(3):
                        uses.n[s] += rounds - s // 2

                def pool(self):
                    stages.next()
                    chunk(A["xattn_w_q"][0], 0, 512, 0)
                    w = A["pool_w"][0].rearrange("g (k p) n -> p (g k) n", p=P)
                    d = raw[:, 2, :].rearrange("p (k n) -> p k n", n=256)
                    slab(2, [(d[:, 4 * j:4 * j + 4, :], w[:, 4 * j:4 * j + 4, :]) for j in range(2)])

                def query(self, l):
                    stages.next()
                    for c in range(1 if l == 0 else 0, 2):
                        chunk(A["xattn_w_q"][l], 512 * c, 512, 2 * c)

                def cross(self, l):
                    stages.next()
                    chunk(A["xattn_w_o"][l], 0, 512, 0)
                    ada_slabs(2 * l)

                def project(self, w, gated=False):
                    stages.next()
                    if not gated:
                        for s in range(2):
                            sp.wait_ge(ada_used[s], ada_seen[s])
                    for c in range(0 if gated else 1, 2):
                        chunk(w, 512 * c, 512, 2 * c)

                def nsa_inputs(self):
                    stages.next()
                    w = A["nsa_w_in"][0]
                    for c in range(2):
                        chunk(w, 512 * c, 512, 2 * c)
                    for c, c0 in enumerate((1024, 1280, 1536, 2048)):
                        chunk(w, c0, 256, 2 * (c % 2))
                    wv = w.rearrange("(k p) n -> p k n", p=P)
                    for s in range(2):
                        d = raw[:, s, :].rearrange("p (k h n) -> p k h n", k=4, h=2)
                        slab(s, [(d[:, :, h, :], wv[:, 4 * s:4 * s + 4, c0:c0 + 256]) for h, c0 in enumerate((1792, 2304))])
                    chunk(w, 2560, 48, 2)

                def nsa_compress(self):
                    stages.next()
                    for v in range(2):
                        w = A["nsa_cmp_w1"][0, v].rearrange("(j p) n -> p j n", p=P)
                        for s in range(2):
                            d = raw[:, 2 * v + s, :].rearrange("p (j n) -> p j n", j=8)
                            slab(2 * v + s, [(d[:, 4 * j:4 * j + 4, :], w[:, 8 * s + 4 * j:8 * s + 4 * j + 4, :])
                                             for j in range(2)])

                def nsa_attend(self):
                    stages.next()
                    chunk(A["nsa_w_o"][0], 0, 512, 0)
                    ada_slabs(1)

                def skip(self, *_):
                    stages.next()

                ada = diff_bias = diff = latent = dsa = skip

                def moba(self):
                    stages.next(2)

                def wide_inputs(self):
                    stages.next()
                    w = A["w_in_2"][0]
                    chunk(w, COLS["g"], 512, 0)
                    pieces(w, [(0, COLS["biq"], 256)] + [(256 + 32 * j, COLS["bik"], 32) for j in range(4)]
                           + [(384, COLS["biw"], 8)], 392, 2)
                    for c in range(1, 6):
                        chunk(w, COLS["g"] + 512 * c, 512, 2 * ((c + 1) % 2))
                    for c, n in enumerate(("aq", "ak", "av"), 7):
                        chunk(w, COLS[n], 512, 2 * (c % 2))

                def sparse_inputs(self):
                    stages.next(2)
                    w = A["w_in_2"][0]
                    chunk(w, COLS["bq"], 512, 0)
                    pieces(w, [(0, COLS["bkv"], P), (P, COLS["cv"], 256)], 384, 2)
                    chunk(w, COLS["cq"], 512, 0)

                def merge(self):
                    stages.next()
                    a = A["w_br_a_2"][0].rearrange("(k p) n -> p k n", p=P)
                    for s in range(2):
                        d = raw[:, 2 + s, :].rearrange("p (k n) -> p k n", k=4)
                        slab(2 + s, [(d[:, 2 * j:2 * j + 2, :], a[:, 2 * j:2 * j + 2, 512 * s:512 * s + 512]) for j in range(2)])
                    for s, n in ((0, "w_br_b_2"), (1, "w_br_c_2")):
                        w = A[n][0].rearrange("(k p) n -> p k n", p=P)
                        d = raw[:, s, :].rearrange("p (k n) -> p k n", k=2)
                        slab(s, [(d[:, j:j + 1, :], w[:, j:j + 1, :]) for j in range(2)])

                def mlp(self):
                    stages.next()
                    rounds = 8
                    wi = A["w_ff1_2"][0].rearrange("(k p) n -> p k n", p=P)
                    wo = A["w_ff2_2"][0].rearrange("(k p) n -> p k n", p=P)
                    base = list(uses.n)

                    def up(i):
                        for s in range(2):
                            d = raw[:, s, :].rearrange("p (k n) -> p k n", k=4)
                            slab(s, [(d[:, 2 * j:2 * j + 2, :], wi[:, 4 * s + 2 * j:4 * s + 2 * j + 2, ds(512 * i, 512)])
                                     for j in range(2)], base[s] + i + 1)

                    def down(i, first=2):
                        for s in range(2):
                            d = raw[:, first + s, :].rearrange("p (k n) -> p k n", k=2)
                            slab(first + s, [(d[:, j:j + 1, :], wo[:, ds(4 * i + 2 * s + j, 1), :]) for j in range(2)],
                                 base[2 + s] + i + 1 if first == 2 else None)

                    up(0)
                    with sp.Fori(1, rounds) as i:
                        up(i)
                        down(i - 1)
                    for s in range(4):
                        uses.n[s] += rounds - s // 2
                    down(rounds - 1, 0)

            for t in range(T):
                sp.dma_start(xn[:, t, :], A["mem"][0, t * P:(t + 1) * P, :]).then_inc(mem_in[0], 16)
            sp.dma_start(cst[:, :], A["constants"][:, 0:C_HOT]).then_inc(const_in, 16)
            program(Sp())
            for t in range(T):
                sp.wait_ge(rows_normed, T * (len(gains) - 1) + t + 1)
                sp.dma_start(out[0, t * P:(t + 1) * P, :], x[:, t, :]).then_inc(stored, 16)
            sp.wait_ge(stored, 16 * T)

        @block.gpsimd
        def _(pool):
            stages, steps = Count(), Count()
            squares = Count()

            def enter():
                if stages.n:
                    pool.wait_ge(stage_act, stages.n)
                    pool.wait_ge(stage_dve, stages.n)
                stages.next()

            def load_gain(m):
                pool.dma_start(gain[:, m % 2, :], gains[m].unsqueeze(0).to_broadcast([P, D])).then_inc(gain_in[m % 2], 16)

            def power(src, dst, n, mean):
                pool.tensor_scalar(var8[:, 0:n], src, 1.0 / mean, EPS, ALU.mult, ALU.add).then_inc(pool_step, 1)
                pool.wait_ge(pool_step, steps.next())
                return pool.tensor_tensor(dst, var8[:, 0:n], minus_half8[:, 0:n], ALU.pow)

            def spread(to, row, done):
                pool.dma_start(to, row.unsqueeze(0).to_broadcast([P, row.shape[0]])).then_inc(done, 16)

            def load_skew(b):
                pool.dma_start(skew, bass.AP(dist_dram.tensor, 4 * 384 * b, [[1, P], [384, 4], [1, S]])).then_inc(skew_in, 16)

            def store_ada(turn):
                cs, buf = ada_turns[turn]
                for c in cs:
                    pool.wait_ge(ada_used[1], c + 1)
                    pool.dma_start(ada_dram[c], ada_acc(c, buf)).then_inc(ada_out[c % 2], 16)
                for b in range(2):
                    pool.wait_ge(ada_out[b], 16 * (cs[-1] + 1) // 2)

            def load_mem():
                for t in range(T):
                    pool.dma_start(xn[:, t, :], A["mem"][0, t * P:(t + 1) * P, :]).then_inc(mem_in[1], 16)

            class Pool:
                def norm(self, m, mem=False, turn=True, keep=False, modulate=False):
                    enter()
                    for t in range(T):
                        pool.wait_ge(squared, squares.next())
                        power(ssq[:, t:t + 1], rstd[:, t:t + 1], 1, D).then_inc(rstd_made, 1)
                        pool.wait_ge(rstd_made, 2 * m + t + 1)
                    if m + 1 < len(gains):
                        load_gain(m + 1)
                    self.norms = m + 1
                    if m == 9:
                        self.load_ada(0)
                        pool.dma_start(hot, A["constants"][0:33, C_HOT:C_HOT + 384]).then_inc(hot_in, 16)
                        pool.dma_start(rel[0:32], A["rel_bias_2"]).then_inc(hot_in, 16)
                        pool.memset(rel[32:33], NEG).then_inc(mask_row, 1)
                        pool.wait_ge(mask_row, 1)
                        spread(lam_in, A["diff_lambda_2"][0].rearrange("a d -> (a d)"), hot_in)

                def kv(self, l):
                    enter()
                    if l == 0:
                        pool.dma_start(condT, A["c_2"].rearrange("a (k p) -> p (a k)", p=P), allow_slow_non_contiguous=True)\
                            .then_inc(cond_in, 16)

                def ffn(self, w_in, w_out):
                    enter()
                    if self.norms == 2:
                        pool.dma_start(pool_b, A["pool_b"][0].unsqueeze(0).to_broadcast([P, D])).then_inc(mix_in, 16)
                        pool.dma_start(pool_s, A["pool_scale"][0].unsqueeze(0).to_broadcast([P, D])).then_inc(mix_in, 16)
                        pool.dma_start(area[:, 8192:8192 + 4 * 384], A["constants"][:, C_BAND:C_END]).then_inc(mix_in, 16)
                    if self.norms == 5:
                        load_mem()

                def pool(self):
                    enter()

                def query(self, l):
                    enter()

                def cross(self, l):
                    enter()
                    store_ada(2 * l)

                def project(self, w, gated=False):
                    enter()
                    if gated:
                        self.load_ada(1)

                def load_ada(self, part):
                    pool.dma_start(ada_parts, ada_dram[6 * part:6 * part + 6].rearrange("c p n -> p c n")).then_inc(ada_in, 16)
                    spread(ada_bias, A["ada_b_2"][0][3072 * part:3072 * part + 3072], ada_in)

                def nsa_inputs(self):
                    enter()
                    pool.dma_start(pos_rows, A["nsa_cmp_pos"][0].rearrange("v (j a) d -> (v j) (a d)", a=2))\
                        .then_inc(pos_in, 16)
                    for to, v in ((w2k[:, :, 0:64], 0), (w2k[:, :, 64:128], 0), (w2v, 1)):
                        pool.dma_start(to, A["nsa_cmp_w2"][0, v].rearrange("(h p) n -> p h n", p=P)).then_inc(w2_in, 16)

                def nsa_compress(self):
                    enter()

                def nsa_attend(self):
                    enter()
                    store_ada(1)

                def ada(self, part):
                    enter()
                    pool.memset(ones, 1.0).then_inc(ones_made, 1)
                    pool.wait_ge(ones_made, part + 1)
                    if part == 0:
                        pool.wait_ge(dist_made, 2)
                        pool.dma_start(dist_dram, dist_rows).then_inc(dist_out, 16)

                def wide_inputs(self):
                    enter()
                    for t in range(T):
                        spread(bgate[:, t, :], A["gate_b_2"][0], gate_b_in)
                    pool.wait_ge(dist_out, 16)
                    load_skew(0)
                    spread(subln, A["diff_subln_2"][0], row_in)

                def diff_bias(self):
                    enter()

                def diff(self):
                    enter()
                    load_skew(1)

                def sparse_inputs(self):
                    enter()
                    pool.wait_ge(summed, 1)
                    power(ss8, rstd8, 8, P).then_inc(powered, 1)
                    spread(kv_gain, A["dsa_kv_norm_2"][0], row_in)
                    pool.dma_start(w_uv, A["dsa_w_uv_2"][0].rearrange("h r e -> r h e")).then_inc(row_in, 16)
                    enter()

                def latent(self):
                    enter()
                    load_skew(2)
                    pool.wait_ge(summed, 3)
                    power(ss8[:, 0:2], rstd8[:, 0:2], 2, P).then_inc(powered, 1)

                def dsa(self, t):
                    enter()

                def moba(self):
                    enter()
                    enter()

                def merge(self):
                    enter()

                def mlp(self):
                    enter()

            load_gain(0)
            pool.memset(minus_half8, -0.5).then_inc(pool_step, 1)
            pool.wait_ge(pool_step, steps.next())
            pool.memset(minus_half, -0.5).then_inc(pool_step, 1)
            pool.memset(zero.bitcast(F32)[:, :], 0.0).then_inc(zero_made, 1)
            pool.wait_ge(pool_step, steps.next())
            program(Pool())

        @block.scalar
        def _(act):
            stages, steps, uses, done = Count(), Count(), Uses(), Uses()
            c_sq, c_turned, c_ffn = Count(), Count(), Count()
            units, groups = Count(), Count()

            def enter(updates_x=False):
                if stages.n:
                    act.wait_ge(stage_dve, stages.n)
                    act.wait_ge(stage_act, stages.n)
                stages.next()
                fresh[0] = updates_x
                x_updates.next(int(updates_x))

            fresh, x_updates = [False], Count()

            def leave():
                act.drain().then_inc(stage_act, 1)

            arrived = [0] * SLOTS

            def split(slot, n=None, doubled=False, transfers=2):
                if n is None:
                    n = uses.next(slot)
                if type(n) is int:
                    arrived[slot] += 16 * transfers
                    act.wait_ge(landed[slot], arrived[slot])
                else:
                    act.wait_ge(landed[slot], 32 * n + (arrived[slot] - 32 * uses.n[slot]))
                if not (type(n) is int and n == 1):
                    act.wait_ge(consumed[slot], n - 1)
                to, of = twice(slot) if doubled else (whi[:, slot, :], raw[:, slot, :])
                act.activation(to, of, ACT.Copy).then_inc(hi_ready[slot], 1)

            def chunks(count, evac, doubled=(), transfers=(), after=None):
                for c in range(count):
                    if c + 1 == count:
                        next_slabs(2 * (count % 2))
                    if c + 1 < count:
                        for s in range(2):
                            split(2 * ((c + 1) % 2) + s, doubled=c + 1 in doubled,
                                  transfers=dict(transfers).get(c + 1, 2))
                    pair = 2 * (c % 2)
                    done.next(pair)
                    act.wait_ge(consumed[pair + 1], done.next(pair + 1))
                    evac(c, 4 * (chunk_no.n % 2)).then_inc(act_evac, 1)
                    chunk_no.next()
                    if after:
                        after(c)

            chunk_no = Count()

            def next_slabs(first=0):
                for s in range(first, first + 2):
                    split(s)

            def turned(banks):
                for b in range(banks):
                    act.wait_ge(rows_turned, c_turned.next())
                    t, k = b // 2, 4 * (b % 2)
                    act.activation(aT_hi[:, k:k + 4, t * P:(t + 1) * P],
                                   ps[:, b, :].rearrange("p (k n) -> p k n", k=4), ACT.Copy).then_inc(aT_hi_made, 1)

            class Act:
                def norm(self, m, mem=False, turn=True, keep=False, modulate=False):
                    early = fresh[0]
                    if early:
                        act.wait_ge(x_half, x_updates.n)
                        act.wait_ge(stage_act, stages.n)
                        stages.next()
                        fresh[0] = False
                    else:
                        enter()
                    if m == 1:
                        act.wait_ge(x_in, 16 * T)
                    src = xn if mem else x
                    for t in range(T):
                        if mem:
                            act.wait_ge(mem_in[m // 5], 16 * T)
                        if early and t:
                            act.wait_ge(stage_dve, stages.n - 1)
                        if mem and t:
                            act.wait_ge(squared, c_sq.n)
                        junk = hs[:, :, :].rearrange("p t n -> p (t n)") if mem else xn[:, t, :]
                        act.activation(junk, src[:, t, :], ACT.Square, accum_out=ssq[:, t:t + 1])\
                           .then_inc(squared, 1)
                        c_sq.next()
                    if turn:
                        turned(4)
                    leave()
                    if m == 0:
                        next_slabs()

                def kv(self, l):
                    enter()

                    def evac(c, b):
                        if c < 2:
                            return act.activation(kT[:, 4 * c:4 * c + 2, :], ps[:, b, :], ACT.Copy)
                        return act.activation(vm[:, 0, 512 * (c - 2):512 * (c - 1)], ps[:, b, :], ACT.Copy)
                    chunks(4, evac)
                    leave()

                def ffn(self, w_in, w_out):
                    enter(updates_x=True)
                    rounds = FF // HI
                    ub, db, fb = list(uses.n), list(done.n), c_ffn.n

                    def first_half(i):
                        act.wait_ge(gate_half, fb + i + 1)
                        act.activation(hs[:, 0, 0:HI], ps[:, 4, 0:HI], ACT.Silu).then_inc(silu_made, 1)
                        act.wait_ge(consumed[1], db[1] + i + 1)
                        act.activation(hs[:, 1, 0:HI], ps[:, 5, 0:HI], ACT.Silu).then_inc(silu_made, 1)

                    def second_half(i):
                        act.wait_ge(hid_turned, fb + i + 1)
                        act.activation(hT_hi[:, 0:2, :], ps[:, 6, :], ACT.Copy).then_inc(hT_hi_made, 1)

                    with act.Fori(0, rounds - 1) as i:
                        split(0, ub[0] + i + 1)
                        first_half(i)
                        split(1, ub[1] + i + 1)
                        second_half(i)
                        split(2, ub[2] + i + 1)
                    for s in range(3):
                        uses.n[s] += rounds - 1
                        arrived[s] += 32 * (rounds - 1)
                    split(3)
                    first_half(rounds - 1)
                    second_half(rounds - 1)
                    for s in range(4):
                        done.n[s] += (rounds, rounds, rounds - 1, 1)[s]
                    next_slabs()
                    c_ffn.next(rounds)
                    leave()

                def pool(self):
                    enter(updates_x=True)
                    act.wait_ge(cond_in, 16)
                    act.activation(condT, condT, ACT.Silu).then_inc(cond_made, 1)
                    split(2)
                    for b in range(4):
                        act.wait_ge(rows_turned, c_turned.next())
                        act.activation(aT_hi[:, 2 * b:2 * b + 2, :], ps[:, b, :], ACT.Copy).then_inc(aT_hi_made, 1)
                    done.next(2)
                    leave()

                def query(self, l):
                    enter()
                    chunks(2, lambda c, b: act.activation(qT[:, 4 * c:4 * c + 2, :], ps[:, b, :], ACT.Copy,
                                                          scale=1.0 / 16))
                    leave()

                def cross(self, l):
                    enter()

                    def exps(u):
                        U = units.n + u
                        act.wait_ge(maxed, U + 1)
                        if u >= 3:
                            act.wait_ge(probs_turned, U - 2)
                        act.activation(Pb[u % 3][:, 0:S], ps[:, u % 3, 0:S], ACT.Exp, bias=nmx[:, 2 * (u % 3):2 * (u % 3) + 1],
                                       accum_out=den[:, 2 * (u % 3):2 * (u % 3) + 1]).then_inc(exped, 1)

                    def keep(u):
                        h, t = u // 2, u % 2
                        act.wait_ge(probs_turned, units.n + u + 1)
                        if h >= 2:
                            act.wait_ge(pv_done, groups.n + h - 1)
                        act.activation(PTc(h)[:, :, t * P:(t + 1) * P],
                                       ps[:, 3 + u % 2, 0:S].rearrange("p (m q) -> p m q", m=2),
                                       ACT.Copy).then_inc(probs_kept, 1)

                    def out_hi(h):
                        act.wait_ge(pv_done, groups.n + h + 1)
                        act.activation(aT_hi[:, 2 * h:2 * h + 2, :], ps[:, 6 + h % 2, :], ACT.Copy).then_inc(o_hi, 1)

                    exps(0)
                    exps(1)
                    for u in range(8):
                        keep(u)
                        if u + 2 < 8:
                            exps(u + 2)
                        if u % 2 == 0 and u:
                            out_hi(u // 2 - 1)
                    out_hi(3)
                    units.next(8)
                    groups.next(4)
                    leave()

                def project(self, w, gated=False):
                    enter(updates_x=True)
                    if gated:
                        turned(4)
                    chunks(2, lambda c, b: act.drain())
                    leave()

                def nsa_inputs(self):
                    enter()

                    def evac(c, b):
                        if c < 2:
                            return act.activation(qT[:, 4 * c:4 * c + 2, :], ps[:, b, :], ACT.Copy, scale=0.125)
                        if c < 4:
                            return act.drain()
                        if c < 6:
                            return act.activation((ksT, kwT)[c - 4][:, 0:2, :], ps[:, b, :], ACT.Copy)
                        if c == 6:
                            return act.activation(area[:, 8192:9216].rearrange("p (v t n) -> p t v n", v=2, t=2)[:, 0],
                                                  ps[:, b, :].rearrange("p (v n) -> p v n", v=2), ACT.Copy)
                        return act.activation(gates[:, :, :], ps[:, b:b + 2, 0:48],
                                              ACT.Sigmoid)
                    chunks(8, evac, range(2, 6))
                    leave()

                def nsa_compress(self):
                    enter()
                    for c, n in cmp_pieces:
                        act.activation(aTf_hi[:, c:c + n], area[:, 9344 + c:9344 + c + n], ACT.Copy).then_inc(aT_hi_made, 1)
                    split(2)
                    split(3)
                    for v in range(2):
                        done.next(2 * v)
                        act.wait_ge(consumed[2 * v + 1], done.next(2 * v + 1))
                        act.activation(hid_rows[v], ps[0:4 * N_CMP, v, 0:CMP_HID],
                                       ACT.Gelu_apprx_tanh).then_inc(gelu_made, 1)
                    act.wait_ge(cmp_made, 1)
                    act.activation(kcT, ps[:, 2, 0:60], ACT.Copy)
                    act.wait_ge(cmp_made, 2)
                    act.activation(vcmp, ps[0:15, 3, 0:256], ACT.Copy)
                    leave()
                    next_slabs()

                def nsa_attend(self):
                    enter()

                    def exps(u):
                        U, t, b = units.n + u, u // 4 % 2, 2 * (u % 3)
                        w = P * (t + 1)
                        act.wait_ge(maxed, U + 1)
                        for j, (c, n) in enumerate(((0, w), (w, w))):
                            last = act.activation(Pb[u % 3][:, c:c + n], Pb[u % 3][:, c:c + n], ACT.Exp, scale=-1.0,
                                                  bias=nmx[:, b + j:b + j + 1], accum_out=den[:, b + j:b + j + 1])
                        last.then_inc(exped, 1)

                    def keep(u):
                        gi, t, r = u // 4, u // 4 % 2, u % 4
                        act.wait_ge(probs_turned, units.n + u + 1)
                        if gi >= 2:
                            act.wait_ge(pv_done, groups.n + gi - 1)
                        act.activation(nsaP[gi % 2][:, r, 0:2 * P * (t + 1)], ps[:, 3 + u % 2, 0:2 * P * (t + 1)], ACT.Copy)\
                           .then_inc(probs_kept, 1)

                    def out_hi(gi):
                        g, t = gi // 2, gi % 2
                        act.wait_ge(pv_done, groups.n + gi + 1)
                        act.activation(aT_hi[:, 2 * g:2 * g + 2, t * P:(t + 1) * P],
                                       ps[:, 6 + gi % 2, 0:256].rearrange("p (j q) -> p j q", j=2), ACT.Copy).then_inc(o_hi, 1)

                    def keep_cmp(gi):
                        act.wait_ge(cmp_turned, gi + 1)
                        if gi >= 2:
                            act.wait_ge(pv_done, groups.n + gi - 1)
                        act.activation(nsaPc[gi % 2][0:N_CMP], ps[0:N_CMP, 5, :].rearrange("p (r q) -> p r q", r=4), ACT.Copy)\
                           .then_inc(cmp_kept, 1)

                    act.wait_ge(cmp_centred, 1)
                    act.activation(cmpP, cmpP, ACT.Exp).then_inc(cmp_exped, 1)
                    exps(0)
                    exps(1)
                    for u in range(32):
                        keep(u)
                        if u + 2 < 32:
                            exps(u + 2)
                        if u % 4 == 2:
                            keep_cmp(u // 4)
                        if u % 4 == 1 and u > 4:
                            out_hi(u // 4 - 1)
                    out_hi(7)
                    units.next(32)
                    groups.next(8)
                    leave()

                def ada(self, part):
                    enter()
                    if part == 0:
                        act.wait_ge(dist_made, 1)
                        act.activation(dist_rows, ps[0:12, 6, 0:384], ACT.Copy).then_inc(dist_made, 1)
                        act.wait_ge(lam_summed, 2)
                        act.activation(lam2, lam2, ACT.Exp).then_inc(dist_made, 1)
                    leave()

                def wide_inputs(self):
                    enter()

                    def evac(c, b):
                        if c == 1:
                            return act.activation(iqT, ps[:, b, :].rearrange("p (k n) -> p k n", k=2), ACT.Copy)
                        if c == 7:
                            act.wait_ge(dist_out, 16)
                            return act.activation(aqT[:, 0:2, :], ps[:, b, :], ACT.Copy, scale=0.125)
                        if c == 8:
                            return act.activation(akT[:, 0:2, :], ps[:, b, :], ACT.Copy)
                        if c == 9:
                            return act.activation(av[:, 0, :], ps[:, b, :], ACT.Copy)
                        at = slice(512 * max(c - 1, 0), 512 * max(c - 1, 0) + 512)
                        act.wait_ge(dve_evac, chunk_no.n + 1)
                        return act.activation(bgate[:, :, at], bgate[:, :, at], ACT.Sigmoid)

                    def rectify(c):
                        for turn, (at, t) in enumerate(((2, 1), (5, 0))):
                            if c == at:
                                act.wait_ge(index_scored, turn + 1)
                                for j in range(4):
                                    o = ps[:, index_bank[j], 0:2 * P * (t + 1)]
                                    act.activation(o, o, ACT.Relu).then_inc(relu_made, 1)

                    chunks(10, evac, transfers=[(1, 6)], after=rectify)
                    leave()

                def keep_bias(self, b):
                    act.wait_ge(bias_turned, b + 1)
                    act.activation(bias[:, 0:2, :], ps[:, 4, :].rearrange("p (h k) -> p h k", h=2), ACT.Copy)

                def diff_bias(self):
                    enter()
                    self.keep_bias(0)
                    leave()

                def exps(self, u, segs, U, depth=2):
                    b = 2 * (u % depth)
                    act.wait_ge(maxed, U + 1)
                    for j, (c, n) in enumerate(segs):
                        last = act.activation(Pb[u % depth][:, c:c + n], Pb[u % depth][:, c:c + n], ACT.Exp, scale=-1.0,
                                              bias=nmx[:, b + j:b + j + 1], accum_out=den[:, b + j:b + j + 1])
                    last.then_inc(exped, 1)

                def diff(self):
                    enter()

                    def exps(u):
                        w = P * (u % 2 + 1)
                        self.exps(u, ((0, w), (w, w)), units.n + u, depth=3)

                    def keep(u):
                        w = P * (u % 2 + 1)
                        act.wait_ge(probs_turned, units.n + u + 1)
                        if u >= 2:
                            act.wait_ge(pv_done, groups.n + u - 1)
                        act.activation(diff_PT[u % 2][:, 0:w], ps[:, 6, 0:w], ACT.Copy).then_inc(probs_kept, 1)

                    def out(u):
                        act.wait_ge(pv_done, groups.n + u + 1)
                        act.activation(oA[:, u % 2, u // 2, :], ps[:, 7, 0:P], ACT.Copy).then_inc(o_hi, 1)

                    exps(0)
                    exps(1)
                    for u in range(8):
                        keep(u)
                        if u + 2 < 8:
                            exps(u + 2)
                        if u:
                            out(u - 1)
                    out(7)
                    units.next(8)
                    groups.next(8)
                    leave()

                def sparse_inputs(self):
                    enter()

                    def evac(c, b):
                        if c == 0:
                            return act.activation(bqT[:, 0:2, :], ps[:, b, :], ACT.Copy, scale=P ** -0.5)
                        if c == 1:
                            return act.activation(kvn, ps[:, b:b + 2, 0:P], ACT.Copy)
                        return act.activation(cqT, ps[:, b, :].rearrange("p (k n) -> p k n", k=2), ACT.Copy, scale=0.125)
                    def keep_result(c):
                        if c == 1:
                            act.wait_ge(branch_done, 1)
                            act.activation(yT[:, 0:2, :], ps[:, 2, :], ACT.Copy)

                    chunks(3, evac, after=keep_result)
                    leave()
                    enter()
                    self.keep_bias(1)
                    leave()

                def latent(self):
                    enter()
                    for t in range(T):
                        act.activation(score_part[:, P * t:P * t + P], kvn[:, t, :], ACT.Square, accum_out=ss8[:, t:t + 1]).then_inc(summed, 1)
                    leave()

                def dsa(self, t):
                    enter()
                    w = P * (t + 1)

                    def keep(u):
                        act.wait_ge(probs_turned, units.n + u + 1)
                        act.activation(PTd[:, u, 0:t + 1, :], ps[:, 2 + u % 2, 0:w].rearrange("p (m q) -> p m q", q=P), ACT.Copy)\
                           .then_inc(probs_kept, 1)

                    self.exps(0, ((0, w),), units.n)
                    for u in range(4):
                        if u + 1 < 4:
                            self.exps(u + 1, ((0, w),), units.n + u + 1)
                        keep(u)
                    act.wait_ge(pv_done, groups.n + 1)
                    act.activation(o_lat, ps[:, 4, :], ACT.Copy).then_inc(lat_kept, 1)
                    units.next(4)
                    groups.next(1)
                    act.wait_ge(branch_done, 2 + t)
                    act.activation(yT[:, 4:6, t * P:(t + 1) * P], ps[:, 5, 0:256].rearrange("p (k q) -> p k q", k=2), ACT.Copy)
                    leave()

                def moba(self):
                    enter()
                    self.keep_bias(2)
                    leave()
                    enter()

                    def exps(u):
                        self.exps(u, ((0, P * (u % 2 + 1)),), units.n + u, depth=3)

                    def keep(u):
                        w = P * (u % 2 + 1)
                        act.wait_ge(probs_turned, units.n + u + 1)
                        if u >= 2:
                            act.wait_ge(pv_done, groups.n + u - 1)
                        act.activation(moba_PT[u % 2][:, 0:w], ps[:, 5 + u % 2, 0:w], ACT.Copy).then_inc(probs_kept, 1)

                    exps(0)
                    exps(1)
                    for u in range(8):
                        keep(u)
                        if u + 2 < 8:
                            exps(u + 2)
                    units.next(8)
                    groups.next(8)
                    act.wait_ge(pv_done, groups.n)
                    act.activation(yT[:, 6:8, :], ps[:, 4, :].rearrange("p (k q) -> p k q", k=2), ACT.Copy)
                    leave()

                def merge(self):
                    enter()
                    for c in (slice(0, 1024), slice(1024, 2048)):
                        act.activation(aTf_hi[:, c], yTf[:, c], ACT.Copy).then_inc(aT_hi_made, 1)
                    split(0)
                    split(1)
                    for s in range(4):
                        done.next(s)
                    leave()
                    next_slabs()

                def mlp(self):
                    enter(updates_x=True)
                    rounds = 8
                    ub, db, fb = list(uses.n), list(done.n), c_ffn.n
                    with act.Fori(0, rounds - 1) as i:
                        split(0, ub[0] + i + 1)
                        self.mlp_round(i, db, fb)
                        split(1, ub[1] + i + 1)
                        self.mlp_turned(i, fb)
                        split(2, ub[2] + i + 1)
                        split(3, ub[3] + i + 1)
                    for s in range(4):
                        uses.n[s] += rounds - 1
                        arrived[s] += 32 * (rounds - 1)
                    self.mlp_round(rounds - 1, db, fb)
                    split(0)
                    split(1)
                    self.mlp_turned(rounds - 1, fb)
                    for s in range(4):
                        done.n[s] += (rounds + 1, rounds + 1, rounds - 1, rounds - 1)[s]
                    leave()

                def mlp_round(self, i, db, fb):
                    act.wait_ge(gate_half, fb + i + 1)
                    act.activation(hs[:, 0, :], ps[:, 4, :], ACT.Relu).then_inc(silu_made, 1)
                    act.wait_ge(consumed[1], db[1] + i + 1)
                    act.activation(hs[:, 1, :], ps[:, 5, :], ACT.Relu).then_inc(silu_made, 1)

                def mlp_turned(self, i, fb):
                    act.wait_ge(hid_turned, fb + i + 1)
                    act.activation(hT_hi[:, :, :], ps[:, 6:8, :], ACT.Copy).then_inc(hT_hi_made, 1)

            program(Act())

        @block.vector
        def _(dve):
            stages, steps, uses, done = Count(), Count(), Uses(), Uses()
            c_turned, c_ffn = Count(), Count()
            units, groups, chunk_no = Count(), Count(), Count()

            def enter():
                if stages.n:
                    dve.wait_ge(stage_dve, stages.n)
                    dve.wait_ge(stage_act, stages.n)
                stages.next()

            def leave():
                dve.drain().then_inc(stage_dve, 1)

            def step(ins):
                ins.then_inc(dve_step, 1)
                dve.wait_ge(dve_step, steps.next())

            def split(slot, n=None, doubled=False):
                if n is None:
                    n = uses.next(slot)
                dve.wait_ge(hi_ready[slot], n)
                if doubled:
                    hi, of = twice(slot)
                    lo = wlo[:, slot, :].rearrange("p (g a n) -> p g a n", a=2, n=64)
                else:
                    hi, of, lo = whi[:, slot, :], raw[:, slot, :], wlo[:, slot, :]
                dve.tensor_tensor(lo, of, hi, ALU.subtract).then_inc(lo_ready[slot], 1)

            def chunks(count, evac, doubled=(), after=None):
                for c in range(count):
                    if c + 1 == count:
                        next_slabs(2 * (count % 2))
                    if c + 1 < count:
                        for s in range(2):
                            split(2 * ((c + 1) % 2) + s, doubled=c + 1 in doubled)
                    pair = 2 * (c % 2)
                    done.next(pair)
                    dve.wait_ge(consumed[pair + 1], done.next(pair + 1))
                    evac(c, 4 * (chunk_no.n % 2)).then_inc(dve_evac, 1)
                    chunk_no.next()
                    if after:
                        after(c)

            def next_slabs(first=0):
                for s in range(first, first + 2):
                    split(s)

            def lower(b, dst_hi, dst_lo, src):
                dve.wait_ge(aT_hi_made, c_turned.next())
                dve.tensor_tensor(dst_lo, src, dst_hi, ALU.subtract).then_inc(aT_made, 1)

            def ada_row(turn, n):
                cs, buf = ada_turns[turn]
                c, k = cs[n // 8], n % 8
                s, r = k // 4, k % 4
                acc, w = ada_acc(c, buf), raw[:, 2 + s, 512 * r:512 * r + 512]
                if r == 0:
                    dve.wait_ge(ada_landed[s], 32 * (c + 1))
                if k == 0:
                    if turn == 0 and n == 0:
                        dve.wait_ge(cond_made, 1)
                    if c >= 2:
                        dve.wait_ge(ada_out[c % 2], 16 * (c // 2))
                    ins = dve.tensor_scalar(acc, w, condT[:, 0:1], None, ALU.mult)
                else:
                    if r == 0:
                        dve.wait_ge(ada_used[0], c + 1)
                    else:
                        dve.wait_ge(dve_step, ada_step[0])
                    ins = dve.scalar_tensor_tensor(out=acc, in0=w, scalar=condT[:, k:k + 1], in1=acc,
                                                   op0=ALU.mult, op1=ALU.add)
                if r == 3:
                    ins.then_inc(ada_used[s], 1)
                else:
                    ins.then_inc(dve_step, 1)
                    ada_step[0] = steps.next()

            ada_step = [0]

            class Dve:
                def norm(self, m, mem=False, turn=True, keep=False, modulate=False):
                    enter()
                    dve.wait_ge(gain_in[m % 2], 16 * (m // 2 + 1))
                    src = xn if mem else x
                    to = x if keep else xn
                    if modulate:
                        step(dve.scalar_tensor_tensor(out=gain[:, m % 2, :], in0=mod[:, 1024:2048], scalar=1.0,
                                                      in1=gain[:, m % 2, :], op0=ALU.add, op1=ALU.mult))
                    for t in range(T):
                        dve.wait_ge(rstd_made, 2 * m + t + 1)
                        last = dve.scalar_tensor_tensor(out=to[:, t, :], in0=src[:, t, :], scalar=rstd[:, t:t + 1],
                                                        in1=gain[:, m % 2, :], op0=ALU.mult, op1=ALU.mult)
                        if modulate:
                            step(last)
                            last = dve.tensor_tensor(xn[:, t, :], xn[:, t, :], mod[:, 0:1024], ALU.add)
                        last.then_inc(rows_normed, 1)
                    if turn:
                        for b in range(4):
                            t, k = b // 2, 4 * (b % 2)
                            at = (slice(None), slice(k, k + 4), slice(t * P, (t + 1) * P))
                            lower(b, aT_hi[at], aT_lo[at], ps[:, b, :].rearrange("p (k n) -> p k n", k=4))
                    leave()
                    if m == 0:
                        next_slabs()

                def kv(self, l):
                    enter()

                    def evac(c, b):
                        if c < 2:
                            return dve.tensor_copy(kT[:, 4 * c + 2:4 * c + 4, :], ps[:, b + 1, :])
                        return dve.tensor_copy(vm[:, 1, 512 * (c - 2):512 * (c - 1)], ps[:, b + 1, :])
                    chunks(4, evac)
                    leave()

                def ffn(self, w_in, w_out):
                    enter()
                    rounds = FF // HI
                    ub, db, fb = list(uses.n), list(done.n), c_ffn.n

                    def first_half(i):
                        for t in range(T):
                            dve.wait_ge(silu_made, 2 * (fb + i) + t + 1)
                            dve.tensor_tensor(hs[:, t, HI:2 * HI], hs[:, t, 0:HI], ps[:, 4 + t, HI:2 * HI], ALU.mult)\
                               .then_inc(hid_made, 1)

                    def second_half(i):
                        dve.wait_ge(hT_hi_made, fb + i + 1)
                        dve.tensor_tensor(hT_lo[:, 0:2, :], ps[:, 6, :].rearrange("p (k n) -> p k n", k=2),
                                          hT_hi[:, 0:2, :], ALU.subtract).then_inc(hT_made, 1)

                    with dve.Fori(0, rounds - 1) as i:
                        split(0, ub[0] + i + 1)
                        first_half(i)
                        split(1, ub[1] + i + 1)
                        second_half(i)
                        split(2, ub[2] + i + 1)
                    for s in range(3):
                        uses.n[s] += rounds - 1
                    split(3)
                    first_half(rounds - 1)
                    second_half(rounds - 1)
                    for s in range(4):
                        done.n[s] += (rounds, rounds, rounds - 1, 1)[s]
                    next_slabs()
                    c_ffn.next(rounds)
                    dve.wait_ge(consumed[3], done.n[3])
                    for b in range(4):
                        t, c = b // 2, b % 2
                        at = x[:, t, 512 * c:512 * c + 512]
                        last = dve.scalar_tensor_tensor(out=at, in0=ps[:, b, :], scalar=0.5, in1=at,
                                                        op0=ALU.mult, op1=ALU.add)
                        if b == 1:
                            last.then_inc(x_half, 1)
                    leave()

                def pool(self):
                    enter()
                    dve.wait_ge(mix_in, 48)
                    step(dve.tensor_tensor(pool_b, pool_b, pool_s, ALU.mult))
                    for t in range(T):
                        dve.tensor_tensor(x[:, t, :], x[:, t, :], pool_b, ALU.add)
                    split(2)
                    for b in range(4):
                        at = (slice(None), slice(2 * b, 2 * b + 2), slice(None))
                        lower(b, aT_hi[at], aT_lo[at], ps[:, b, :].rearrange("p (k n) -> p k n", k=2))
                    dve.wait_ge(consumed[2], done.next(2))
                    for b in range(4):
                        t, c = b // 2, slice(512 * (b % 2), 512 * (b % 2) + 512)
                        step(dve.tensor_tensor(xn[:, t, c], ps[:, 4 + b, :], pool_s[:, c], ALU.mult))
                        last = dve.tensor_tensor(x[:, t, c], x[:, t, c], xn[:, t, c], ALU.add)
                        if b == 1:
                            last.then_inc(x_half, 1)
                    leave()

                def query(self, l):
                    enter()
                    chunks(2, lambda c, b: dve.tensor_scalar(qT[:, 4 * c + 2:4 * c + 4, :],
                                                             ps[:, b + 1, :].rearrange("p (k n) -> p k n", k=2), 1.0 / 16, None, ALU.mult))
                    leave()

                def cross(self, l):
                    enter()

                    def top(u):
                        U = units.n + u
                        dve.wait_ge(scored, U + 1)
                        if u >= 3:
                            dve.wait_ge(exped, U - 2)
                        dve.tensor_reduce(nmx[:, 2 * (u % 3):2 * (u % 3) + 1], ps[:, u % 3, 0:S], AX.X, ALU.max, negate=True)\
                           .then_inc(maxed, 1)

                    def weigh(u):
                        b = 2 * (u % 3)
                        dve.wait_ge(exped, units.n + u + 1)
                        step(dve.reciprocal(rec[:, b:b + 1], den[:, b:b + 1]))
                        dve.tensor_scalar(Pb[u % 3][:, 0:S], Pb[u % 3][:, 0:S], rec[:, b:b + 1], None, ALU.mult)\
                           .then_inc(weighed, 1)

                    def out_lo(h):
                        dve.wait_ge(o_hi, groups.n + h + 1)
                        dve.tensor_tensor(aT_lo[:, 2 * h:2 * h + 2, :], ps[:, 6 + h % 2, :].rearrange("p (k n) -> p k n", k=2),
                                          aT_hi[:, 2 * h:2 * h + 2, :], ALU.subtract).then_inc(o_kept, 1)

                    top(0)
                    top(1)
                    for u in range(8):
                        weigh(u)
                        ada_row(2 * l, 2 * u)
                        if u + 2 < 8:
                            top(u + 2)
                        ada_row(2 * l, 2 * u + 1)
                        if u % 2 == 0 and u:
                            out_lo(u // 2 - 1)
                    out_lo(3)
                    units.next(8)
                    groups.next(4)
                    leave()

                def project(self, w, gated=False):
                    enter()
                    if gated:
                        for b in range(4):
                            t, k = b // 2, 4 * (b % 2)
                            at = (slice(None), slice(k, k + 4), slice(t * P, (t + 1) * P))
                            lower(b, aT_hi[at], aT_lo[at], ps[:, b, :].rearrange("p (k n) -> p k n", k=4))

                    def evac(c, b):
                        for t in range(T):
                            at = x[:, t, 512 * c:512 * c + 512]
                            if gated:
                                y = hs[:, t, :]
                                step(dve.tensor_tensor(y, ps[:, b + t, :], out_gate[:, 512 * c:512 * c + 512], ALU.mult))
                                last = dve.tensor_tensor(at, at, y, ALU.add)
                            else:
                                last = dve.tensor_tensor(at, at, ps[:, b + t, :], ALU.add)
                            if t == 0 and c == 1:
                                last.then_inc(x_half, 1)
                        return last
                    chunks(2, evac)
                    leave()

                def nsa_inputs(self):
                    enter()

                    def evac(c, b):
                        if c < 2:
                            return dve.tensor_scalar(qT[:, 4 * c + 2:4 * c + 4, :],
                                                     ps[:, b + 1, :].rearrange("p (k n) -> p k n", k=2), 0.125, None, ALU.mult)
                        if c in (2, 3):
                            v = c - 2
                            if c == 2:
                                step(dve.tensor_copy(posT, ps[:, b + 2, 0:32]))
                            for g in range(4):
                                for a in range(2):
                                    half = slice(64 * a, 64 * a + 64)
                                    src = ps[half, b + g // 2, 256 * (g % 2) + a:256 * (g % 2) + a + 255]
                                    win = bass.AP(src.tensor, src.offset, [list(src.ap[0]), [2, 16], [16, N_CMP]])
                                    last = dve.tensor_tensor(blk[half, v, :, g, :], win,
                                                             posT[half, 16 * v:16 * v + 16].unsqueeze(2)
                                                             .to_broadcast([64, 16, N_CMP]), ALU.add)
                            return last
                        if c in (4, 5):
                            return dve.tensor_copy((ksT, kwT)[c - 4][:, 2:4, :], ps[:, b + 1, :])
                        if c == 6:
                            return dve.tensor_copy(area[:, 8192:9216].rearrange("p (v t n) -> p t v n", v=2, t=2)[:, 1],
                                                   ps[:, b + 1, :].rearrange("p (v n) -> p v n", v=2))
                        return dve.drain()
                    chunks(8, evac, range(2, 6))
                    leave()

                def nsa_compress(self):
                    enter()
                    dve.tensor_scalar(gates[:, 0, 0:48:3], gates[:, 0, 0:48:3], cst[:, C_VIS:C_VIS + 1], None, ALU.mult)
                    for c, n in cmp_pieces:
                        dve.wait_ge(aT_hi_made, c_turned.next())
                        dve.tensor_tensor(aTf_lo[:, c:c + n], area[:, 9344 + c:9344 + c + n], aTf_hi[:, c:c + n],
                                          ALU.subtract).then_inc(aT_made, 1)
                    split(2)
                    split(3)
                    for v in range(2):
                        done.next(2 * v)
                        done.next(2 * v + 1)
                    for v in range(2):
                        dve.wait_ge(cmp_hid_turned, v + 1)
                        dve.tensor_copy(hidT[:, v], ps[:, 4 + v, 0:P].rearrange("p (h n) -> p h n", h=2)[:, :, 0:4 * N_CMP])\
                           .then_inc(cmp_hid_kept, 1)
                    leave()
                    next_slabs()

                def nsa_attend(self):
                    enter()

                    def top(u):
                        U, t, b = units.n + u, u // 4 % 2, 2 * (u % 3)
                        w = P * (t + 1)
                        dve.wait_ge(scored, U + 1)
                        if u >= 3:
                            dve.wait_ge(probs_turned, U - 2)
                        for j in range(2):
                            last = dve.tensor_tensor_reduce(Pb[u % 3][:, w * j:w * j + w], ps[:, u % 3, w * j:w * j + w],
                                                            cst[:, C_CAUSAL + S - w:C_CAUSAL + S], -1.0, BIG, ALU.add, ALU.min,
                                                            nmx[:, b + j:b + j + 1])
                        last.then_inc(maxed, 1)

                    def weigh(u):
                        t, b = u // 4 % 2, 2 * (u % 3)
                        w, h = P * (t + 1), 4 * (u // 8) + u % 4
                        dve.wait_ge(exped, units.n + u + 1)
                        step(dve.reciprocal(rec[:, b:b + 2], den[:, b:b + 2]))
                        for j in range(2):
                            p = Pb[u % 3][:, w * j:w * j + w]
                            last = dve.tensor_scalar(p, p, rec[:, b + j:b + j + 1], gates[:, t, 3 * h + 1 + j:3 * h + 2 + j],
                                                     ALU.mult, ALU.mult)
                        last.then_inc(weighed, 1)

                    def out_lo(gi):
                        g, t = gi // 2, gi % 2
                        dve.wait_ge(o_hi, groups.n + gi + 1)
                        at = (slice(None), slice(2 * g, 2 * g + 2), slice(t * P, (t + 1) * P))
                        dve.tensor_tensor(aT_lo[at], ps[:, 6 + gi % 2, 0:256].rearrange("p (j q) -> p j q", j=2),
                                          aT_hi[at], ALU.subtract).then_inc(o_kept, 1)

                    mask = cst[:, C_CMP:C_CMP + 32].rearrange("p (t n) -> p t n", t=T)[:, :, 0:N_CMP]
                    every = [P, T, NSA_H, N_CMP]
                    dve.wait_ge(cmp_scored, 2)
                    for par in range(2):
                        scores = ps[:, 6 + par, 0:256].rearrange("p (t h n) -> p t h n", t=T, h=NSA_H // 2)[:, :, :, 0:N_CMP]
                        step(dve.tensor_tensor(cmpP[:, :, par::2, :], scores,
                                               mask.unsqueeze(2).to_broadcast([P, T, NSA_H // 2, N_CMP]), ALU.add))
                    step(dve.tensor_reduce(cmp_max, cmpP, AX.X, ALU.max))
                    dve.tensor_tensor(cmpP, cmpP, cmp_max.unsqueeze(3).to_broadcast(every), ALU.subtract).then_inc(cmp_centred, 1)
                    top(0)
                    top(1)
                    dve.wait_ge(cmp_exped, 1)
                    step(dve.tensor_reduce(cmp_rec, cmpP, AX.X, ALU.add))
                    step(dve.reciprocal(cmp_rec, cmp_rec))
                    step(dve.tensor_tensor(cmp_rec, cmp_rec, gates[:, :, 0::3], ALU.mult))
                    dve.tensor_tensor(cmpP, cmpP, cmp_rec.unsqueeze(3).to_broadcast(every), ALU.mult).then_inc(cmp_weighed, 1)
                    for u in range(32):
                        weigh(u)
                        ada_row(1, 2 * u)
                        if u + 2 < 32:
                            top(u + 2)
                        ada_row(1, 2 * u + 1)
                        if u % 4 == 1 and u > 4:
                            out_lo(u // 4 - 1)
                    out_lo(7)
                    units.next(32)
                    groups.next(8)
                    leave()

                def ada(self, part):
                    enter()
                    if part == 0:
                        dve.wait_ge(hot_in, 48)
                        for j in range(2):
                            dve.tensor_tensor_reduce(lam_prod[:, 64 * j:64 * j + 64], lam_in[:, P * j:P * j + 64],
                                                     lam_in[:, P * j + 64:P * j + P], 1.0, 0.0, ALU.mult, ALU.add,
                                                     lam2[:, j:j + 1]).then_inc(lam_summed, 1)
                        dve.wait_ge(dist_made, 3)
                        step(dve.tensor_tensor(neg_lam, lam2[:, 1:2], lam2[:, 0:1], ALU.subtract))
                        step(dve.tensor_scalar(neg_lam, neg_lam, -LAM_INIT, None, ALU.add))
                    for c in range(6):
                        dve.wait_ge(ada_summed, 6 * part + c + 1)
                        dve.tensor_tensor(mod[:, 512 * c:512 * c + 512], ps[:, c, :], ada_bias[:, 512 * c:512 * c + 512], ALU.add)
                    leave()

                def wide_inputs(self):
                    enter()

                    def evac(c, b):
                        if c == 1:
                            dve.tensor_copy(ikT, ps[:, b + 1, 0:S])
                            return dve.tensor_scalar(iw, ps[:, b + 2:b + 4, 0:8], 0.0625,
                                                     None, ALU.mult)
                        if c == 7:
                            dve.wait_ge(dist_out, 16)
                            return dve.tensor_scalar(aqT[:, 2:4, :], ps[:, b + 1, :].rearrange("p (k n) -> p k n", k=2),
                                                     0.125, None, ALU.mult)
                        if c == 8:
                            return dve.tensor_copy(akT[:, 2:4, :], ps[:, b + 1, :])
                        if c == 9:
                            return dve.tensor_copy(av[:, 1, :], ps[:, b + 1, :])
                        if c == 0:
                            dve.wait_ge(gate_b_in, 32)
                        at = bgate[:, :, 512 * max(c - 1, 0):512 * max(c - 1, 0) + 512]
                        return dve.tensor_tensor(at, at, ps[:, b:b + 2, :], ALU.add)

                    def choose(c):
                        t = 1 if c < 6 else 0
                        if c in (3, 6):
                            self.index_sums(t)
                        if c in (4, 5, 7, 8):
                            self.index_top(t, TOPK // 16)
                        if c in (5, 8):
                            step(dve.tensor_scalar(sel[t], work[t].rearrange("p (k n) -> p k n", n=P), -2.0e38, NEG,
                                                   ALU.is_gt, ALU.mult))

                    chunks(10, evac, after=choose)
                    leave()

                def index_sums(self, t):
                    w = P * (t + 1)
                    wk = work[t]
                    for h in (0, 4, 1, 5, 2, 6, 3, 7):
                        if h < 4:
                            dve.wait_ge(relu_made, 4 * (1 - t) + h + 1)
                        src = ps[:, index_bank[h % 4], w * (h // 4):w * (h // 4) + w]
                        if h == 0:
                            last = dve.tensor_scalar(wk, src, iw[:, t, h:h + 1], None, ALU.mult)
                        else:
                            last = dve.scalar_tensor_tensor(out=wk, in0=src, scalar=iw[:, t, h:h + 1], in1=wk,
                                                            op0=ALU.mult, op1=ALU.add)
                        if h < 7:
                            step(last)
                    last.then_inc(index_read, 1)
                    dve.wait_ge(index_read, 2 - t)
                    step(dve.tensor_tensor(wk, wk, cst[:, C_CAUSAL + S - w:C_CAUSAL + S], ALU.add))

                def index_top(self, t, rounds):
                    for _ in range(rounds):
                        step(dve.max(top8[t], work[t]))
                        step(dve.match_replace(work[t], top8[t], work[t], -BIG))

                def keep_bias(self, b):
                    dve.wait_ge(bias_turned, b + 1)
                    dve.tensor_copy(bias[:, 2:4, :], ps[:, 5, :].rearrange("p (h k) -> p h k", h=2))

                def diff_bias(self):
                    enter()
                    self.keep_bias(0)
                    dve.wait_ge(row_in, 16)
                    dve.tensor_scalar(subln, subln, 1.0 - LAM_INIT, None, ALU.mult)
                    leave()

                def diff(self):
                    enter()

                    def top(u):
                        U, h, t, b = units.n + u, u // 2, u % 2, 2 * (u % 3)
                        w = P * (t + 1)
                        dve.wait_ge(scored, U + 1)
                        if u >= 3:
                            dve.wait_ge(probs_turned, U - 2)
                        for j in range(2):
                            last = dve.tensor_tensor_reduce(Pb[u % 3][:, w * j:w * j + w], ps[:, 2 * (u % 3) + j, 0:w],
                                                            bias[:, h, S - w:S], -1.0, BIG, ALU.add, ALU.min,
                                                            nmx[:, b + j:b + j + 1])
                        last.then_inc(maxed, 1)

                    def weigh(u):
                        b, w = 2 * (u % 3), P * (u % 2 + 1)
                        p0, p1 = Pb[u % 3][:, 0:w], Pb[u % 3][:, w:2 * w]
                        dve.wait_ge(exped, units.n + u + 1)
                        step(dve.reciprocal(rec[:, b:b + 2], den[:, b:b + 2]))
                        step(dve.tensor_tensor(rec[:, b + 1:b + 2], rec[:, b + 1:b + 2], neg_lam, ALU.mult))
                        step(dve.tensor_scalar(p1, p1, rec[:, b + 1:b + 2], None, ALU.mult))
                        dve.scalar_tensor_tensor(out=p0, in0=p0, scalar=rec[:, b:b + 1], in1=p1, op0=ALU.mult, op1=ALU.add)\
                           .then_inc(weighed, 1)

                    top(0)
                    top(1)
                    for u in range(8):
                        weigh(u)
                        if u + 2 < 8:
                            top(u + 2)
                    units.next(8)
                    groups.next(8)
                    leave()

                def sparse_inputs(self):
                    enter()
                    sq = xnf[:, 0:1024]
                    step(dve.tensor_tensor(sq, hsf, hsf, ALU.mult))
                    dve.tensor_reduce(ss8, sq.rearrange("p (u e) -> p u e", u=8), AX.X, ALU.add).then_inc(summed, 1)

                    def evac(c, b):
                        if c == 0:
                            return dve.tensor_scalar(bqT[:, 2:4, :], ps[:, b + 1, :].rearrange("p (k n) -> p k n", k=2),
                                                     P ** -0.5, None, ALU.mult)
                        if c == 1:
                            dve.wait_ge(act_evac, chunk_no.n + 1)
                            return dve.tensor_copy(cv, ps[:, b:b + 2, P:P + 256])
                        return dve.tensor_copy(ckT, ps[:, b + 1, :].rearrange("p (k n) -> p k n", k=2))
                    def norm_results(c):
                        if c == 0:
                            dve.wait_ge(powered, 1)
                            o8 = hsf.rearrange("p (u e) -> p u e", u=8)
                            step(dve.tensor_tensor(o8, o8, rstd8.unsqueeze(2).to_broadcast([P, 8, P]), ALU.mult))
                            dve.tensor_tensor(o8, o8, subln.unsqueeze(1).to_broadcast([P, 8, P]), ALU.mult)\
                               .then_inc(branch_kept, 1)
                        if c == 1:
                            dve.wait_ge(branch_done, 1)
                            dve.tensor_copy(yT[:, 2:4, :], ps[:, 3, :].rearrange("p (k n) -> p k n", k=2))

                    chunks(3, evac, after=norm_results)
                    leave()
                    enter()
                    self.keep_bias(1)
                    leave()

                def latent(self):
                    enter()
                    dve.wait_ge(row_in, 48)
                    dve.wait_ge(powered, 2)
                    for t in range(T):
                        last = dve.scalar_tensor_tensor(out=kvn[:, t, :], in0=kvn[:, t, :], scalar=rstd8[:, t:t + 1],
                                                        in1=kv_gain, op0=ALU.mult, op1=ALU.mult)
                    last.then_inc(branch_kept, 1)
                    dve.wait_ge(branch_kept, 3)
                    dve.tensor_copy(kvT, ps[:, 0, 0:S])
                    leave()

                def dsa(self, t):
                    enter()
                    w = P * (t + 1)

                    def top(u):
                        U, b = units.n + u, 2 * (u % 2)
                        pb = Pb[u % 2][:, 0:w]
                        blocks = "p (k n) -> p k n"
                        if u >= 2:
                            dve.wait_ge(probs_turned, U - 1)
                        step(dve.tensor_tensor(pb.rearrange(blocks, n=P), bias[:, u, S - w:S].rearrange(blocks, n=P), sel[t], ALU.add))
                        dve.wait_ge(scored, U + 1)
                        dve.tensor_tensor_reduce(pb, ps[:, u % 2, 0:w], pb, -1.0, BIG, ALU.add, ALU.min,
                                                 nmx[:, b:b + 1]).then_inc(maxed, 1)

                    top(0)
                    for u in range(4):
                        if u + 1 < 4:
                            top(u + 1)
                        self.weigh_one(u, w)
                    units.next(4)
                    groups.next(1)
                    leave()

                def weigh_one(self, u, w, depth=2):
                    b = 2 * (u % depth)
                    dve.wait_ge(exped, units.n + u + 1)
                    step(dve.reciprocal(rec[:, b:b + 1], den[:, b:b + 1]))
                    dve.tensor_scalar(Pb[u % depth][:, 0:w], Pb[u % depth][:, 0:w], rec[:, b:b + 1], None, ALU.mult)\
                       .then_inc(weighed, 1)

                def moba(self):
                    enter()
                    self.keep_bias(2)
                    leave()
                    enter()

                    def top(u):
                        U, h, b, w = units.n + u, u // 2, 2 * (u % 3), P * (u % 2 + 1)
                        dve.wait_ge(scored, U + 1)
                        if u >= 3:
                            dve.wait_ge(probs_turned, U - 2)
                        dve.tensor_tensor_reduce(Pb[u % 3][:, 0:w], ps[:, u % 3, 0:w], bias[:, h, S - w:S], -1.0, BIG,
                                                 ALU.add, ALU.min, nmx[:, b:b + 1]).then_inc(maxed, 1)

                    top(0)
                    top(1)
                    for u in range(8):
                        self.weigh_one(u, P * (u % 2 + 1), depth=3)
                        if u + 2 < 8:
                            top(u + 2)
                    units.next(8)
                    groups.next(8)
                    leave()

                def merge(self):
                    enter()
                    for c in (slice(0, 1024), slice(1024, 2048)):
                        dve.wait_ge(aT_hi_made, c_turned.next())
                        dve.tensor_tensor(aTf_lo[:, c], yTf[:, c], aTf_hi[:, c], ALU.subtract).then_inc(aT_made, 1)
                    split(0)
                    split(1)
                    for s in range(4):
                        done.next(s)
                    for br in range(3):
                        dve.wait_ge(branch_done, 4 + br)
                        for t in range(T):
                            g = bgate[:, t, 1024 * br:1024 * br + 1024].rearrange("p (c n) -> p c n", c=2)
                            y = ps[:, 4 * (br % 2) + 2 * t:4 * (br % 2) + 2 * t + 2, :]
                            m = xn[:, t, :].rearrange("p (c n) -> p c n", c=2)
                            if br == 0:
                                last = dve.tensor_tensor(m, y, g, ALU.mult)
                                continue
                            last = dve.tensor_tensor(g, y, g, ALU.mult)
                        last.then_inc(branch_kept, 1)
                        if br:
                            dve.wait_ge(branch_kept, 3 + br + 1)
                            for t in range(T):
                                g = bgate[:, t, 1024 * br:1024 * br + 1024]
                                last = dve.tensor_tensor(xn[:, t, :], xn[:, t, :], g, ALU.add)
                            if br == 1:
                                step(last)
                    leave()
                    next_slabs()

                def mlp(self):
                    enter()
                    rounds = 8
                    ub, db, fb = list(uses.n), list(done.n), c_ffn.n
                    with dve.Fori(0, rounds - 1) as i:
                        split(0, ub[0] + i + 1)
                        self.mlp_round(i, fb)
                        split(1, ub[1] + i + 1)
                        self.mlp_turned(i, fb)
                        split(2, ub[2] + i + 1)
                        split(3, ub[3] + i + 1)
                    for s in range(4):
                        uses.n[s] += rounds - 1
                    self.mlp_round(rounds - 1, fb)
                    split(0)
                    split(1)
                    self.mlp_turned(rounds - 1, fb)
                    for s in range(4):
                        done.n[s] += (rounds + 1, rounds + 1, rounds - 1, rounds - 1)[s]
                    dve.wait_ge(consumed[1], done.n[1])
                    for t in range(T):
                        y = xn[:, t, :]
                        step(dve.tensor_tensor(y.rearrange("p (c n) -> p c n", c=2), ps[:, 2 * t:2 * t + 2, :],
                                               out_gate.rearrange("p (c n) -> p c n", c=2), ALU.mult))
                        last = dve.tensor_tensor(x[:, t, :], x[:, t, :], y, ALU.add)
                        if t == 0:
                            last.then_inc(x_half, 1)
                    leave()

                def mlp_round(self, i, fb):
                    for t in range(T):
                        dve.wait_ge(silu_made, 2 * (fb + i) + t + 1)
                        dve.tensor_tensor(hs[:, t, :], hs[:, t, :], ps[:, 4 + t, :], ALU.mult).then_inc(hid_made, 1)

                def mlp_turned(self, i, fb):
                    dve.wait_ge(hT_hi_made, fb + i + 1)
                    dve.tensor_tensor(hT_lo[:, :, :], ps[:, 6:8, :].rearrange("p b (k n) -> p (b k) n", k=2), hT_hi[:, :, :],
                                      ALU.subtract).then_inc(hT_made, 1)

            program(Dve())

        @block.tensor
        def _(pe):
            stages, uses = Count(), Uses()
            c_turned, c_ffn = Count(), Count()
            units, groups, chunk_no = Count(), Count(), Count()

            def enter():
                if stages.n:
                    pe.wait_ge(stage_act, stages.n)
                    pe.wait_ge(stage_dve, stages.n)
                stages.next()

            def parts(o, lh, ll, rh, rl, start, stop):
                pe.matmul(o, lh, rl, start=start, stop=False, skip_group_check=True)
                pe.matmul(o, ll, rh, start=False, stop=False, skip_group_check=True)
                return pe.matmul(o, lh, rh, start=False, stop=stop, skip_group_check=True)

            def chunk(pair, n, outs):
                before = chunk_no.next() - 2
                if before >= 0:
                    pe.wait_ge(act_evac, before)
                    pe.wait_ge(dve_evac, before)
                for s in range(2):
                    pe.wait_ge(lo_ready[pair + s], uses.next(pair + s))
                for j, (kind, *a, o) in enumerate(outs):
                    for k in range(KD):
                        s, r = k // 4, k % 4
                        if kind == "N":
                            t, c, m = a
                            tok = slice(t * P, (t + 1) * P)
                            last = parts(o, aT_hi[:, k, tok], aT_lo[:, k, tok], whi[:, pair + s, r * n + c:r * n + c + m],
                                         wlo[:, pair + s, r * n + c:r * n + c + m], k == 0, k == KD - 1)
                        else:
                            c, m = a
                            last = parts(o, whi[:, pair + s, r * n + c:r * n + c + m],
                                         wlo[:, pair + s, r * n + c:r * n + c + m], aT_hi[:, k, :], aT_lo[:, k, :],
                                         k == 0, k == KD - 1)
                        if j == len(outs) - 1 and r == 3:
                            last.then_inc(consumed[pair + s], 1)

            def rows(b):
                return [("N", t, 0, 512, ps[:, b + t, :]) for t in range(T)]

            def turned(b):
                return [("T", 128 * j, 128, ps[:, b + j // 2, 256 * (j % 2):256 * (j % 2) + 256]) for j in range(4)]

            def bank():
                return 4 * (chunk_no.n % 2)

            def turn_rows(normed=None):
                for b in range(4):
                    t = b // 2
                    if normed is not None and b % 2 == 0:
                        pe.wait_ge(rows_normed, normed + t + 1)
                    for k in range(4):
                        f = 4 * (b % 2) + k
                        last = pe.transpose(ps[:, b, P * k:P * k + P], xn[:, t, P * f:P * f + P], ident)
                    last.then_inc(rows_turned, 1)

            class Pe:
                def norm(self, m, mem=False, turn=True, keep=False, modulate=False):
                    enter()
                    if turn:
                        turn_rows(2 * m)
                        c_turned.next(4)

                def kv(self, l):
                    enter()
                    for c in range(4):
                        chunk(2 * (c % 2), 512, turned(bank()) if c < 2 else rows(bank()))

                def ffn(self, w_in, w_out):
                    stages.next()
                    rows_ready = c_turned.n - 4
                    rounds = FF // HI
                    ub, fb = list(uses.n), c_ffn.n
                    def up(i):
                        for s in range(2):
                            pe.wait_ge(lo_ready[s], ub[s] + i + 1)
                            h, lw = (w[:, s, :].rearrange("p (k n) -> p k n", k=4) for w in (whi, wlo))
                            for t in range(T):
                                if type(i) is int and i == 0:
                                    pe.wait_ge(aT_made, rows_ready + 2 * t + s + 1)
                                tok = slice(t * P, (t + 1) * P)
                                for r in range(4):
                                    k = 4 * s + r
                                    last = parts(ps[:, 4 + t, :], aT_hi[:, k, tok], aT_lo[:, k, tok], h[:, r, :],
                                                 lw[:, r, :], k == 0, k == KD - 1)
                                if s == 1 and t == 0:
                                    last.then_inc(gate_half, 1)
                            last.then_inc(consumed[s], 1)

                    def turn(i):
                        for t in range(T):
                            pe.wait_ge(hid_made, 2 * (fb + i) + t + 1)
                            for k in range(2):
                                last = pe.transpose(ps[:, 6, S * k + P * t:S * k + P * t + P],
                                                    hs[:, t, HI + P * k:HI + P * k + P], ident)
                        last.then_inc(hid_turned, 1)

                    def down(i, stop, slot=2):
                        pe.wait_ge(lo_ready[slot], ub[2] + i + 1 if slot == 2 else uses.next(3))
                        pe.wait_ge(hT_made, fb + i + 1)
                        h, lw = (w[:, slot, :].rearrange("p (k c n) -> p k c n", k=2, c=2) for w in (whi, wlo))
                        for t in range(T):
                            tok = slice(t * P, (t + 1) * P)
                            for c in range(2):
                                for k in range(2):
                                    last = parts(ps[:, 2 * t + c, :], hT_hi[:, k, tok], hT_lo[:, k, tok],
                                                 h[:, k, c, :], lw[:, k, c, :], False, stop and k == 1)
                        last.then_inc(consumed[slot], 1)

                    up(0)
                    for b in range(4):
                        pe.matmul(ps[:, b, :], zero[:, 0:P], zero[:, :], start=True, stop=False, skip_group_check=True)
                    turn(0)
                    with pe.Fori(1, rounds) as i:
                        up(i)
                        down(i - 1, False)
                        turn(i)
                    down(rounds - 1, True, 3)
                    for s in range(3):
                        uses.n[s] += rounds - s // 2
                    c_ffn.next(rounds)

                def pool(self):
                    enter()
                    pe.wait_ge(mix_in, 48)
                    for b in range(4):
                        for j in range(2):
                            k = 2 * b + j
                            o = ps[:, b, S * j:S * j + S]
                            pe.matmul(o, xn[:, 0, P * k:P * k + P], band[:, k // 2, 0:S], start=True, stop=False)
                            last = pe.matmul(o[:, P:S], xn[:, 1, P * k:P * k + P], band[:, k // 2, S:S + P],
                                             start=False, stop=True)
                        last.then_inc(rows_turned, 1)
                    pe.wait_ge(aT_made, c_turned.next(4))
                    pe.wait_ge(lo_ready[2], uses.next(2))
                    h, lw = (w[:, 2, :].rearrange("p (k n) -> p k n", n=256) for w in (whi, wlo))
                    for t in range(T):
                        tok = slice(t * P, (t + 1) * P)
                        for g in range(4):
                            o = ps[:, 4 + 2 * t + g // 2, 256 * (g % 2):256 * (g % 2) + 256]
                            for k in range(2 * g, 2 * g + 2):
                                last = parts(o, aT_hi[:, k, tok], aT_lo[:, k, tok], h[:, k, :], lw[:, k, :],
                                             k % 2 == 0, k % 2 == 1)
                    last.then_inc(consumed[2], 1)

                def query(self, l):
                    enter()
                    for c in range(2):
                        chunk(2 * c, 512, turned(bank()))

                def cross(self, l):
                    enter()

                    def score(u):
                        h, t = u // 2, u % 2
                        if u >= 3:
                            pe.wait_ge(exped, units.n + u - 2)
                        for j in range(2):
                            last = pe.matmul(ps[:, u % 3, 0:S], qT[:, 2 * h + j, t * P:(t + 1) * P], kT[:, 2 * h + j, :],
                                             start=j == 0, stop=j == 1)
                        last.then_inc(scored, 1)

                    def turn(u):
                        U = units.n + u
                        pe.wait_ge(weighed, U + 1)
                        if u >= 2:
                            pe.wait_ge(probs_kept, U - 1)
                        for m in range(2):
                            last = pe.transpose(ps[:, 3 + u % 2, P * m:P * m + P], Pb[u % 3][:, P * m:P * m + P], ident)
                        last.then_inc(probs_turned, 1)

                    def values(h):
                        pe.wait_ge(probs_kept, units.n + 2 * h + 2)
                        if h >= 2:
                            pe.wait_ge(o_kept, groups.n + h - 1)
                        for j in range(2):
                            for m in range(2):
                                last = pe.matmul(ps[:, 6 + h % 2, S * j:S * j + S],
                                                 vm[:, m, 256 * h + P * j:256 * h + P * j + P], PTc(h)[:, m, :],
                                                 start=m == 0, stop=m == 1)
                        last.then_inc(pv_done, 1)

                    score(0)
                    score(1)
                    for u in range(8):
                        if u + 2 < 8:
                            score(u + 2)
                        turn(u)
                        if u % 2 == 0 and u:
                            values(u // 2 - 1)
                    values(3)
                    units.next(8)
                    groups.next(4)

                def project(self, w, gated=False):
                    enter()
                    if gated:
                        turn_rows()
                        pe.wait_ge(aT_made, c_turned.next(4))
                    for c in range(2):
                        chunk(2 * c, 512, rows(bank()))

                def nsa_inputs(self):
                    enter()

                    for c in range(6):
                        b = bank()
                        if c == 2:
                            pe.wait_ge(pos_in, 16)
                            pe.wait_ge(dve_evac, chunk_no.n - 1)
                            pe.transpose(ps[:, b + 2, 0:32], pos_rows, ident[0:32, 0:32])
                        chunk(2 * (c % 2), 512, turned(b))
                    chunk(0, 512, rows(bank()))
                    b = bank()
                    chunk(2, 48, [("N", t, 0, 256, ps[:, b + t, 0:256]) for t in range(T)])

                def nsa_compress(self):
                    enter()
                    for v in range(2):
                        pe.wait_ge(aT_made, c_turned.next())
                        for s in range(2):
                            pe.wait_ge(lo_ready[2 * v + s], uses.next(2 * v + s))
                        for j in range(16):
                            s, c = 2 * v + j // 8, CMP_HID * (j % 8)
                            r = slice(960 * v + 60 * j, 960 * v + 60 * j + P)
                            last = parts(ps[:, v, 0:CMP_HID], aTf_hi[:, r], aTf_lo[:, r], whi[:, s, c:c + CMP_HID],
                                         wlo[:, s, c:c + CMP_HID], j == 0, j == 15)
                            if j % 8 == 7:
                                last.then_inc(consumed[s], 1)
                    for v in range(2):
                        pe.wait_ge(gelu_made, v + 1)
                        for h in range(2):
                            last = pe.transpose(ps[:, 4 + v, 64 * h:64 * h + 60], hid_rows[v][:, P * h:P * h + P],
                                                ident[0:60, 0:60])
                        last.then_inc(cmp_hid_turned, 1)
                    pe.wait_ge(w2_in, 48)
                    pe.wait_ge(cmp_hid_kept, 1)
                    for h in range(2):
                        last = pe.matmul(ps[:, 2, 0:60], w2k[:, h, :], hidT[:, 0, h, :], start=h == 0, stop=h == 1)
                    last.then_inc(cmp_made, 1)
                    pe.wait_ge(cmp_hid_kept, 2)
                    for g in range(4):
                        for h in range(2):
                            last = pe.matmul(ps[0:N_CMP, 3, 64 * g:64 * g + 64], hidT[:, 1, h, N_CMP * g:N_CMP * g + N_CMP],
                                             w2v[:, h, :], start=h == 0, stop=h == 1)
                    last.then_inc(cmp_made, 1)

                def nsa_attend(self):
                    enter()

                    def score(u):
                        g, t, r = u // 8, u // 4 % 2, u % 4
                        half, w = slice(64 * (r % 2), 64 * (r % 2) + 64), P * (t + 1)
                        if u >= 3:
                            pe.wait_ge(maxed, units.n + u - 2)
                        q = qT[half, 2 * g + r // 2, t * P:(t + 1) * P]
                        pe.matmul(ps[:, u % 3, 0:w], q, ksT[half, g, 0:w], start=True, stop=True)
                        pe.matmul(ps[:, u % 3, w:2 * w], q, kwT[half, g, 0:w], start=True, stop=True).then_inc(scored, 1)

                    def turn(u):
                        U, t = units.n + u, u // 4 % 2
                        pe.wait_ge(weighed, U + 1)
                        if u >= 2:
                            pe.wait_ge(probs_kept, U - 1)
                        for m in range(2 * (t + 1)):
                            last = pe.transpose(ps[:, 3 + u % 2, P * m:P * m + P], Pb[u % 3][:, P * m:P * m + P], ident)
                        last.then_inc(probs_turned, 1)

                    def values(gi, half):
                        g, t = gi // 2, gi % 2
                        pe.wait_ge(probs_kept, units.n + 4 * gi + 4)
                        pe.wait_ge(cmp_kept, gi + 1)
                        if gi >= 2:
                            pe.wait_ge(o_kept, groups.n + gi - 1)
                        o = ps[64 * half:64 * half + 64, 6 + gi % 2, 0:256]
                        pe.matmul(o, vcmp[:, 64 * g:64 * g + 64], nsaPc[gi % 2][0:N_CMP, half::2, :], start=True, stop=False)
                        for j, v in enumerate((vs, vw)):
                            for m in range(t + 1):
                                c = P * (j * (t + 1) + m)
                                last = pe.matmul(o, v[:, m, 64 * g:64 * g + 64], nsaP[gi % 2][:, half::2, c:c + P],
                                                 start=False, stop=j == 1 and m == t)
                        if half == 1:
                            last.then_inc(pv_done, 1)

                    def turn_cmp(gi):
                        g, t = gi // 2, gi % 2
                        pe.wait_ge(cmp_weighed, 1)
                        if gi:
                            pe.wait_ge(cmp_kept, gi)
                        for r in range(4):
                            last = pe.transpose(ps[0:N_CMP, 5, P * r:P * r + P], cmpP[:, t, 4 * g + r, :], ident)
                        last.then_inc(cmp_turned, 1)

                    for t in range(T):
                        for h in range(NSA_H):
                            half, c = slice(64 * (h % 2), 64 * (h % 2) + 64), 16 * (NSA_H // 2 * t + h // 2)
                            last = pe.matmul(ps[:, 6 + h % 2, c:c + N_CMP], qT[half, h // 2, t * P:(t + 1) * P],
                                             kcT[half, N_CMP * (h // 4):N_CMP * (h // 4) + N_CMP], start=True, stop=True)
                            if t == T - 1 and h >= NSA_H - 2:
                                last.then_inc(cmp_scored, 1)
                    score(0)
                    score(1)
                    for u in range(32):
                        if u + 2 < 32:
                            score(u + 2)
                        turn(u)
                        if u % 4 == 2:
                            turn_cmp(u // 4)
                        if u % 4 < 2 and u >= 4:
                            values(u // 4 - 1, u % 4)
                    for half in range(2):
                        values(7, half)
                    units.next(32)
                    groups.next(8)

                def ada(self, part):
                    enter()
                    if part == 0:
                        pe.wait_ge(hot_in, 48)
                        pe.wait_ge(mask_row, 1)
                        pe.matmul(ps[0:12, 6, 0:384], rel, hot, start=True, stop=True).then_inc(dist_made, 1)
                    pe.wait_ge(ones_made, part + 1)
                    pe.wait_ge(ada_in, 32 * (part + 1))
                    for c in range(6):
                        pe.matmul(ps[:, c, :], ones, ada_parts[:, c, :], start=True, stop=True).then_inc(ada_summed, 1)

                def wide_inputs(self):
                    enter()

                    def index_scores(t):
                        w = P * (t + 1)
                        for h in range(8):
                            r = slice(32 * (h % 4), 32 * (h % 4) + 32)
                            pe.matmul(ps[:, index_bank[h % 4], w * (h // 4):w * (h // 4) + w],
                                      iqT[r, h // 4, t * P:(t + 1) * P], ikT[r, 0:w], start=True, stop=True,
                                      tile_position=(32 * (h % 4), 0))
                        pe.drain().then_inc(index_scored, 1)

                    for c in range(10):
                        b = bank()
                        if c == 1:
                            chunk(2, 392, [("T", P * j, P, ps[:, b, S * j:S * j + S]) for j in range(2)]
                                  + [("T", 256, P, ps[:, b + 1, 0:S])]
                                  + [("N", t, 384, 256, ps[:, b + 2 + t, 0:256]) for t in range(T)])
                        else:
                            chunk(2 * (c % 2), 512, turned(b) if c in (7, 8) else rows(b))
                        if c == 2:
                            pe.wait_ge(act_evac, chunk_no.n - 1)
                            pe.wait_ge(dve_evac, chunk_no.n - 1)
                            index_scores(1)
                        if c == 5:
                            pe.wait_ge(index_read, 1)
                            index_scores(0)

                def turn_bias(self, b):
                    enter()
                    pe.wait_ge(skew_in, 16 * (b + 1))
                    for j in range(2):
                        last = pe.matmul(ps[:, 4 + j, :], cst[:, C_FLIP:C_FLIP + P], skew[:, 2 * j:2 * j + 2, :],
                                         start=True, stop=True)
                    last.then_inc(bias_turned, 1)

                def diff_bias(self):
                    self.turn_bias(0)

                def turn_probs(self, u, t, b, depth=2, banks=2):
                    U = units.n + u
                    pe.wait_ge(weighed, U + 1)
                    if u >= banks:
                        pe.wait_ge(probs_kept, U + 1 - banks)
                    for m in range(t + 1):
                        last = pe.transpose(ps[:, b, P * m:P * m + P], Pb[u % depth][:, P * m:P * m + P], ident)
                    last.then_inc(probs_turned, 1)

                def diff(self):
                    enter()

                    def score(u):
                        h, t = u // 2, u % 2
                        if u >= 3:
                            pe.wait_ge(maxed, units.n + u - 2)
                        for j in range(2):
                            half = slice(64 * j, 64 * j + 64)
                            last = pe.matmul(ps[:, 2 * (u % 3) + j, 0:P * (t + 1)], aqT[half, h, t * P:(t + 1) * P],
                                             akT[half, h, 0:P * (t + 1)], start=True, stop=True)
                        last.then_inc(scored, 1)

                    def values(u):
                        h, t = u // 2, u % 2
                        pe.wait_ge(probs_kept, units.n + u + 1)
                        if u >= 1:
                            pe.wait_ge(o_hi, 16 + u)
                        for m in range(t + 1):
                            last = pe.matmul(ps[:, 7, 0:P], diff_PT[u % 2][:, P * m:P * m + P], av[:, m, P * h:P * h + P],
                                             start=m == 0, stop=m == t)
                        last.then_inc(pv_done, 1)

                    score(0)
                    score(1)
                    for u in range(8):
                        if u + 2 < 8:
                            score(u + 2)
                        self.turn_probs(u, u % 2, 6, depth=3, banks=1)
                        if u:
                            values(u - 1)
                    values(7)
                    units.next(8)
                    groups.next(8)

                def sparse_inputs(self):
                    enter()
                    chunk(0, 512, turned(bank()))
                    b = bank()
                    chunk(2, 384, [("N", t, 0, 384, ps[:, b + t, 0:384]) for t in range(T)])
                    pe.wait_ge(branch_kept, 1)
                    for h in range(4):
                        for t in range(T):
                            c = S * (h % 2) + P * t
                            last = pe.transpose(ps[:, 2 + h // 2, c:c + P], oA[:, t, h, :], ident)
                    last.then_inc(branch_done, 1)
                    chunk(0, 512, turned(bank()))
                    self.turn_bias(1)

                def latent(self):
                    enter()
                    pe.wait_ge(branch_kept, 2)
                    for t in range(T):
                        last = pe.transpose(ps[:, 0, P * t:P * t + P], kvn[:, t, :], ident)
                    last.then_inc(branch_kept, 1)

                def dsa(self, t):
                    enter()
                    w = P * (t + 1)

                    def score(u):
                        if u >= 2:
                            pe.wait_ge(maxed, units.n + u - 1)
                        pe.matmul(ps[:, u % 2, 0:w], bqT[:, u, t * P:(t + 1) * P], kvT[:, 0:w], start=True, stop=True)\
                          .then_inc(scored, 1)

                    score(0)
                    for u in range(4):
                        if u + 1 < 4:
                            score(u + 1)
                        self.turn_probs(u, t, 2 + u % 2)
                    units.next(4)
                    pe.wait_ge(probs_kept, units.n)
                    for m in range(t + 1):
                        last = pe.matmul(ps[:, 4, :], kvn[:, m, :], PTd[:, :, m, :], start=m == 0, stop=m == t)
                    last.then_inc(pv_done, 1)
                    groups.next(1)
                    pe.wait_ge(lat_kept, t + 1)
                    for h in range(4):
                        last = pe.matmul(ps[64 * (h % 2):64 * (h % 2) + 64, 5, P * (h // 2):P * (h // 2) + P],
                                         w_uv[:, h, :], o_lat[:, P * h:P * h + P], start=True, stop=True)
                    last.then_inc(branch_done, 1)

                def moba(self):
                    self.turn_bias(2)
                    enter()

                    def score(u):
                        h, t = u // 2, u % 2
                        r, w = slice(64 * (h % 2), 64 * (h % 2) + 64), P * (t + 1)
                        if u >= 3:
                            pe.wait_ge(maxed, units.n + u - 2)
                        pe.matmul(ps[:, u % 3, 0:w], cqT[r, h // 2, t * P:(t + 1) * P], ckT[r, h // 2, 0:w],
                                  start=True, stop=True).then_inc(scored, 1)

                    def values(u):
                        h, t = u // 2, u % 2
                        pe.wait_ge(probs_kept, units.n + u + 1)
                        for m in range(t + 1):
                            c = S * (h // 2) + P * t
                            last = pe.matmul(ps[64 * (h % 2):64 * (h % 2) + 64, 4, c:c + P], cv[:, m, 64 * h:64 * h + 64],
                                             moba_PT[u % 2][:, P * m:P * m + P], start=m == 0, stop=m == t)
                        last.then_inc(pv_done, 1)

                    score(0)
                    score(1)
                    for u in range(8):
                        if u + 2 < 8:
                            score(u + 2)
                        self.turn_probs(u, u % 2, 5 + u % 2, depth=3)
                        if u:
                            values(u - 1)
                    values(7)
                    units.next(8)
                    groups.next(8)

                def merge(self):
                    enter()
                    for br in range(3):
                        if br < 2:
                            pe.wait_ge(aT_made, c_turned.next())
                        if br == 2:
                            pe.wait_ge(branch_kept, 4)
                        for s in ((2, 3), (0,), (1,))[br]:
                            pe.wait_ge(lo_ready[s], uses.next(s))
                        for c in range(2):
                            for t in range(T):
                                o, tok = ps[:, 4 * (br % 2) + 2 * t + c, :], slice(t * P, (t + 1) * P)
                                n = (4, 2, 2)[br]
                                for k in range(n):
                                    kk = (0, 4, 6)[br] + k
                                    s, at = (2 + c, 512 * k) if br == 0 else (br - 1, 1024 * k + 512 * c)
                                    last = parts(o, aT_hi[:, kk, tok], aT_lo[:, kk, tok], whi[:, s, at:at + 512],
                                                 wlo[:, s, at:at + 512], k == 0, k == n - 1)
                            if br == 0:
                                last.then_inc(consumed[2 + c], 1)
                        if br:
                            last.then_inc(consumed[br - 1], 1)
                        pe.drain().then_inc(branch_done, 1)

                def mlp(self):
                    stages.next()
                    rows_ready = c_turned.n - 4
                    rounds = 8
                    ub, fb = list(uses.n), c_ffn.n
                    def up(i):
                        for s in range(2):
                            pe.wait_ge(lo_ready[s], ub[s] + i + 1)
                            h, lw = (w[:, s, :].rearrange("p (k n) -> p k n", k=4) for w in (whi, wlo))
                            for t in range(T):
                                if type(i) is int and i == 0:
                                    pe.wait_ge(aT_made, rows_ready + 2 * t + s + 1)
                                tok = slice(t * P, (t + 1) * P)
                                for r in range(4):
                                    k = 4 * s + r
                                    last = parts(ps[:, 4 + t, :], aT_hi[:, k, tok], aT_lo[:, k, tok], h[:, r, :],
                                                 lw[:, r, :], k == 0, k == KD - 1)
                                if s == 1 and t == 0:
                                    last.then_inc(gate_half, 1)
                            last.then_inc(consumed[s], 1)

                    def turn(i):
                        for t in range(T):
                            pe.wait_ge(hid_made, 2 * (fb + i) + t + 1)
                            for k in range(4):
                                c = S * (k % 2) + P * t
                                last = pe.transpose(ps[:, 6 + k // 2, c:c + P], hs[:, t, P * k:P * k + P], ident)
                        last.then_inc(hid_turned, 1)

                    def down(i, stop, first=2):
                        pe.wait_ge(hT_made, fb + i + 1)
                        for s in (first, first + 1):
                            pe.wait_ge(lo_ready[s], ub[s] + i + 1 if first == 2 else ub[s] + rounds + 1)
                            h, lw = (w[:, s, :].rearrange("p (k c n) -> p k c n", k=2, c=2) for w in (whi, wlo))
                            for t in range(T):
                                tok = slice(t * P, (t + 1) * P)
                                for c in range(2):
                                    for k in range(2):
                                        kk = 2 * (s - first) + k
                                        last = parts(ps[:, 2 * t + c, :], hT_hi[:, kk, tok], hT_lo[:, kk, tok],
                                                     h[:, k, c, :], lw[:, k, c, :], False, stop and kk == 3)
                            last.then_inc(consumed[s], 1)

                    up(0)
                    for b in range(4):
                        pe.matmul(ps[:, b, :], zero[:, 0:P], zero[:, :], start=True, stop=False, skip_group_check=True)
                    turn(0)
                    with pe.Fori(1, rounds) as i:
                        up(i)
                        down(i - 1, False)
                        turn(i)
                    down(rounds - 1, True, 0)

            pe.wait_ge(const_in, 16)
            pe.wait_ge(zero_made, 1)
            program(Pe())


_NAMES = ["x", "mem", "ffn1_norm", "ffn1_w_in", "ffn1_w_out", "mix_norm", "xattn_norm", "mem_norm", "xattn_w_q",
          "xattn_w_kv", "xattn_w_o", "ffn2_norm", "ffn2_w_in", "ffn2_w_out", "pool_w", "pool_b", "pool_scale",
          "nsa_w_in", "nsa_cmp_pos", "nsa_cmp_w1", "nsa_cmp_w2", "nsa_w_o", "final_norm", "c_2", "rel_bias_2",
          "ada_w_2", "ada_b_2", "norm_mix_2", "w_in_2", "gate_b_2", "diff_lambda_2", "diff_subln_2",
          "dsa_kv_norm_2", "dsa_w_uv_2", "w_br_a_2", "w_br_b_2", "w_br_c_2", "w_o_2", "norm_mlp_2", "w_ff1_2",
          "w_ff2_2", "norm_final_2"]


def kernel(**inputs):
    import concourse.bacc as bacc
    from concourse.bass_utils import run_bass_kernel_spmd

    arrays = {n: np.ascontiguousarray(inputs[n]) for n in _NAMES}
    arrays["constants"] = constant_table()
    nc = bacc.Bacc("TRN2", target_bir_lowering=False, num_devices=1)
    A = {n: nc.dram_tensor(f"in_{n}", a.shape, F32, kind="ExternalInput").ap() for n, a in arrays.items()}
    out = nc.dram_tensor("out_x", (1, S, D), F32, kind="ExternalOutput").ap()
    build(nc, A, out)
    r = run_bass_kernel_spmd(nc, [{f"in_{n}": a for n, a in arrays.items()}], core_ids=[0])
    return r.results[0]["out_x"]
```
